# Optimizing a Trainium2 kernel written in Bass

```python
import math
import jax
import jax.numpy as jnp
from jax import lax
import numpy as np
import jax, jax.numpy as jnp

D_MODEL = 1024
BATCH = 1
SEQ = 1024
DEPTH = 2

CTX_LEN = 256
GRID_W = 64
MIX_W = D_MODEL
FOURIER_W = MIX_W // 4
FOURIER_GROUPS = 4
FOURIER_GD = FOURIER_W // FOURIER_GROUPS
POOL_W = MIX_W // 4
POOL_WINDOWS = (2, 4, 8, 16)
POOL_GD = POOL_W // len(POOL_WINDOWS)
ATTN_W = MIX_W - FOURIER_W - POOL_W
QK_DIM = 64
V_DIM = 2 * QK_DIM
N_HEADS = ATTN_W // V_DIM
QK_W = N_HEADS * 2 * QK_DIM
Q_BLOCK = 128
ROPE_THETA = 10000.0
EPS = 1e-6

A_OFF = 0
B_OFF = A_OFF + FOURIER_W
Q_OFF = B_OFF + POOL_W
K_OFF = Q_OFF + QK_W
V_OFF = K_OFF + QK_W
G_OFF = V_OFF + ATTN_W
IN_W = G_OFF + MIX_W


def rms_norm(t, g):
    tf = t.astype(jnp.float32)
    y = tf * lax.rsqrt(jnp.mean(tf * tf, axis=-1, keepdims=True) + EPS)
    return (y * g.astype(jnp.float32)).astype(t.dtype)

def axial_rope_tables(rows):
    row = jnp.repeat(jnp.arange(rows), GRID_W).astype(jnp.float32)
    col = jnp.tile(jnp.arange(GRID_W), rows).astype(jnp.float32)
    half = QK_DIM // 2
    inv_freq = ROPE_THETA ** (-jnp.arange(0, half, 2, dtype=jnp.float32) / half)
    ang_r = row[:, None] * inv_freq[None, :]
    ang_c = col[:, None] * inv_freq[None, :]
    ang = jnp.concatenate([ang_r, ang_r, ang_c, ang_c], axis=-1)
    return jnp.cos(ang), jnp.sin(ang)

def apply_rope(t, cos, sin):
    tr = t.reshape(t.shape[:-1] + (2, 2, QK_DIM // 4))
    rot = jnp.stack([-tr[..., 1, :], tr[..., 0, :]], axis=-2).reshape(t.shape)
    return (t * cos + rot * sin).astype(t.dtype)

def centred_window_mean(u, w):
    L = u.shape[1]
    lo = w // 2
    hi = w - lo - 1
    cs = jnp.pad(jnp.cumsum(u.astype(jnp.float32), axis=1), ((0, 0), (1, 0), (0, 0)))
    t = jnp.arange(L)
    a = jnp.clip(t - lo, 0, L - 1)
    b = jnp.clip(t + hi, 0, L - 1)
    s = cs[:, b + 1] - cs[:, a]
    cnt = (b - a + 1).astype(jnp.float32)
    return (s / cnt[None, :, None]).astype(u.dtype)

def fourier_mix(a, w_fourier):
    B_, L = a.shape[:2]
    ag = a.reshape(B_, L, FOURIER_GROUPS, FOURIER_GD).astype(jnp.float32)
    f = jnp.fft.fftn(ag, axes=(1, 3), norm='ortho').real.astype(a.dtype)
    y = jnp.einsum('blgc,gcd->blgd', f, w_fourier)
    return y.reshape(B_, L, FOURIER_W)

def pool_mix(b, w_pool, pool_scale):
    B_, L = b.shape[:2]
    bg = b.reshape(B_, L, len(POOL_WINDOWS), POOL_GD)
    pooled = jnp.stack([centred_window_mean(bg[:, :, gi], w) for gi, w in enumerate(POOL_WINDOWS)], axis=2) - bg
    y = jnp.einsum('blgc,gcd->blgd', pooled, w_pool).reshape(B_, L, POOL_W)
    return y * pool_scale

def split_heads_qk(t):
    B_, L = t.shape[:2]
    return t.reshape(B_, L, N_HEADS, 2, QK_DIM).transpose(0, 2, 3, 1, 4)

def split_heads_v(t):
    B_, L = t.shape[:2]
    return t.reshape(B_, L, N_HEADS, V_DIM).transpose(0, 2, 1, 3)

def diff_attend(q, k, v, lam):
    s = jnp.einsum('bhmqd,bhmkd->bhmqk', q, k).astype(jnp.float32) * (QK_DIM ** -0.5)
    p = jax.nn.softmax(s, axis=-1)
    p = p[:, :, 0] - lam * p[:, :, 1]
    return jnp.einsum('bhqk,bhkd->bhqd', p.astype(v.dtype), v)

def attn_post(o, subln_g, lam_init):
    o = rms_norm(o, subln_g) * (1.0 - lam_init)
    B_, H, L, dv = o.shape
    return o.transpose(0, 2, 1, 3).reshape(B_, L, H * dv)

def mixer_out(a_in, b_in, attn, gate, w_fourier, w_pool, pool_scale, w_out):
    y = jnp.concatenate([fourier_mix(a_in, w_fourier), pool_mix(b_in, w_pool, pool_scale), attn], axis=-1)
    return (y * jax.nn.silu(gate)) @ w_out

def mixer_layer(layer_idx, x, ctx, c, c_ctx, norm_g, w_mod, b_mod, w_in, w_fourier, w_pool,
                pool_scale, qk_norm_g, lam_vecs, subln_g, w_out, rope_cos, rope_sin, update_ctx):
    shift, scale, gate = jnp.split(jax.nn.silu(c) @ w_mod + b_mod, 3, axis=-1)
    shift_c, scale_c, gate_c = jnp.split(jax.nn.silu(c_ctx) @ w_mod + b_mod, 3, axis=-1)
    h = rms_norm(x, norm_g) * (1 + scale[:, None]) + shift[:, None]
    hc = rms_norm(ctx, norm_g) * (1 + scale_c) + shift_c

    lam_init = 0.8 - 0.6 * math.exp(-0.3 * layer_idx)
    lv = lam_vecs.astype(jnp.float32)
    lam = jnp.exp(jnp.sum(lv[0] * lv[1])) - jnp.exp(jnp.sum(lv[2] * lv[3])) + lam_init

    p = h @ w_in
    a_in, b_in = p[..., A_OFF:B_OFF], p[..., B_OFF:Q_OFF]
    q, k, v, g = p[..., Q_OFF:K_OFF], p[..., K_OFF:V_OFF], p[..., V_OFF:G_OFF], p[..., G_OFF:]

    if update_ctx:
        pc = hc @ w_in
        kc, vc = pc[..., K_OFF:V_OFF], pc[..., V_OFF:G_OFF]
    else:
        pkv = hc @ w_in[:, K_OFF:G_OFF]
        kc, vc = pkv[..., :QK_W], pkv[..., QK_W:]

    q_lat = apply_rope(rms_norm(split_heads_qk(q), qk_norm_g[0]), rope_cos, rope_sin)
    k_lat = apply_rope(rms_norm(split_heads_qk(k), qk_norm_g[1]), rope_cos, rope_sin)
    k_ctx = rms_norm(split_heads_qk(kc), qk_norm_g[1])
    v_ctx = split_heads_v(vc)
    k_all = jnp.concatenate([k_ctx, k_lat], axis=3)
    v_all = jnp.concatenate([v_ctx, split_heads_v(v)], axis=2)

    B_, H, _, L, d = q_lat.shape
    nb = L // Q_BLOCK
    qb = jnp.moveaxis(q_lat.reshape(B_, H, 2, nb, Q_BLOCK, d), 3, 0)
    ob = lax.map(lambda qblk: diff_attend(qblk, k_all, v_all, lam), qb)
    o = jnp.moveaxis(ob, 0, 2).reshape(B_, H, L, V_DIM)
    attn = attn_post(o, subln_g, lam_init)

    x_new = x + gate[:, None] * mixer_out(a_in, b_in, attn, g, w_fourier, w_pool, pool_scale, w_out)

    if update_ctx:
        qc = rms_norm(split_heads_qk(pc[..., Q_OFF:K_OFF]), qk_norm_g[0])
        attn_c = attn_post(diff_attend(qc, k_ctx, v_ctx, lam), subln_g, lam_init)
        ctx = ctx + gate_c * mixer_out(pc[..., A_OFF:B_OFF], pc[..., B_OFF:Q_OFF], attn_c,
                                       pc[..., G_OFF:], w_fourier, w_pool, pool_scale, w_out)
    return x_new, ctx

def first_inputs(seed: int = 0) -> dict:
    key = jax.random.key(seed)
    ks = jax.random.split(key, 16)
    f32 = jnp.float32
    nrm = lambda k, shape: jax.random.normal(k, shape, dtype=f32)
    return {
        'x': nrm(ks[0], (BATCH, SEQ, D_MODEL)),
        'c': nrm(ks[1], (BATCH, D_MODEL)),
        'ctx': nrm(ks[2], (BATCH, CTX_LEN, D_MODEL)),
        'c_ctx': nrm(ks[3], (D_MODEL,)),
        'norm_g': 1.0 + 0.02 * nrm(ks[4], (DEPTH, D_MODEL)),
        'w_mod': nrm(ks[5], (DEPTH, D_MODEL, 3 * D_MODEL)) * D_MODEL ** -0.5,
        'b_mod': 0.02 * nrm(ks[6], (DEPTH, 3 * D_MODEL)),
        'w_in': nrm(ks[7], (DEPTH, D_MODEL, IN_W)) * D_MODEL ** -0.5,
        'w_fourier': nrm(ks[8], (DEPTH, FOURIER_GROUPS, FOURIER_GD, FOURIER_GD)) * FOURIER_GD ** -0.5,
        'w_pool': nrm(ks[9], (DEPTH, len(POOL_WINDOWS), POOL_GD, POOL_GD)) * POOL_GD ** -0.5,
        'pool_scale': 1.0 + 0.1 * nrm(ks[10], (DEPTH, POOL_W)),
        'qk_norm_g': 1.0 + 0.02 * nrm(ks[11], (DEPTH, 2, QK_DIM)),
        'lam_vecs': 0.1 * nrm(ks[12], (DEPTH, 4, QK_DIM)),
        'subln_g': 1.0 + 0.02 * nrm(ks[13], (DEPTH, V_DIM)),
        'w_out': nrm(ks[14], (DEPTH, MIX_W, D_MODEL)) * MIX_W ** -0.5,
    }

def first_block(x, c, ctx, c_ctx, norm_g, w_mod, b_mod, w_in, w_fourier, w_pool, pool_scale,
              qk_norm_g, lam_vecs, subln_g, w_out):
    rows = x.shape[1] // GRID_W
    rope_cos, rope_sin = axial_rope_tables(rows)
    for l in range(DEPTH):
        x, ctx = mixer_layer(l, x, ctx, c, c_ctx, norm_g[l], w_mod[l], b_mod[l], w_in[l],
                             w_fourier[l], w_pool[l], pool_scale[l], qk_norm_g[l], lam_vecs[l],
                             subln_g[l], w_out[l], rope_cos, rope_sin, l < DEPTH - 1)
    return x


DEPTH_2 = 1

CHUNK = 64
SUB = 16
N_SUB = CHUNK // SUB

A_HEADS = 8
A_DK = 128
A_KEY = A_HEADS * A_DK
A_DV = D_MODEL // A_HEADS
B_HEADS = 4
B_KEY = D_MODEL // 2
B_DK = B_KEY // B_HEADS
B_DV = D_MODEL // B_HEADS
B_RANK = 16
B_GATE_NORM = 16.0
C_HEADS = 8
C_DK = 128
C_KEY = C_HEADS * C_DK
C_DV = D_MODEL // C_HEADS
C_CONV = 4
C_QKV = 2 * C_KEY + D_MODEL
D_FF = 4 * D_MODEL
N_BRANCH = 3

SPLITS = (A_KEY, A_KEY, D_MODEL, D_MODEL,
          B_KEY, B_KEY, D_MODEL, B_RANK, D_MODEL,
          C_QKV, C_HEADS, C_HEADS, D_MODEL,
          N_BRANCH * D_MODEL)
N_IN = 2 * A_KEY + 2 * D_MODEL + 2 * B_KEY + 2 * D_MODEL + B_RANK + C_QKV + 2 * C_HEADS + D_MODEL + N_BRANCH * D_MODEL


def rmsnorm(x, w):
    xf = x.astype(jnp.float32)
    y = xf * lax.rsqrt(jnp.mean(xf * xf, axis=-1, keepdims=True) + EPS)
    return (y * w.astype(jnp.float32)).astype(x.dtype)

def l2norm(x):
    return x * lax.rsqrt(jnp.sum(x * x, axis=-1, keepdims=True) + EPS)

def to_chunks(t):
    b, t_len, h, d = t.shape
    return t.reshape(b, t_len // CHUNK, CHUNK, h, d).transpose(1, 0, 3, 2, 4)

def from_chunks(t):
    nc, b, h, c, d = t.shape
    return t.transpose(1, 0, 3, 2, 4).reshape(b, nc * c, h, d)

def scalar_chunks(t):
    b, t_len, h = t.shape
    return t.reshape(b, t_len // CHUNK, CHUNK, h).transpose(1, 0, 3, 2)

def gated_linear_attention(q, k, v, log_f):
    bsz, _, h, kd = q.shape
    vd = v.shape[-1]
    qc, kc, vc, gc = (to_chunks(t.astype(jnp.float32)) for t in (q, k, v, log_f))
    tri = jnp.tril(jnp.ones((SUB, SUB), bool))
    strict_sub = jnp.tril(jnp.ones((N_SUB, N_SUB), bool), -1)
    eye_sub = jnp.eye(N_SUB, dtype=jnp.float32)

    def step(state, inp):
        qi, ki, vi, gi = inp
        b = jnp.cumsum(gi, axis=-2)
        o_inter = jnp.einsum('bhck,bhkv->bhcv', qi * jnp.exp(b), state)
        qs, ks, bs = (t.reshape(bsz, h, N_SUB, SUB, kd) for t in (qi, ki, b))
        b_excl = (b - gi).reshape(bsz, h, N_SUB, SUB, kd)
        diff = jnp.where(tri[:, :, None], bs[..., :, None, :] - bs[..., None, :, :], -jnp.inf)
        a_diag = jnp.einsum('bhnik,bhnijk,bhnjk->bhnij', qs, jnp.exp(diff), ks)
        b_start = b_excl[..., 0, :]
        b_end = bs[..., -1, :]
        q_off = qs * jnp.exp(bs - b_start[..., None, :])
        k_off = ks * jnp.exp(b_end[..., None, :] - bs)
        pair = jnp.where(strict_sub[:, :, None],
                         b_start[:, :, :, None, :] - b_end[:, :, None, :, :], -jnp.inf)
        a_off = jnp.einsum('bhsik,bhstk,bhtjk->bhsitj', q_off, jnp.exp(pair), k_off)
        a = (a_off + jnp.einsum('bhnij,nm->bhnimj', a_diag, eye_sub)).reshape(bsz, h, CHUNK, CHUNK)
        o = o_inter + jnp.einsum('bhij,bhjv->bhiv', a, vi)
        b_last = b[..., -1, :]
        state = jnp.exp(b_last)[..., None] * state + jnp.einsum(
            'bhck,bhcv->bhkv', ki * jnp.exp(b_last[..., None, :] - b), vi)
        return state, o

    s0 = jnp.zeros((bsz, h, kd, vd), jnp.float32)
    _, o = lax.scan(step, s0, (qc, kc, vc, gc))
    return from_chunks(o)

def gated_delta_rule(q, k, v, log_a, beta):
    bsz, _, h, kd = q.shape
    vd = v.shape[-1]
    qc, kc, vc = (to_chunks(t.astype(jnp.float32)) for t in (q, k, v))
    gc = scalar_chunks(log_a.astype(jnp.float32))
    bc = scalar_chunks(beta.astype(jnp.float32))
    b = jnp.cumsum(gc, axis=-1)
    causal = jnp.tril(jnp.ones((CHUNK, CHUNK), bool))
    strict = jnp.tril(jnp.ones((CHUNK, CHUNK), bool), -1)
    decay = jnp.exp(jnp.where(causal, b[..., :, None] - b[..., None, :], -jnp.inf))
    kk = jnp.einsum('nbhik,nbhjk->nbhij', kc, kc)
    m = jnp.eye(CHUNK, dtype=jnp.float32) + jnp.where(strict, bc[..., :, None] * kk * decay, 0.0)
    rhs = jnp.concatenate([vc * bc[..., None], kc * (bc * jnp.exp(b))[..., None]], axis=-1)
    sol = lax.linalg.triangular_solve(m, rhs, left_side=True, lower=True, unit_diagonal=True)
    u, w = sol[..., :vd], sol[..., vd:]
    qk = jnp.einsum('nbhik,nbhjk->nbhij', qc, kc) * decay
    q_dec = qc * jnp.exp(b)[..., None]
    k_dec = kc * jnp.exp(b[..., -1:] - b)[..., None]
    a_last = jnp.exp(b[..., -1])

    def step(state, inp):
        u_i, w_i, qk_i, qd_i, kd_i, al_i = inp
        v_new = u_i - jnp.einsum('bhck,bhkv->bhcv', w_i, state)
        o = jnp.einsum('bhck,bhkv->bhcv', qd_i, state) + jnp.einsum('bhij,bhjv->bhiv', qk_i, v_new)
        state = al_i[..., None, None] * state + jnp.einsum('bhck,bhcv->bhkv', kd_i, v_new)
        return state, o

    s0 = jnp.zeros((bsz, h, kd, vd), jnp.float32)
    _, o = lax.scan(step, s0, (u, w, qk, q_dec, k_dec, a_last))
    return from_chunks(o)

def causal_short_conv(x, w):
    kw = w.shape[0]
    t_len = x.shape[1]
    xp = jnp.pad(x, ((0, 0), (kw - 1, 0), (0, 0)))
    out = xp[:, 0:t_len] * w[0]
    for j in range(1, kw):
        out = out + xp[:, j:j + t_len] * w[j]
    return out

def hybrid_mixer(h, w_in, lb, gla_w_gk, gla_b_gk, gdn_conv, gdn_a_log, gdn_dt_bias,
                 hgrn_onorm, gla_onorm, gdn_onorm, w_out):
    bsz, t_len, _ = h.shape
    proj = h @ w_in
    cuts = [int(c) for c in np.cumsum(SPLITS)[:-1]]
    (a_q, a_f, a_i, a_g, b_q, b_k, b_v, b_gk, b_g,
     c_qkv, c_a, c_b, c_g, merge) = jnp.split(proj, cuts, axis=-1)

    z = a_f.astype(jnp.float32).reshape(bsz, t_len, A_HEADS, A_DK)
    lb_h = lb.reshape(A_HEADS, A_DK)
    log_f_a = jnp.logaddexp(jnp.log(lb_h), jnp.log1p(-lb_h) + jax.nn.log_sigmoid(z))
    k_a = (1.0 - lb_h) * jax.nn.sigmoid(-z)
    q_a = jax.nn.silu(a_q).reshape(bsz, t_len, A_HEADS, A_DK)
    o_a = gated_linear_attention(q_a, k_a, a_i.reshape(bsz, t_len, A_HEADS, A_DV), log_f_a)
    y_a = (rmsnorm(o_a, hgrn_onorm) * jax.nn.silu(a_g.reshape(bsz, t_len, A_HEADS, A_DV))).reshape(bsz, t_len, D_MODEL)

    q_b = b_q.reshape(bsz, t_len, B_HEADS, B_DK) * (B_DK ** -0.5)
    k_b = b_k.reshape(bsz, t_len, B_HEADS, B_DK)
    gk = (b_gk @ gla_w_gk + gla_b_gk).astype(jnp.float32)
    log_f_b = (jax.nn.log_sigmoid(gk) / B_GATE_NORM).reshape(bsz, t_len, B_HEADS, B_DK)
    o_b = gated_linear_attention(q_b, k_b, b_v.reshape(bsz, t_len, B_HEADS, B_DV), log_f_b)
    y_b = (rmsnorm(o_b, gla_onorm) * jax.nn.silu(b_g.reshape(bsz, t_len, B_HEADS, B_DV))).reshape(bsz, t_len, D_MODEL)

    qkv = jax.nn.silu(causal_short_conv(c_qkv, gdn_conv))
    q_c = l2norm(qkv[..., :C_KEY].astype(jnp.float32).reshape(bsz, t_len, C_HEADS, C_DK)) * (C_DK ** -0.5)
    k_c = l2norm(qkv[..., C_KEY:2 * C_KEY].astype(jnp.float32).reshape(bsz, t_len, C_HEADS, C_DK))
    v_c = qkv[..., 2 * C_KEY:].reshape(bsz, t_len, C_HEADS, C_DV)
    log_a_c = -jnp.exp(gdn_a_log.astype(jnp.float32)) * jax.nn.softplus((c_a + gdn_dt_bias).astype(jnp.float32))
    beta_c = jax.nn.sigmoid(c_b.astype(jnp.float32))
    o_c = gated_delta_rule(q_c, k_c, v_c, log_a_c, beta_c)
    y_c = (rmsnorm(o_c, gdn_onorm) * jax.nn.silu(c_g.reshape(bsz, t_len, C_HEADS, C_DV))).reshape(bsz, t_len, D_MODEL)

    g = jax.nn.sigmoid(merge.astype(jnp.float32)).reshape(bsz, t_len, N_BRANCH, D_MODEL)
    y = g[:, :, 0] * y_a + g[:, :, 1] * y_b + g[:, :, 2] * y_c
    return (y.astype(h.dtype) @ w_out).astype(h.dtype)

def squared_relu_mlp(h, w_up, w_down):
    return jnp.square(jax.nn.relu(h @ w_up)) @ w_down

def second_inputs(seed: int = 0) -> dict:
    key = jax.random.key(seed)
    ks = jax.random.split(key, 20)
    f32 = jnp.float32

    def gain(k, n):
        return 1.0 + 0.02 * jax.random.normal(k, (DEPTH_2, n), f32)

    dt = jnp.exp(jax.random.uniform(ks[11], (DEPTH_2, C_HEADS), f32, np.log(1e-3), np.log(1e-1)))
    return {
        'x': jax.random.normal(ks[0], (BATCH, SEQ, D_MODEL), f32),
        'ln_mix_pre': gain(ks[1], D_MODEL),
        'ln_mix_post': gain(ks[2], D_MODEL),
        'ln_mlp_pre': gain(ks[3], D_MODEL),
        'ln_mlp_post': gain(ks[4], D_MODEL),
        'w_in': jax.random.normal(ks[5], (DEPTH_2, D_MODEL, N_IN), f32) * D_MODEL ** -0.5,
        'hgrn_lb_logits': 0.1 * jax.random.normal(ks[6], (DEPTH_2, A_KEY), f32),
        'gla_w_gk': jax.random.normal(ks[7], (DEPTH_2, B_RANK, B_KEY), f32) * B_RANK ** -0.5,
        'gla_b_gk': 0.1 * jax.random.normal(ks[8], (DEPTH_2, B_KEY), f32),
        'gdn_conv': jax.random.normal(ks[9], (DEPTH_2, C_CONV, C_QKV), f32) * C_CONV ** -0.5,
        'gdn_a_log': jnp.log(jax.random.uniform(ks[10], (DEPTH_2, C_HEADS), f32, 1.0, 16.0)),
        'gdn_dt_bias': dt + jnp.log(-jnp.expm1(-dt)),
        'hgrn_onorm': gain(ks[12], A_DV),
        'gla_onorm': gain(ks[13], B_DV),
        'gdn_onorm': gain(ks[14], C_DV),
        'w_out': jax.random.normal(ks[15], (DEPTH_2, D_MODEL, D_MODEL), f32) * D_MODEL ** -0.5,
        'w_up': jax.random.normal(ks[16], (DEPTH_2, D_MODEL, D_FF), f32) * D_MODEL ** -0.5,
        'w_down': jax.random.normal(ks[17], (DEPTH_2, D_FF, D_MODEL), f32) * D_FF ** -0.5,
    }

def second_block(x, ln_mix_pre, ln_mix_post, ln_mlp_pre, ln_mlp_post, w_in, hgrn_lb_logits,
              gla_w_gk, gla_b_gk, gdn_conv, gdn_a_log, gdn_dt_bias, hgrn_onorm, gla_onorm,
              gdn_onorm, w_out, w_up, w_down):
    lb_cum = jnp.cumsum(jax.nn.softmax(hgrn_lb_logits.astype(jnp.float32), axis=0), axis=0)
    for layer in range(DEPTH_2):
        lb = jnp.clip(lb_cum[layer] - lb_cum[0], 0.0, 1.0)
        h = rmsnorm(x, ln_mix_pre[layer])
        mix = hybrid_mixer(h, w_in[layer], lb, gla_w_gk[layer], gla_b_gk[layer], gdn_conv[layer],
                           gdn_a_log[layer], gdn_dt_bias[layer], hgrn_onorm[layer], gla_onorm[layer],
                           gdn_onorm[layer], w_out[layer])
        x = x + rmsnorm(mix, ln_mix_post[layer]).astype(x.dtype)
        h = rmsnorm(x, ln_mlp_pre[layer])
        x = x + rmsnorm(squared_relu_mlp(h, w_up[layer], w_down[layer]), ln_mlp_post[layer]).astype(x.dtype)
    return x


_first_inputs = second_inputs


def second_inputs(seed=0):
    import zlib

    import numpy as np

    out = dict(_first_inputs(seed))
    spreads = {}
    factors = {'ln_mix_post': 3.722,
     'ln_mlp_pre': 14.725,
     'ln_mlp_post': 18.193,
     'gla_b_gk': 3.039,
     'hgrn_onorm': 33.405,
     'gla_onorm': 29.527,
     'gdn_onorm': 32.181}
    for name, (base, spread) in spreads.items():
        noise = np.random.default_rng([zlib.crc32(name.encode()), seed]).standard_normal(out[name].shape)
        drawn = base * np.exp(spread * noise) if base else spread * noise
        out[name] = __import__('jax').numpy.asarray(drawn.astype(out[name].dtype))
    for name, factor in factors.items():
        out[name] = (out[name] * factor).astype(out[name].dtype)
    return out


_narrow_inputs = second_inputs


def second_inputs(seed=0):

    out = dict(_narrow_inputs(seed))
    wider = {'ln_mlp_post': 3.31, 'hgrn_onorm': 5.07, 'gla_onorm': 5.08, 'gdn_onorm': 5.08}
    for name, times in wider.items():
        mean = out[name].mean()
        out[name] = (mean + times * (out[name] - mean)).astype(out[name].dtype)
    return out


def setup_inputs(seed=0):
    out = dict(first_inputs(seed))
    for name, value in second_inputs(seed + 1).items():
        if name != "x":
            out[name + "_2"] = value
    return out


def reference(
    x, c, ctx, c_ctx, norm_g, w_mod, b_mod, w_in, w_fourier, w_pool, pool_scale, qk_norm_g,
    lam_vecs, subln_g, w_out, ln_mix_pre_2, ln_mix_post_2, ln_mlp_pre_2, ln_mlp_post_2, w_in_2,
    hgrn_lb_logits_2, gla_w_gk_2, gla_b_gk_2, gdn_conv_2, gdn_a_log_2, gdn_dt_bias_2,
    hgrn_onorm_2, gla_onorm_2, gdn_onorm_2, w_out_2, w_up_2, w_down_2,
):
    x = first_block(
        x, c, ctx, c_ctx, norm_g, w_mod, b_mod, w_in, w_fourier, w_pool, pool_scale, qk_norm_g,
        lam_vecs, subln_g, w_out,
    )
    return second_block(
        x, ln_mix_pre_2, ln_mix_post_2, ln_mlp_pre_2, ln_mlp_post_2, w_in_2, hgrn_lb_logits_2,
        gla_w_gk_2, gla_b_gk_2, gdn_conv_2, gdn_a_log_2, gdn_dt_bias_2, hgrn_onorm_2,
        gla_onorm_2, gdn_onorm_2, w_out_2, w_up_2, w_down_2,
    )


_drawn_inputs = setup_inputs


def setup_inputs(seed=0):
    import zlib

    import numpy as np

    out = dict(_drawn_inputs(seed))
    spreads = {}
    factors = {'qk_norm_g': 8.0, 'lam_vecs': 2.81, 'subln_g': 3.789}
    for name, (base, spread) in spreads.items():
        noise = np.random.default_rng([zlib.crc32(name.encode()), seed]).standard_normal(out[name].shape)
        drawn = base * np.exp(spread * noise) if base else spread * noise
        out[name] = jnp.asarray(drawn.astype(out[name].dtype))
    for name, factor in factors.items():
        out[name] = (out[name] * factor).astype(out[name].dtype)
    return out
```

```python
from contextlib import ExitStack, contextmanager

import math

import concourse.bass as bass
import concourse.mybir as mybir

F32 = mybir.dt.float32
ALU = mybir.AluOpType
ACT = mybir.ActivationFunctionType
AX = mybir.AxisListType

P = 128
D = 1024
KD = D // P
SEQ, CTX = 1024, 256
NT, NTC = SEQ // P, CTX // P
NTA = NT + NTC
DEPTH = 2
EPS = 1e-6
CH = 512
FW = 256
HEADS, QK, DV = 4, 64, 128
Q0, K0, V0, G0, INW = 512, 1024, 1536, 2048, 3072
WINDOWS = (2, 4, 8, 16)

A_HEADS, B_HEADS, C_HEADS = 8, 4, 8
FF = 4096
CK = 128
NCK = SEQ // CK
LEVELS = 7


class Shared:
    pass


def ds(start, size):
    return bass.ds(start, size)


@contextmanager
def fresh_semaphores(nc):
    before = nc.snapshot_sems()
    yield
    nc.clear_and_free_semaphores(nc.allocated_since(before))
    nc.all_engine_barrier()


def load_constants(C):
    nc, ins = C.nc, C.ins
    with ExitStack() as st:
        s_in = nc.alloc_semaphore("c0_in")
        block = st.enter_context(nc.Block())

        @block.sync
        def _(sp):
            sp.dma_start(C.x_sb[:, 0:NT, :], ins["x"][0].rearrange("(t p) d -> p t d", p=P)).then_inc(s_in, 16)
            sp.dma_start(C.x_sb[:, NT:NTA, :], ins["ctx"][0].rearrange("(t p) d -> p t d", p=P)).then_inc(s_in, 16)
            sp.dma_start(C.ident[:], ins["t_ident"]).then_inc(s_in, 16)
            sp.wait_ge(s_in, 48)

        @block.gpsimd
        def _(pool):
            pool.memset(C.eps[:], EPS)
            pool.memset(C.zero[:], 0.0)
            pool.memset(C.ones[:], 1.0)


def modulation(C, l):
    nc, ins = C.nc, C.ins
    NCH = 3 * D // CH
    with ExitStack() as st:
        sb = lambda n, s: st.enter_context(nc.sbuf_tensor(f"m{l}_{n}", s, F32))
        sem = lambda n: nc.alloc_semaphore(f"m{l}_{n}")
        cT = sb("cT", [P, KD, 2])
        sc = sb("sc", [P, KD, 2])
        w = sb("w", [P, 2, KD, CH])
        bm = sb("bm", [2, 3 * D])
        mrow = sb("mrow", [2, 3 * D])
        sel = sb("sel", [2, 2, P])
        ng = sb("ng", [P, KD])
        lv = sb("lv", [P, 4, QK])
        lp = sb("lp", [P, 2, QK])
        ls = sb("ls", [P, 4])
        ps = st.enter_context(nc.psum_tensor(f"m{l}_ps", [P, 2, CH], F32))
        psT = st.enter_context(nc.psum_tensor(f"m{l}_psT", [P, 16, 2], F32))
        psG = st.enter_context(nc.psum_tensor(f"m{l}_psG", [P, 4, CH], F32))
        s_in = sem("small_loaded")
        s_w = [sem(f"w_loaded{b}") for b in range(2)]
        s_sc = sem("silu_ready")
        s_mm = sem("row_product_done")
        s_ev = sem("row_taken")
        s_T = sem("columns_transposed")
        s_G = sem("gates_spread")
        s_lp = sem("lam_sums")
        s_le = sem("lam_exps")
        block = st.enter_context(nc.Block())
        wv = ins["w_mod"][l].rearrange("(k p) n -> p k n", p=P)

        @block.sync
        def _(sp):
            with nc.allow_non_contiguous_dma("4 KB of channel vectors"):
                sp.dma_start(cT[:, :, 0], ins["c"][0].rearrange("(k p) -> p k", p=P)).then_inc(s_in, 16)
                sp.dma_start(cT[:, :, 1], ins["c_ctx"].rearrange("(k p) -> p k", p=P)).then_inc(s_in, 16)
                sp.dma_start(ng[:], ins["norm_g"][l].rearrange("(k p) -> p k", p=P)).then_inc(s_in, 16)
            for r in range(2):
                sp.dma_start(bm[r:r + 1, :], ins["b_mod"][l:l + 1, :]).then_inc(s_in, 16)
            sp.dma_start(sel[:], ins["t_sel"]).then_inc(s_in, 16)
            sp.dma_start(lv[:], ins["lam_vecs"][l].rearrange("a b -> (a b)").partition_broadcast(P)
                         .rearrange("p (a b) -> p a b", a=4)).then_inc(s_in, 16)
            for b in range(2):
                sp.dma_start(w[:, b], wv[:, :, b * CH:(b + 1) * CH]).then_inc(s_w[b], 16)
            with sp.Fori(1, NCH // 2) as i:
                for b in range(2):
                    sp.wait_ge(s_mm, 2 * i + b - 1)
                    sp.dma_start(w[:, b], wv[:, :, ds((2 * i + b) * CH, CH)]).then_inc(s_w[b], 16)

        @block.scalar
        def _(act):
            act.wait_ge(s_in, 16 * 7)
            act.activation(sc[:], cT[:], ACT.Silu).then_inc(s_sc, 1)
            act.wait_ge(s_lp, 1)
            act.activation(ls[:, 2:4], ls[:, 0:2], ACT.Exp).then_inc(s_le, 1)

        @block.tensor
        def _(pe):
            pe.wait_ge(s_sc, 1)
            with pe.Fori(0, NCH // 2) as i:
                for b in range(2):
                    pe.wait_ge(s_w[b], 16 * i + 16)
                    pe.wait_ge(s_ev, 2 * i + b + 1)
                    for k in range(KD):
                        mm = pe.matmul(ps[0:2, b, :], sc[:, k, :], w[:, b, k, :], start=(k == 0), stop=(k == KD - 1))
                    mm.then_inc(s_mm, 1)
            pe.wait_ge(s_ev, NCH + 2)
            for j in range(16):
                mm = pe.transpose(psT[:, j, :], mrow[:, j * P:(j + 1) * P], C.ident[0:2, 0:2])
            mm.then_inc(s_T, 1)
            for r in range(2):
                for h in range(2):
                    mm = pe.matmul(psG[:, 2 * r + h, :], sel[:, r, :], mrow[:, 2 * D + h * CH:2 * D + (h + 1) * CH],
                                   start=True, stop=True)
            mm.then_inc(s_G, 1)

        @block.vector
        def _(dve):
            dve.sem_inc(s_ev, 2)
            dve.wait_ge(s_in, 16 * 7)
            for r in range(2):
                dve.tensor_tensor(lp[:, r, :], lv[:, 2 * r, :], lv[:, 2 * r + 1, :], ALU.mult)
            dve.drain()
            dve.tensor_reduce(ls[:, 0:2], lp[:], AX.X, ALU.add).then_inc(s_lp, 1)
            dve.wait_ge(s_le, 1)
            dve.tensor_tensor(C.neglam[:], ls[:, 3:4], ls[:, 2:3], ALU.subtract)
            dve.drain()
            lam_init = 0.8 - 0.6 * math.exp(-0.3 * l)
            dve.tensor_scalar(C.neglam[:], C.neglam[:], lam_init, None, ALU.subtract)
            with dve.Fori(0, NCH // 2) as i:
                for b in range(2):
                    dve.wait_ge(s_mm, 2 * i + b + 1)
                    dve.tensor_tensor(mrow[:, ds((2 * i + b) * CH, CH)], ps[0:2, b, :],
                                      bm[:, ds((2 * i + b) * CH, CH)], ALU.add).then_inc(s_ev, 1)
            dve.wait_ge(s_T, 1)
            for r in range(2):
                dve.tensor_copy(C.shift[:, r, :], psT[:, 0:KD, r])
                dve.scalar_tensor_tensor(C.scale[:, r, :], psT[:, KD:2 * KD, r], 1.0, ng[:], ALU.add, ALU.mult)
            dve.wait_ge(s_G, 1)
            for r in range(2):
                for h in range(2):
                    dve.tensor_copy(C.gate[:, r, h * CH:(h + 1) * CH], psG[:, 2 * r + h, :])


def norm_transpose(C, tag, segs):
    nc = C.nc
    with ExitStack() as st:
        sb = lambda n, s: st.enter_context(nc.sbuf_tensor(f"{tag}_{n}", s, F32))
        sem = lambda n: nc.alloc_semaphore(f"{tag}_{n}")
        sq = sb("sq", [P, D])
        ms = sb("ms", [P, 2])
        ln = sb("ln", [P, 2])
        rs = sb("rs", [P, 2])
        xs = sb("xs", [P, 2, D])
        pt = st.enter_context(nc.psum_tensor(f"{tag}_pt", [P, 2, KD, P], F32))
        s_rs = sem("rs_ready")
        s_xs = sem("xs_ready")
        s_T = sem("transposed")
        s_eA = sem("taken_by_act")
        s_eD = sem("taken_by_dve")
        block = st.enter_context(nc.Block())
        bases, n = [], 0
        for _, m, _ in segs:
            bases.append(n)
            n += m

        @block.scalar
        def _(act):
            act.sem_inc(s_eA, 2)
            for (t0, m, r), n0 in zip(segs, bases):
                with act.Fori(0, m // 2) as i:
                    for b in range(2):
                        act.wait_ge(s_xs, n0 + 2 * i + b + 1)
                        act.activation(sq[:], C.x_sb[:, t0 + 2 * i + b, :], ACT.Square, accum_out=ms[:, b:b + 1])
                        act.drain()
                        act.activation(ln[:, b:b + 1], ms[:, b:b + 1], ACT.Ln, bias=C.eps[:], scale=1.0 / D)
                        act.drain()
                        act.activation(rs[:, b:b + 1], ln[:, b:b + 1], ACT.Exp, scale=-0.5).then_inc(s_rs, 1)
                    for b in range(2):
                        act.wait_ge(s_T, n0 + 2 * i + b + 3)
                        for k in range(KD // 2):
                            e = act.activation(C.hT[:, k, ds((t0 + 2 * i + b) * P, P)], pt[:, b, k, :], ACT.Identity,
                                               bias=C.shift[:, r, k:k + 1], scale=C.scale[:, r, k:k + 1])
                        e.then_inc(s_eA, 1)

        @block.vector
        def _(dve):
            dve.sem_inc(s_xs, 2)
            dve.sem_inc(s_eD, 2)
            for (t0, m, r), n0 in zip(segs, bases):
                with dve.Fori(0, m // 2) as i:
                    for b in range(2):
                        dve.wait_ge(s_rs, n0 + 2 * i + b + 1)
                        dve.wait_ge(s_T, n0 + 2 * i + b + 1)
                        dve.tensor_scalar(xs[:, b, :], C.x_sb[:, t0 + 2 * i + b, :], rs[:, b:b + 1], None,
                                          ALU.mult).then_inc(s_xs, 1)
                    for b in range(2):
                        dve.wait_ge(s_T, n0 + 2 * i + b + 3)
                        for k in range(KD // 2, KD):
                            e = dve.tensor_scalar(C.hT[:, k, ds((t0 + 2 * i + b) * P, P)], pt[:, b, k, :],
                                                  C.scale[:, r, k:k + 1], C.shift[:, r, k:k + 1], ALU.mult, ALU.add)
                        e.then_inc(s_eD, 1)

        @block.tensor
        def _(pe):
            pe.sem_inc(s_T, 2)
            for (t0, m, r), n0 in zip(segs, bases):
                with pe.Fori(0, m // 2) as i:
                    for b in range(2):
                        pe.wait_ge(s_xs, n0 + 2 * i + b + 3)
                        pe.wait_ge(s_eA, n0 + 2 * i + b + 1)
                        pe.wait_ge(s_eD, n0 + 2 * i + b + 1)
                        for k in range(KD):
                            mm = pe.transpose(pt[:, b, k, :], xs[:, b, k * P:(k + 1) * P], C.ident[:])
                        mm.then_inc(s_T, 1)


def project(C, tag, hT, segs):
    nc = C.nc
    NB = 4
    with ExitStack() as st:
        sb = lambda n, s: st.enter_context(nc.sbuf_tensor(f"{tag}_{n}", s, F32))
        sem = lambda n: nc.alloc_semaphore(f"{tag}_{n}")
        w = sb("w", [P, 2, KD, CH])
        stg = sb("stg", [P, NB, CH])
        ps = st.enter_context(nc.psum_tensor(f"{tag}_ps", [P, NB, CH], F32))
        s_w = [sem(f"w_loaded{b}") for b in range(2)]
        s_mm = sem("unit_done")
        s_eA = sem("taken_by_act")
        s_eD = sem("taken_by_dve")
        s_st = [sem(f"stored{q}") for q in range(NB)]
        block = st.enter_context(nc.Block())

        plan, n0, pr0 = [], 0, 0
        for s in segs:
            chunks = s["w"].shape[1] // CH
            per = len(s["tiles"]) if s["kind"] == "token" else 2 * (CH // P)
            plan.append(dict(s, pairs=chunks // 2, per=per, n0=n0, pr0=pr0,
                                        wv=s["w"].rearrange("(k p) n -> p k n", p=P)))
            assert (2 * per) % NB == 0 and chunks % 2 == 0
            n0 += chunks * per
            pr0 += chunks // 2
        total = n0

        @block.tensor
        def _(pe):
            for s in plan:
                with pe.Fori(0, s["pairs"]) as i:
                    for b in range(2):
                        pe.wait_ge(s_w[b], 16 * i + 16 * (s["pr0"] + 1))
                        for j in range(s["per"]):
                            u = b * s["per"] + j
                            n = s["n0"] + 2 * s["per"] * i + u
                            pe.wait_ge(s_eA if u % 2 == 0 else s_eD, s["n0"] // 2 + s["per"] * i + u // 2 + 1)
                            for k in range(KD):
                                if s["kind"] == "token":
                                    t = s["tiles"][j]
                                    lhsT, rhs = hT[:, k, t * P:(t + 1) * P], w[:, b, k, :]
                                else:
                                    c, h = j // 2, j % 2
                                    lhsT, rhs = w[:, b, k, c * P:(c + 1) * P], hT[:, k, h * CH:(h + 1) * CH]
                                mm = pe.matmul(ps[:, u % NB, :], lhsT, rhs, start=(k == 0), stop=(k == KD - 1))
                            mm.then_inc(s_mm, 1)

        @block.scalar
        def _(act):
            act.sem_inc(s_eA, 2)
            for b in range(2):
                act.dma_start(w[:, b], plan[0]["wv"][:, :, b * CH:(b + 1) * CH]).then_inc(s_w[b], 16)

            def evacuate(s, i, b):
                for j in range(s["per"]):
                    u = b * s["per"] + j
                    if u % 2 == 0:
                        act.wait_ge(s_mm, s["n0"] + 2 * s["per"] * i + u + 1)
                        act.wait_ge(s_st[u % NB], 16 * (s["n0"] // NB + (2 * s["per"] // NB) * i + u // NB + 1))
                        act.copy(stg[:, u % NB, :], ps[:, u % NB, :]).then_inc(s_eA, 1)
                act.wait_ge(s_mm, s["n0"] + 2 * s["per"] * i + (b + 1) * s["per"])

            for q, s in enumerate(plan):
                if s["pairs"] > 1:
                    with act.Fori(0, s["pairs"] - 1) as i:
                        for b in range(2):
                            evacuate(s, i, b)
                            act.dma_start(w[:, b], s["wv"][:, :, ds((2 * i + 2 + b) * CH, CH)]).then_inc(s_w[b], 16)
                for b in range(2):
                    evacuate(s, s["pairs"] - 1, b)
                    if q + 1 < len(plan):
                        act.dma_start(w[:, b], plan[q + 1]["wv"][:, :, b * CH:(b + 1) * CH]).then_inc(s_w[b], 16)

        @block.vector
        def _(dve):
            dve.sem_inc(s_eD, 2)
            for s in plan:
                with dve.Fori(0, s["pairs"]) as i:
                    for u in range(1, 2 * s["per"], 2):
                        dve.wait_ge(s_mm, s["n0"] + 2 * s["per"] * i + u + 1)
                        dve.wait_ge(s_st[u % NB], 16 * (s["n0"] // NB + (2 * s["per"] // NB) * i + u // NB + 1))
                        dve.tensor_copy(stg[:, u % NB, :], ps[:, u % NB, :]).then_inc(s_eD, 1)

        @block.sync
        def _(sp):
            for q in range(NB):
                sp.sem_inc(s_st[q], 16)
            for s in plan:
                with sp.Fori(0, s["pairs"]) as i:
                    for b in range(2):
                        for j in range(s["per"]):
                            u = b * s["per"] + j
                            sp.wait_ge(s_eA if u % 2 == 0 else s_eD, s["n0"] // 2 + s["per"] * i + u // 2 + 3)
                            if s["kind"] == "token":
                                t = s["tiles"][j]
                                dst = s["out"][t * P:(t + 1) * P, ds((2 * i + b) * CH, CH)]
                            else:
                                c, h = j // 2, j % 2
                                dst = s["out"][ds((2 * i + b) * CH + c * P, P), h * CH:(h + 1) * CH]
                            sp.dma_start(dst, stg[:, u % NB, :]).then_inc(s_st[u % NB], 16)
            for q in range(NB):
                sp.wait_ge(s_st[q], 16 * (total // NB + 1))


def fourier_pool(C, l, rows):
    nc, ins = C.nc, C.ins
    tiles, r0 = (NT, 0) if rows == "x" else (NTC, SEQ)
    length = tiles * P
    N = min(CH, length)
    NH = length // N
    tag = f"f{l}{rows}"
    with ExitStack() as st:
        sb = lambda n, s: st.enter_context(nc.sbuf_tensor(f"{tag}_{n}", s, F32))
        sem = lambda n: nc.alloc_semaphore(f"{tag}_{n}")
        ab = sb("ab", [P, tiles, 2 * FW])
        dft = sb("dft", [P, 2, tiles, N])
        chan = sb("chan", [P, 2, P])
        band = sb("band", [P, 5, 4, P])
        wfb = sb("wfb", [P, 2, P])
        wpb = sb("wpb", [P, 2, P])
        psc = sb("psc", [P, 2, P])
        G = sb("G", [P, 2, 2, P])
        yt = sb("yt", [P, 2, 2, length])
        pool = sb("pool", [P, 2, length])
        pg = st.enter_context(nc.psum_tensor(f"{tag}_pg", [P, 2, 2, P], F32))
        py = st.enter_context(nc.psum_tensor(f"{tag}_py", [P, 2, CH], F32))
        pp = st.enter_context(nc.psum_tensor(f"{tag}_pp", [P, 2, CH], F32))
        po = st.enter_context(nc.psum_tensor(f"{tag}_po", [P, 2, CH], F32))
        s_ab = sem("ab_loaded")
        s_tab = sem("tables_loaded")
        s_z = sem("diagonals_zeroed")
        s_wd = sem("diagonals_loaded")
        s_wp = sem("w_pool_scaled")
        s_dft = [sem(f"dft_loaded{b}") for b in range(2)]
        s_g = sem("G_product")
        s_gc = sem("G_ready")
        s_y = sem("token_dft")
        s_yc = sem("token_dft_taken")
        s_p = sem("pooled")
        s_pc = sem("pooled_taken")
        s_o = sem("branch_out")
        s_oc = sem("branch_out_taken")
        block = st.enter_context(nc.Block())
        table = ins["t_dft_x" if rows == "x" else "t_dft_c"]
        order = [(h, g) for h in range(NH) for g in range(2)]

        def table_chunk(h, g):
            return table[g].rearrange("(k p) n -> p k n", p=P)[:, :, h * N:(h + 1) * N]

        @block.sync
        def _(sp):
            sp.dma_start(ab[:], C.p_dram[r0:r0 + length, 0:2 * FW].rearrange("(t p) n -> p t n", p=P)).then_inc(s_ab, 16)
            for q, (h, g) in enumerate(order):
                if q >= 2:
                    sp.wait_ge(s_y, 2 * (q - 1))
                sp.dma_start(dft[:, q % 2], table_chunk(h, g)).then_inc(s_dft[q % 2], 16)

        @block.gpsimd
        def _(pool_eng):
            pool_eng.memset(wfb[:], 0.0).then_inc(s_z, 1)
            pool_eng.memset(wpb[:], 0.0).then_inc(s_z, 1)
            pool_eng.dma_start(chan[:], ins["t_chan"].rearrange("g p n -> p g n")).then_inc(s_tab, 16)
            pool_eng.dma_start(band[:], ins["t_band"]).then_inc(s_tab, 16)
            pool_eng.dma_start(psc[:].rearrange("p a b -> p (a b)"),
                               ins["pool_scale"][l].partition_broadcast(P)).then_inc(s_tab, 16)
            pool_eng.wait_ge(s_z, 2)
            for g in range(4):
                o = QK * (g % 2)
                pool_eng.dma_start(wfb[o:o + QK, g // 2, o:o + QK], ins["w_fourier"][l, g]).then_inc(s_wd, 16)
                pool_eng.dma_start(wpb[o:o + QK, g // 2, o:o + QK], ins["w_pool"][l, g]).then_inc(s_wd, 16)

        @block.tensor
        def _(pe):
            pe.wait_ge(s_tab, 48)
            pe.wait_ge(s_wd, 16 * 8)
            for g in range(2):
                for c in range(2):
                    mm = pe.matmul(pg[:, g, c, :], chan[:, g, :], wfb[:, c, :], start=True, stop=True)
            mm.then_inc(s_g, 1)
            pe.wait_ge(s_ab, 16)
            for q, (h, g) in enumerate(order):
                pe.wait_ge(s_dft[q % 2], 16 * (q // 2 + 1))
                for c in range(2):
                    if q >= 1:
                        pe.wait_ge(s_yc, 2 * (q - 1) + c + 1)
                    for k in range(tiles):
                        mm = pe.matmul(py[:, c, 0:N], ab[:, k, c * P:(c + 1) * P], dft[:, q % 2, k, :],
                                       start=(k == 0), stop=(k == tiles - 1))
                    mm.then_inc(s_y, 1)
            for t in range(tiles):
                if t >= 2:
                    pe.wait_ge(s_pc, t - 1)
                for g in range(4):
                    near = [(t, 0 if t == 0 else 2 if t == tiles - 1 else 1)]
                    near += [(t - 1, 3)] * (t > 0) + [(t + 1, 4)] * (t < tiles - 1)
                    o = QK * (g % 2)
                    for q, (src, kind) in enumerate(near):
                        mm = pe.matmul(pp[o:o + QK, t % 2, (g // 2) * P:(g // 2 + 1) * P],
                                       ab[:, src, FW + g * QK:FW + (g + 1) * QK], band[:, kind, g, :],
                                       start=(q == 0), stop=(q == len(near) - 1))
                mm.then_inc(s_p, 1)
            pe.wait_ge(s_gc, 1)
            pe.wait_ge(s_wp, 1)
            pe.wait_ge(s_yc, 2 * len(order))
            for t in range(tiles):
                pe.wait_ge(s_pc, t + 1)
                if t >= 2:
                    pe.wait_ge(s_oc, t - 1)
                for c in range(2):
                    for g in range(2):
                        pe.matmul(po[:, t % 2, c * P:(c + 1) * P], yt[:, g, c, t * P:(t + 1) * P], G[:, g, c, :],
                                  start=(g == 0), stop=(g == 1))
                for c in range(2):
                    mm = pe.matmul(po[:, t % 2, FW + c * P:FW + (c + 1) * P], pool[:, c, t * P:(t + 1) * P],
                                   wpb[:, c, :], start=True, stop=True)
                mm.then_inc(s_o, 1)

        @block.scalar
        def _(act):
            for q, (h, g) in enumerate(order):
                for c in range(2):
                    act.wait_ge(s_y, 2 * q + c + 1)
                    act.copy(yt[:, g, c, h * N:(h + 1) * N], py[:, c, 0:N]).then_inc(s_yc, 1)

        @block.vector
        def _(dve):
            dve.wait_ge(s_tab, 48)
            dve.wait_ge(s_wd, 16 * 8)
            dve.tensor_tensor(wpb[:], wpb[:], psc[:], ALU.mult).then_inc(s_wp, 1)
            dve.wait_ge(s_g, 1)
            dve.tensor_copy(G[:], pg[:]).then_inc(s_gc, 1)
            for t in range(tiles):
                dve.wait_ge(s_p, t + 1)
                dve.tensor_copy(pool[:, :, t * P:(t + 1) * P],
                                pp[:, t % 2, 0:2 * P].rearrange("p (c n) -> p c n", c=2)).then_inc(s_pc, 1)
            for t in range(tiles):
                dve.wait_ge(s_o, t + 1)
                dve.tensor_copy(C.mix[:, r0 // P + t, 0:2 * FW], po[:, t % 2, :]).then_inc(s_oc, 1)


def qk_prepare(C, l):
    nc, ins = C.nc, C.ins
    NG = 16
    with ExitStack() as st:
        sb = lambda n, s: st.enter_context(nc.sbuf_tensor(f"q{l}_{n}", s, F32))
        sem = lambda n: nc.alloc_semaphore(f"q{l}_{n}")
        raw = sb("raw", [P, 2, 2 * 512])
        sq = sb("sq", [P, 2, 2 * 512])
        st1 = sb("st1", [P, 2, NG])
        rs = sb("rs", [P, 2, NG])
        nrm = sb("nrm", [P, 2, 2 * 512])
        t1 = sb("t1", [P, 2 * 512])
        gq = sb("gq", [P, 2, QK])
        cs = sb("cs", [P, 2, NT, QK])
        pt = st.enter_context(nc.psum_tensor(f"q{l}_pt", [P, 2, 8, P], F32))
        s_v = sem("v_loaded")
        s_tab = sem("tables_loaded")
        s_raw = [sem(f"qk_loaded{b}") for b in range(2)]
        s_ms = sem("sums_ready")
        s_rs = sem("rs_ready")
        s_n = sem("normed")
        s_T = sem("transposed")
        s_eA = sem("q_taken")
        s_eD = sem("k_taken")
        block = st.enter_context(nc.Block())

        def src(n):
            return C.p_dram[ds(n * P, P), Q0:V0]

        @block.sync
        def _(sp):
            sp.dma_start(gq[:].rearrange("p a b -> p (a b)"),
                         ins["qk_norm_g"][l].rearrange("a b -> (a b)").partition_broadcast(P)).then_inc(s_tab, 16)
            for q in range(2):
                sp.dma_start(cs[:, q], ins["t_rope"][q].rearrange("(t p) n -> p t n", p=P)).then_inc(s_tab, 16)
            for b in range(2):
                sp.dma_start(raw[:, b, :], src(b)).then_inc(s_raw[b], 16)
            with sp.Fori(1, NT // 2) as i:
                for b in range(2):
                    sp.wait_ge(s_n, 2 * i + b - 1)
                    sp.dma_start(raw[:, b, :], src(2 * i + b)).then_inc(s_raw[b], 16)
            for b in range(2):
                sp.wait_ge(s_n, NT - 1 + b)
                if l < DEPTH - 1:
                    sp.dma_start(raw[:, b, :], src(NT + b)).then_inc(s_raw[b], 16)
                else:
                    sp.dma_start(raw[:, b, 512:1024], C.p_dram[(NT + b) * P:(NT + b + 1) * P, K0:V0]).then_inc(s_raw[b], 16)
            sp.dma_start(C.v_sb[:], C.p_dram[:, V0:G0].rearrange("(t p) n -> p t n", p=P)).then_inc(s_v, 16)
            sp.wait_ge(s_v, 16)

        def cols(ctx_tile):
            return (512, 1024) if ctx_tile and l == DEPTH - 1 else (0, 1024)

        @block.scalar
        def _(act):
            act.sem_inc(s_eA, 2)

            def take_q(n, b, ctx_tile):
                act.wait_ge(s_T, n + 3)
                if cols(ctx_tile)[0] == 0:
                    e = act.copy(C.qT[:, :, ds(n * P, P)], pt[:, b, 0:4, :])
                    e.then_inc(s_eA, 1)
                else:
                    act.sem_inc(s_eA, 1)

            with act.Fori(0, NT // 2) as i:
                for b in range(2):
                    act.wait_ge(s_ms, 2 * i + b + 1)
                    act.activation(rs[:, b, :], st1[:, b, :], ACT.Ln, bias=C.eps[:], scale=1.0 / QK)
                    act.drain()
                    act.activation(rs[:, b, :], rs[:, b, :], ACT.Exp, scale=-0.5).then_inc(s_rs, 1)
                for b in range(2):
                    take_q(2 * i + b, b, False)
            for b in range(2):
                a, z = cols(True)
                act.wait_ge(s_ms, NT + b + 1)
                act.activation(rs[:, b, a // QK:z // QK], st1[:, b, a // QK:z // QK], ACT.Ln, bias=C.eps[:], scale=1.0 / QK)
                act.drain()
                act.activation(rs[:, b, a // QK:z // QK], rs[:, b, a // QK:z // QK], ACT.Exp, scale=-0.5).then_inc(s_rs, 1)
            for b in range(2):
                take_q(NT + b, b, True)

        @block.vector
        def _(dve):
            dve.sem_inc(s_eD, 2)
            dve.wait_ge(s_tab, 48)

            def tile_stats(n, b, load, ctx_tile):
                a, z = cols(ctx_tile)
                dve.wait_ge(s_raw[b], load)
                dve.tensor_tensor(sq[:, b, a:z], raw[:, b, a:z], raw[:, b, a:z], ALU.mult)
                dve.drain()
                dve.tensor_reduce(st1[:, b, a // QK:z // QK], sq[:, b, a:z].rearrange("p (g n) -> p g n", n=QK), AX.X,
                                  ALU.add).then_inc(s_ms, 1)

            def tile_norm(n, b, ctx_tile):
                a, z = cols(ctx_tile)
                ng = (z - a) // QK
                dve.wait_ge(s_rs, n + 1)
                dve.wait_ge(s_T, n + 1)
                out = nrm[:, b, a:z].rearrange("p (g n) -> p g n", n=QK)
                dve.tensor_tensor(out, raw[:, b, a:z].rearrange("p (g n) -> p g n", n=QK),
                                  rs[:, b, a // QK:z // QK].unsqueeze(2).to_broadcast([P, ng, QK]), ALU.mult)
                dve.drain()
                for w in range(a // 512, 2):
                    o = nrm[:, b, w * 512:(w + 1) * 512].rearrange("p (g n) -> p g n", n=QK)
                    e = dve.tensor_tensor(o, o, gq[:, w, :].unsqueeze(1).to_broadcast([P, 8, QK]), ALU.mult)
                if ctx_tile:
                    e.then_inc(s_n, 1)
                    return
                dve.drain()
                v = nrm[:, b, :].rearrange("p (g a h n) -> p g a h n", a=2, h=2, n=16)
                r = t1[:].rearrange("p (g a h n) -> p g a h n", a=2, h=2, n=16)
                for ax in range(2):
                    for h in range(2):
                        sine = cs[:, 1, ds(n, 1), :].rearrange("p t (a h n) -> p (t a) h n", a=2, h=2)[:, ax, h, :]
                        dve.tensor_tensor(r[:, :, ax, h, :], v[:, :, ax, 1 - h, :],
                                          sine.unsqueeze(1).to_broadcast([P, NG, 16]), ALU.mult)
                dve.drain()
                cosine = cs[:, 0, ds(n, 1), :].rearrange("p t n -> p (t n)")
                dve.tensor_tensor(out, out, cosine.unsqueeze(1).to_broadcast([P, NG, QK]), ALU.mult)
                dve.drain()
                dve.tensor_tensor(nrm[:, b, :], nrm[:, b, :], t1[:], ALU.add).then_inc(s_n, 1)

            def take_k(n, b):
                dve.wait_ge(s_T, n + 3)
                dve.tensor_copy(C.kT[:, :, ds(n * P, P)], pt[:, b, 4:8, :]).then_inc(s_eD, 1)

            with dve.Fori(0, NT // 2) as i:
                for b in range(2):
                    tile_stats(2 * i + b, b, 16 * i + 16, False)
                for b in range(2):
                    tile_norm(2 * i + b, b, False)
                for b in range(2):
                    take_k(2 * i + b, b)
            for b in range(2):
                tile_stats(NT + b, b, 16 * (NT // 2) + 16, True)
            for b in range(2):
                tile_norm(NT + b, b, True)
            for b in range(2):
                take_k(NT + b, b)

        @block.tensor
        def _(pe):
            pe.sem_inc(s_T, 2)

            def turn(n, b, ctx_tile):
                pe.wait_ge(s_n, n + 1)
                pe.wait_ge(s_eA, n + 1)
                pe.wait_ge(s_eD, n + 1)
                for c in range(cols(ctx_tile)[0] // P, 8):
                    mm = pe.transpose(pt[:, b, c, :], nrm[:, b, c * P:(c + 1) * P], C.ident[:])
                mm.then_inc(s_T, 1)

            with pe.Fori(0, NT // 2) as i:
                for b in range(2):
                    turn(2 * i + b, b, False)
            for b in range(2):
                turn(NT + b, b, True)


def attention(C, l):
    nc = C.nc
    SCALE = QK ** -0.5
    segs = [(NT, 0, 0, SEQ + CTX)] + ([(NTC, NT, SEQ, CTX)] if l < DEPTH - 1 else [])
    with ExitStack() as st:
        sb = lambda n, s: st.enter_context(nc.sbuf_tensor(f"a{l}_{n}", s, F32))
        sem = lambda n: nc.alloc_semaphore(f"a{l}_{n}")
        qs = sb("qs", [P, 2, P])
        pr = sb("pr", [P, 2, 2, SEQ + CTX])
        df = sb("df", [P, SEQ + CTX])
        pT = sb("pT", [P, NTA, P])
        mx = sb("mx", [P, 2, 4])
        nb = sb("nb", [P, 2, 2])
        sm = sb("sm", [P, 2, 2])
        ri = sb("ri", [P, 2, 4])
        sc = st.enter_context(nc.psum_tensor(f"a{l}_sc", [P, 2, 3, CH], F32))
        tp = st.enter_context(nc.psum_tensor(f"a{l}_tp", [P, 2, CH], F32))
        s_q = sem("query_staged")
        s_s = sem("scores_done")
        s_m = sem("max_ready")
        s_e = sem("exp_done")
        s_d = sem("difference_ready")
        s_t = sem("probs_transposed")
        s_tc = sem("transposed_taken")
        s_o = sem("pv_done")
        s_oc = sem("pv_taken")
        block = st.enter_context(nc.Block())

        bases, tot = [], 0
        for m, *_ in segs:
            bases.append(tot)
            tot += HEADS * m

        def walk(eng, before, lead, after):
            for (m, *seg), base in zip(segs, bases):
                for h in range(HEADS):
                    n0 = base + m * h
                    lead(n0, h, 0, 0, *seg)
                    if m > 2:
                        with eng.Fori(0, (m - 2) // 2) as i:
                            for b in range(2):
                                t = 2 * i + b
                                before(n0 + t, h, t, b, *seg)
                                lead(n0 + t + 1, h, t + 1, 1 - b, *seg)
                                after(n0 + t, h, t, b, *seg)
                    before(n0 + m - 2, h, m - 2, 0, *seg)
                    lead(n0 + m - 1, h, m - 1, 1, *seg)
                    after(n0 + m - 2, h, m - 2, 0, *seg)
                    before(n0 + m - 1, h, m - 1, 1, *seg)
                    after(n0 + m - 1, h, m - 1, 1, *seg)

        nothing = lambda *a: None

        def batches(nk):
            tiles = list(range(nk // P))
            return [tiles[i:i + 4] for i in range(0, len(tiles), 4)]

        nbt = [len(batches(s[3])) for s in segs]
        t_base = [0, HEADS * segs[0][0] * nbt[0]]

        def tn(n, base_index, q):
            base, per = bases[base_index], nbt[base_index]
            return t_base[base_index] + (n - base) * per + q

        def seg_of(t0):
            return [s[1] for s in segs].index(t0)

        @block.gpsimd
        def _(pool):
            def stage(n, h, t, b, t0, k0, nk):
                pool.wait_ge(s_s, 2 * n + 2)
                pool.tensor_copy(qs[:, b, :], C.qT[:, h, ds((t0 + t) * P, P)]).then_inc(s_q, 1)
            walk(pool, nothing, stage, nothing)

        @block.tensor
        def _(pe):
            pe.sem_inc(s_s, 4)

            def scores(n, h, t, b, t0, k0, nk):
                pe.wait_ge(s_q, n + 1)
                for m in range(2):
                    pe.wait_ge(s_e, 2 * n + m + 1)
                    for j, c in enumerate(range(0, nk, CH)):
                        w = min(CH, nk - c)
                        mm = pe.matmul(sc[:, m, j, 0:w], qs[m * QK:(m + 1) * QK, b, :],
                                       C.kT[m * QK:(m + 1) * QK, h, k0 + c:k0 + c + w], start=True, stop=True)
                    mm.then_inc(s_s, 1)

            def rest(n, h, t, b, t0, k0, nk):
                g = seg_of(t0)
                pe.wait_ge(s_d, n + 3)
                for q, tiles in enumerate(batches(nk)):
                    if q == 1 or nbt[g] == 1:
                        pe.wait_ge(s_oc, n + 1)
                    if q == 2:
                        pe.wait_ge(s_tc, tn(n, g, 1))
                    for k in tiles:
                        mm = pe.transpose(tp[:, q % 2, (k % 4) * P:(k % 4 + 1) * P], df[:, k * P:(k + 1) * P], C.ident[:])
                    mm.then_inc(s_t, 1)
                pe.wait_ge(s_tc, tn(n, g, nbt[g]))
                for k in range(nk // P):
                    mm = pe.matmul(tp[:, 1, 0:P], pT[:, k, :], C.v_sb[:, k0 // P + k, h * DV:(h + 1) * DV],
                                   start=(k == 0), stop=(k == nk // P - 1))
                mm.then_inc(s_o, 1)
            walk(pe, nothing, scores, rest)

        @block.scalar
        def _(act):
            act.sem_inc(s_e, 2)

            def exps(n, h, t, b, t0, k0, nk):
                act.wait_ge(s_d, n + 1)
                for m in range(2):
                    act.wait_ge(s_m, 2 * n + m + 1)
                    act.activation(pr[:, b, m, 0:nk], sc[:, m].rearrange("p a b -> p (a b)")[:, 0:nk], ACT.Exp,
                                   bias=nb[:, b, m:m + 1], scale=SCALE, accum_out=sm[:, b, m:m + 1]).then_inc(s_e, 1)

            def rest(n, h, t, b, t0, k0, nk):
                g = seg_of(t0)
                for q, tiles in enumerate(batches(nk)):
                    act.wait_ge(s_t, tn(n, g, q) + 1)
                    act.copy(pT[:, tiles[0]:tiles[-1] + 1, :].rearrange("p a b -> p (a b)"),
                             tp[:, q % 2, 0:len(tiles) * P]).then_inc(s_tc, 1)
            walk(act, rest, exps, nothing)

        @block.vector
        def _(dve):
            dve.sem_inc(s_oc, 1)
            dve.sem_inc(s_d, 2)

            def maxima(n, h, t, b, t0, k0, nk):
                for m in range(2):
                    dve.wait_ge(s_s, 2 * n + m + 5)
                    dve.tensor_reduce(mx[:, b, m:m + 1], sc[:, m].rearrange("p a b -> p (a b)")[:, 0:nk], AX.X, ALU.max)
                    dve.drain()
                    dve.tensor_scalar(nb[:, b, m:m + 1], mx[:, b, m:m + 1], -SCALE, None, ALU.mult).then_inc(s_m, 1)

            def combine(n, h, t, b, t0, k0, nk):
                dve.wait_ge(s_e, 2 * n + 4)
                dve.reciprocal(ri[:, b, 0:2], sm[:, b, 0:2])
                dve.drain()
                dve.scalar_tensor_tensor(ri[:, b, 2:3], ri[:, b, 1:2], sm[:, b, 0:1], C.neglam[:], ALU.mult, ALU.mult)
                dve.drain()
                dve.scalar_tensor_tensor(df[:, 0:nk], pr[:, b, 1, 0:nk], ri[:, b, 2:3], pr[:, b, 0, 0:nk],
                                         ALU.mult, ALU.add).then_inc(s_d, 1)

            def take(n, h, t, b, t0, k0, nk):
                dve.wait_ge(s_o, n + 1)
                dve.tensor_scalar(C.mix[:, ds(t0 + t, 1), 2 * FW + h * DV:2 * FW + (h + 1) * DV].rearrange("p t n -> p (t n)"),
                                  tp[:, 1, 0:P], ri[:, b, 0:1], None, ALU.mult).then_inc(s_oc, 1)
            walk(dve, combine, maxima, take)


def mix_out(C, l):
    nc, ins = C.nc, C.ins
    lam_init = 0.8 - 0.6 * math.exp(-0.3 * l)
    segs = [(NT, 0, 0)] + ([(NTC, NT, 1)] if l < DEPTH - 1 else [])
    tiles = sum(m for m, *_ in segs)
    with ExitStack() as st:
        sb = lambda n, s: st.enter_context(nc.sbuf_tensor(f"o{l}_{n}", s, F32))
        sem = lambda n: nc.alloc_semaphore(f"o{l}_{n}")
        w = sb("w", [P, KD, D])
        g = sb("g", [P, 2, D])
        sg = sb("sg", [P, 2, D])
        sq = sb("sq", [P, 2, 512])
        ms = sb("ms", [P, 2, HEADS])
        rs = sb("rs", [P, 2, HEADS])
        sub = sb("sub", [P, DV])
        y = sb("y", [P, 2, D])
        yT = sb("yT", [P, 2, KD, P])
        up = sb("up", [P, 2, D])
        pt = st.enter_context(nc.psum_tensor(f"o{l}_pt", [P, KD, P], F32))
        po = st.enter_context(nc.psum_tensor(f"o{l}_po", [P, 2, 2, CH], F32))
        s_w = sem("w_loaded")
        s_sub = sem("subln_loaded")
        s_g = [sem(f"gate_loaded{b}") for b in range(2)]
        s_sg = sem("silu_ready")
        s_ms = sem("head_sums")
        s_rs = sem("head_rs")
        s_y = sem("y_ready")
        s_T = sem("y_transposed")
        s_cA = sem("yT_taken_act")
        s_cD = sem("yT_taken_dve")
        s_o = sem("product_done")
        s_x = sem("x_updated")
        block = st.enter_context(nc.Block())

        @block.sync
        def _(sp):
            def load(n, b):
                sp.dma_start(g[:, b, :], C.p_dram[ds(n * P, P), G0:INW]).then_inc(s_g[b], 16)
            sp.dma_start(sub[:], ins["subln_g"][l].partition_broadcast(P)).then_inc(s_sub, 16)
            for b in range(2):
                load(b, b)
            sp.dma_start(w[:], ins["w_out"][l].rearrange("(k p) n -> p k n", p=P)).then_inc(s_w, 16)
            with sp.Fori(1, tiles // 2) as i:
                for b in range(2):
                    sp.wait_ge(s_sg, 2 * i + b - 1)
                    load(2 * i + b, b)

        @block.scalar
        def _(act):
            act.sem_inc(s_cA, 1)
            for m, t0, r in segs:
                with act.Fori(t0 // 2, (t0 + m) // 2) as i:
                    for b in range(2):
                        act.wait_ge(s_g[b], 16 * i + 16)
                        act.wait_ge(s_y, 2 * i + b + 1)
                        act.activation(sg[:, b, :], g[:, b, :], ACT.Silu).then_inc(s_sg, 1)
                    for b in range(2):
                        act.wait_ge(s_ms, 2 * i + b + 1)
                        act.activation(rs[:, b, :], ms[:, b, :], ACT.Ln, bias=C.eps[:], scale=1.0 / DV)
                        act.drain()
                        act.activation(rs[:, b, :], rs[:, b, :], ACT.Exp, scale=-0.5).then_inc(s_rs, 1)
                    for b in range(2):
                        act.wait_ge(s_T, 2 * i + b + 3)
                        act.wait_ge(s_o, 2 * i + b + 1)
                        act.copy(yT[:, b, 0:4, :], pt[:, 0:4, :]).then_inc(s_cA, 1)

        @block.vector
        def _(dve):
            dve.sem_inc(s_y, 2)
            dve.sem_inc(s_cD, 1)
            dve.sem_inc(s_x, 2)
            dve.wait_ge(s_sub, 16)
            dve.tensor_scalar(sub[:], sub[:], 1.0 - lam_init, None, ALU.mult)
            dve.drain()
            for m, t0, r in segs:
                with dve.Fori(t0 // 2, (t0 + m) // 2) as i:
                    for b in range(2):
                        o = C.mix[:, ds(2 * i + b, 1), 2 * FW:D].rearrange("p t n -> p (t n)")
                        dve.tensor_tensor(sq[:, b], o, o, ALU.mult)
                        dve.drain()
                        dve.tensor_reduce(ms[:, b, :], sq[:, b].rearrange("p (h n) -> p h n", h=HEADS), AX.X, ALU.add).then_inc(s_ms, 1)
                    for b in range(2):
                        dve.wait_ge(s_sg, 2 * i + b + 1)
                        dve.wait_ge(s_T, 2 * i + b + 1)
                        f = C.mix[:, ds(2 * i + b, 1), 0:2 * FW].rearrange("p t n -> p (t n)")
                        o = C.mix[:, ds(2 * i + b, 1), 2 * FW:D].rearrange("p t n -> p (t n)")
                        dve.tensor_tensor(y[:, b, 0:2 * FW], f, sg[:, b, 0:2 * FW], ALU.mult)
                        s = sg[:, b, 2 * FW:D].rearrange("p (h n) -> p h n", h=HEADS)
                        dve.tensor_tensor(s, s, sub[:].unsqueeze(1).to_broadcast([P, HEADS, DV]), ALU.mult)
                        dve.drain()
                        dve.wait_ge(s_rs, 2 * i + b + 1)
                        for h in range(HEADS):
                            e = dve.scalar_tensor_tensor(y[:, b, 2 * FW + h * DV:2 * FW + (h + 1) * DV],
                                                         o[:, h * DV:(h + 1) * DV], rs[:, b, h:h + 1],
                                                         sg[:, b, 2 * FW + h * DV:2 * FW + (h + 1) * DV], ALU.mult, ALU.mult)
                        e.then_inc(s_y, 1)
                    for b in range(2):
                        dve.wait_ge(s_T, 2 * i + b + 3)
                        dve.wait_ge(s_o, 2 * i + b + 1)
                        dve.tensor_copy(yT[:, b, 4:8, :], pt[:, 4:8, :]).then_inc(s_cD, 1)
                    for b in range(2):
                        dve.wait_ge(s_o, 2 * i + b + 3)
                        for h in range(2):
                            dve.tensor_tensor(up[:, b, h * CH:(h + 1) * CH], po[:, b, h, :],
                                              C.gate[:, r, h * CH:(h + 1) * CH], ALU.mult)
                        dve.drain()
                        x = C.x_sb[:, ds(2 * i + b, 1), :].rearrange("p t n -> p (t n)")
                        dve.tensor_tensor(x, x, up[:, b, :], ALU.add).then_inc(s_x, 1)

        @block.tensor
        def _(pe):
            pe.sem_inc(s_o, 2)
            pe.sem_inc(s_T, 2)
            pe.wait_ge(s_w, 16)
            for m, t0, r in segs:
                with pe.Fori(t0 // 2, (t0 + m) // 2) as i:
                    for b in range(2):
                        pe.wait_ge(s_y, 2 * i + b + 3)
                        pe.wait_ge(s_cA, 2 * i + b + 1)
                        pe.wait_ge(s_cD, 2 * i + b + 1)
                        for k in range(KD):
                            mm = pe.transpose(pt[:, k, :], y[:, b, k * P:(k + 1) * P], C.ident[:])
                        mm.then_inc(s_T, 1)
                    for b in range(2):
                        pe.wait_ge(s_cA, 2 * i + b + 2)
                        pe.wait_ge(s_cD, 2 * i + b + 2)
                        pe.wait_ge(s_x, 2 * i + b + 1)
                        for h in range(2):
                            for k in range(KD):
                                mm = pe.matmul(po[:, b, h, :], yT[:, b, k, :], w[:, k, h * CH:(h + 1) * CH],
                                               start=(k == 0), stop=(k == KD - 1))
                        mm.then_inc(s_o, 1)


A_Q, A_F, A_I, A_G = 0, 1024, 2048, 3072
B_Q, B_K, B_V, B_GK, B_G = 4096, 4608, 5120, 6144, 6160
C_QKV, C_A, C_G, MERGE, N_IN = 7184, 10256, 10272, 11296, 14368
RANK = 16
T_AQ, T_AF, T_BQ, T_BK, T_C = 0, 1024, 2048, 2560, 3072
N_AI, N_AG, N_BV, N_BG, N_CG, N_M = 0, 1024, 2048, 3072, 4096, 5120


def load_norm_gain(C, tag, gain):
    nc = C.nc
    with ExitStack() as st:
        s_in = nc.alloc_semaphore(f"{tag}_in")
        block = st.enter_context(nc.Block())

        @block.sync
        def _(sp):
            with nc.allow_non_contiguous_dma("4 KB of channel gains"):
                sp.dma_start(C.scale[:, 0, :], gain.rearrange("(k p) -> p k", p=P)).then_inc(s_in, 16)
            sp.wait_ge(s_in, 16)

        @block.gpsimd
        def _(pool):
            pool.memset(C.shift[:], 0.0)


def small_projections(C):
    nc, ins = C.nc, C.ins
    BH = B_HEADS
    with ExitStack() as st:
        sb = lambda n, s: st.enter_context(nc.sbuf_tensor(f"s_{n}", s, F32))
        sem = lambda n: nc.alloc_semaphore(f"s_{n}")
        wl = sb("wl", [P, KD, RANK])
        wc = sb("wc", [P, KD, 2 * C_HEADS])
        wg = sb("wg", [RANK, BH * P])
        bg = sb("bg", [P, BH])
        low = sb("low", [RANK, SEQ])
        pl = st.enter_context(nc.psum_tensor("s_pl", [P, 2, CH], F32))
        pc = st.enter_context(nc.psum_tensor("s_pc", [P, NT, 2 * C_HEADS], F32))
        pg = st.enter_context(nc.psum_tensor("s_pg", [P, 2, CH], F32))
        s_in = sem("loaded")
        s_l = sem("low_done")
        s_lc = sem("low_ready")
        s_c = sem("ab_done")
        s_g = sem("logits_done")
        s_gc = sem("logits_taken")
        block = st.enter_context(nc.Block())
        w = ins["w_in_2"][0].rearrange("(k p) n -> p k n", p=P)

        @block.sync
        def _(sp):
            with nc.allow_non_contiguous_dma("64-byte rows, 128 KB in all"):
                sp.dma_start(wl[:], w[:, :, B_GK:B_GK + RANK]).then_inc(s_in, 16)
                sp.dma_start(wc[:], w[:, :, C_A:C_A + 2 * C_HEADS]).then_inc(s_in, 16)
                sp.dma_start(bg[:], ins["gla_b_gk_2"][0].rearrange("(h p) -> p h", p=P)).then_inc(s_in, 16)
            sp.dma_start(wg[:], ins["gla_w_gk_2"][0]).then_inc(s_in, 16)

        @block.tensor
        def _(pe):
            pe.wait_ge(s_in, 64)
            for h in range(2):
                for k in range(KD):
                    mm = pe.matmul(pl[0:RANK, h, :], wl[:, k, :], C.hT[:, k, h * CH:(h + 1) * CH],
                                   start=(k == 0), stop=(k == KD - 1))
            mm.then_inc(s_l, 1)
            for t in range(NT):
                for k in range(KD):
                    mm = pe.matmul(pc[:, t, :], C.hT[:, k, t * P:(t + 1) * P], wc[:, k, :],
                                   start=(k == 0), stop=(k == KD - 1))
            mm.then_inc(s_c, 1)
            pe.wait_ge(s_lc, 1)
            for c in range(BH):
                for h in range(2):
                    if c > 0:
                        pe.wait_ge(s_gc, 2 * (c - 1) + h + 1)
                    pe.matmul(pg[:, h, :], wg[:, c * P:(c + 1) * P], low[:, h * CH:(h + 1) * CH],
                              start=True, stop=True).then_inc(s_g, 1)

        @block.vector
        def _(dve):
            dve.wait_ge(s_l, 1)
            dve.tensor_copy(low[:], pl[0:RANK].rearrange("p a b -> p (a b)")).then_inc(s_lc, 1)
            dve.wait_ge(s_c, 1)
            dve.tensor_copy(C.ab[:], pc[:])
            for c in range(BH):
                for h in range(2):
                    dve.wait_ge(s_g, 2 * c + h + 1)
                    dve.tensor_scalar(C.gk[:, c, h * CH:(h + 1) * CH], pg[:, h, :], bg[:, c:c + 1], None,
                                      ALU.add).then_inc(s_gc, 1)


def gated_linear(C, branch):
    nc, ins = C.nc, C.ins
    A = branch == "a"
    H, dv = (A_HEADS, D // A_HEADS) if A else (B_HEADS, D // B_HEADS)
    GS = 1.0 if A else 1.0 / 16.0
    L2 = LEVELS + 2
    tag = f"g{branch}"
    with ExitStack() as st:
        sb = lambda n, s: st.enter_context(nc.sbuf_tensor(f"{tag}_{n}", s, F32))
        sem = lambda n: nc.alloc_semaphore(f"{tag}_{n}")
        z = sb("z", [P, 2, SEQ])
        q = sb("q", [P, 2, SEQ])
        k = sb("k", [P, 2, SEQ])
        v = sb("v", [P, 2, NCK, dv])
        lt = sb("lt", [P, 2, SEQ])
        bb = sb("bb", [P, 2, SEQ])
        X = sb("X", [P, 2, L2, SEQ])
        el = sb("el", [P, 2, NCK])
        masks = sb("masks", [P, LEVELS + 1, CK])
        restart = sb("restart", [P, SEQ])
        am = sb("am", [P, 2, LEVELS + 1, CK])
        AT = sb("AT", [P, 2, CK])
        kd = sb("kd", [P, 2, CK])
        S = sb("S", [P, 2, dv])
        o = sb("o", [P, 2, dv])
        pa = st.enter_context(nc.psum_tensor(f"{tag}_pa", [P, 2, LEVELS + 1, CK], F32))
        pk = st.enter_context(nc.psum_tensor(f"{tag}_pk", [P, CH], F32))
        po = st.enter_context(nc.psum_tensor(f"{tag}_po", [P, 2, CH], F32))
        pS = st.enter_context(nc.psum_tensor(f"{tag}_pS", [P, CH], F32))
        s_tab = sem("tables_loaded")
        s_in = [sem(f"head_loaded{b}") for b in range(2)]
        s_ln = sem("log_term_ready")
        s_kz = sem("k_logits_ready")
        s_b = sem("b_ready")
        s_qk = sem("q_and_k_ready")
        s_sub = sem("exponents_ready")
        s_exp = sem("exps_ready")
        s_X = sem("X_ready")
        s_A = sem("level_products_done")
        s_At = sem("A_ready")
        s_kT = sem("k_transposed")
        s_kc = sem("k_taken")
        s_o = sem("o_done")
        s_oc = sem("o_taken")
        s_S = sem("state_product_done")
        s_Sc = sem("state_ready")
        s_st = [sem(f"o_stored{b}") for b in range(2)]
        block = st.enter_context(nc.Block())
        q0 = T_AQ if A else T_BQ
        v0 = N_AI if A else N_BV
        o_dram = C.o_dram[0 if A else 1]

        def heads(eng, prepare, chunk, steps):
            for s in range(steps):
                prepare(0, 0, s, 1)

            def one(n, b, more, use):
                for c in range(NCK):
                    chunk(n, b, c, c < NCK - 1)
                    if more:
                        for s in range(c * steps // NCK, (c + 1) * steps // NCK):
                            prepare(n + 1, 1 - b, s, use)

            with eng.Fori(0, H // 2 - 1) as i:
                one(2 * i, 0, True, i + 1)
                one(2 * i + 1, 1, True, i + 2)
            one(H - 2, 0, True, H // 2)
            one(H - 1, 1, False, None)

        @block.sync
        def _(sp):
            sp.dma_start(masks[:], ins["t_levels"]).then_inc(s_tab, 16)
            sp.dma_start(restart[:], ins["t_restart"]).then_inc(s_tab, 16)

            def load(n, b):
                sp.dma_start(q[:, b, :], C.pt_dram[ds(q0 + n * P, P), :]).then_inc(s_in[b], 16)
                if A:
                    sp.dma_start(z[:, b, :], C.pt_dram[ds(T_AF + n * P, P), :]).then_inc(s_in[b], 16)
                else:
                    sp.dma_start(k[:, b, :], C.pt_dram[ds(T_BK + n * P, P), :]).then_inc(s_in[b], 16)
                sp.dma_start(v[:, b], C.pn_dram[:, ds(v0 + n * dv, dv)].rearrange("(c p) n -> p c n", p=P)).then_inc(s_in[b], 16)

            def store(n, c):
                sp.wait_ge(s_oc, NCK * n + c + 3)
                sp.dma_start(o_dram[c * P:(c + 1) * P, ds(n * dv, dv)], o[:, c % 2, :]).then_inc(s_st[c % 2], 16)

            for b in range(2):
                load(b, b)
            for b in range(2):
                sp.sem_inc(s_st[b], 16)

            def one(n, b, more):
                for c in range(NCK):
                    store(n, c)
                if more:
                    load(n + 2, b)
            with sp.Fori(0, H // 2 - 1) as i:
                for b in range(2):
                    one(2 * i + b, b, True)
            one(H - 2, 0, False)
            one(H - 1, 1, False)
            for b in range(2):
                sp.wait_ge(s_st[b], 16 * (H * NCK // 2 + 1))

        @block.scalar
        def _(act):
            act.sem_inc(s_kc, 1)
            act.sem_inc(s_oc, 2)

            def exps(n, b, lev, order):
                act.wait_ge(s_sub, (L2 - 1) * n + order)
                act.activation(X[:, b, lev], X[:, b, lev], ACT.Exp, scale=GS).then_inc(s_exp, 1)

            def prepare(n, b, s, use):
                if s == 0:
                    act.wait_ge(s_in[b], 48 * use)
                    act.activation(lt[:, b], z[:, b] if A else C.gk[:, ds(n, 1), :].rearrange("p h t -> p (h t)"), ACT.Abs)
                    act.drain()
                    act.activation(lt[:, b], lt[:, b], ACT.Exp, scale=-1.0)
                    act.drain()
                    act.activation(lt[:, b], lt[:, b], ACT.Ln, bias=1.0).then_inc(s_ln, 1)
                elif s == 1:
                    if A:
                        act.wait_ge(s_kz, n + 1)
                        act.activation(k[:, b], k[:, b], ACT.Exp)
                        act.activation(q[:, b], q[:, b], ACT.Silu).then_inc(s_qk, 1)
                    else:
                        act.mul(q[:, b], q[:, b], float(P) ** -0.5).then_inc(s_qk, 1)
                elif s == 2:
                    act.wait_ge(s_b, n + 1)
                    act.activation(el[:, b], bb[:, b].rearrange("p (c t) -> p c t", c=NCK)[:, :, CK - 1], ACT.Exp, scale=GS)
                    act.activation(X[:, b, LEVELS], bb[:, b], ACT.Exp, scale=GS).then_inc(s_exp, 1)
                elif s == 3:
                    exps(n, b, LEVELS + 1, 1)
                else:
                    exps(n, b, s - 4, s - 2)

            def chunk(n, b, c, more):
                m = NCK * n + c
                act.wait_ge(s_kT, m + 1)
                act.copy(kd[:, c % 2], pk[:, 0:CK]).then_inc(s_kc, 1)
                act.wait_ge(s_o, m + 3)
                act.wait_ge(s_st[c % 2], 16 * ((NCK // 2) * n + c // 2 + 1))
                act.copy(o[:, c % 2], po[:, c % 2, 0:dv]).then_inc(s_oc, 1)
            heads(act, prepare, chunk, 4 + LEVELS)

        @block.vector
        def _(dve):
            dve.sem_inc(s_At, 2)
            dve.sem_inc(s_Sc, 1)
            dve.wait_ge(s_tab, 32)

            def blocks(ap, lev):
                s = 1 << lev
                return ap.rearrange("p (n a s) -> p n a s", a=2, s=s)

            def prepare(n, b, s, use):
                zs = z[:, b] if A else C.gk[:, ds(n, 1), :].rearrange("p h t -> p (h t)")
                if s == 0:
                    dve.wait_ge(s_ln, n + 1)
                    dve.scalar_tensor_tensor(lt[:, b], zs, 0.0, lt[:, b], ALU.min, ALU.subtract)
                    dve.drain()
                    if A:
                        dve.tensor_tensor(k[:, b], lt[:, b], z[:, b], ALU.subtract).then_inc(s_kz, 1)
                    dve.tensor_tensor_scan(bb[:, b], restart[:], lt[:, b], 0.0, ALU.mult, ALU.add).then_inc(s_b, 1)
                    dve.drain()
                elif s == 1:
                    t = bb[:, b].rearrange("p (c t) -> p c t", c=NCK)
                    dve.tensor_tensor(X[:, b, LEVELS + 1].rearrange("p (c t) -> p c t", c=NCK),
                                      t[:, :, CK - 1:CK].to_broadcast([P, NCK, CK]), t, ALU.subtract).then_inc(s_sub, 1)
                else:
                    lev = s - 2
                    src, dst, h = blocks(bb[:, b], lev), blocks(X[:, b, lev], lev), 1 << lev
                    nb = SEQ // (2 * h)
                    mid = src[:, :, 0, h - 1:h].to_broadcast([P, nb, h])
                    dve.tensor_tensor(dst[:, :, 0, :], mid, src[:, :, 0, :], ALU.subtract)
                    dve.tensor_tensor(dst[:, :, 1, :], src[:, :, 1, :], mid, ALU.subtract).then_inc(s_sub, 1)

            def chunk(n, b, c, more):
                m = NCK * n + c
                dve.wait_ge(s_A, m + 1)
                dve.tensor_tensor(am[:, c % 2], pa[:, c % 2], masks[:], ALU.mult)
                dve.drain()
                dve.wait_ge(s_o, m + 1)
                dve.tensor_reduce(AT[:, c % 2], am[:, c % 2].rearrange("p l i -> p i l"), AX.X, ALU.add).then_inc(s_At, 1)
                dve.wait_ge(s_S, m + 1)
                nxt = S[:, (c + 1) % 2]
                if c == 0:
                    dve.tensor_copy(nxt, pS[:, 0:dv]).then_inc(s_Sc, 1)
                else:
                    dve.scalar_tensor_tensor(nxt, S[:, c % 2], el[:, b, c:c + 1], pS[:, 0:dv], ALU.mult, ALU.add).then_inc(s_Sc, 1)
            heads(dve, prepare, chunk, 2 + LEVELS)

        @block.gpsimd
        def _(pool):
            def prepare(n, b, s, use):
                e = L2 * n
                if s == 0:
                    pool.wait_ge(s_qk, n + 1)
                    pool.wait_ge(s_exp, e + 1)
                    pool.tensor_tensor(X[:, b, LEVELS], X[:, b, LEVELS], q[:, b], ALU.mult).then_inc(s_X, 1)
                elif s == 1:
                    pool.wait_ge(s_exp, e + 2)
                    pool.tensor_tensor(X[:, b, LEVELS + 1], X[:, b, LEVELS + 1], k[:, b], ALU.mult).then_inc(s_X, 1)
                else:
                    lev, h = s - 2, 1 << (s - 2)
                    pool.wait_ge(s_exp, e + s + 1)
                    f = lambda ap: ap.rearrange("p (n a s) -> p n a s", a=2, s=h)
                    x = f(X[:, b, lev])
                    pool.tensor_tensor(x[:, :, 0, :], x[:, :, 0, :], f(k[:, b])[:, :, 0, :], ALU.mult)
                    pool.tensor_tensor(x[:, :, 1, :], x[:, :, 1, :], f(q[:, b])[:, :, 1, :], ALU.mult).then_inc(s_X, 1)
            heads(pool, prepare, lambda *a: None, L2)

        @block.tensor
        def _(pe):
            pe.sem_inc(s_o, 2)

            def levels(n, b, c):
                m = NCK * n + c
                sl = slice(c * CK, (c + 1) * CK)
                pe.wait_ge(s_At, m + 1)
                for lev in range(LEVELS):
                    pe.matmul(pa[:, c % 2, lev, :], X[:, b, lev, sl], X[:, b, lev, sl], start=True, stop=True)
                pe.matmul(pa[:, c % 2, LEVELS, :], k[:, b, sl], q[:, b, sl], start=True, stop=True).then_inc(s_A, 1)

            def chunk(n, b, c, more):
                m = NCK * n + c
                sl = slice(c * CK, (c + 1) * CK)
                if c == 0:
                    pe.wait_ge(s_X, L2 * n + L2)
                    levels(n, b, 0)
                if more:
                    levels(n, b, c + 1)
                pe.wait_ge(s_kc, m + 1)
                pe.transpose(pk[:, 0:CK], X[:, b, LEVELS + 1, sl], C.ident[:]).then_inc(s_kT, 1)
                pe.wait_ge(s_kc, m + 2)
                pe.wait_ge(s_Sc, m + 1)
                pe.matmul(pS[:, 0:dv], kd[:, c % 2], v[:, b, c, :], start=True, stop=True).then_inc(s_S, 1)
                pe.wait_ge(s_oc, m + 1)
                pe.wait_ge(s_At, m + 3)
                if c > 0:
                    pe.matmul(po[:, c % 2, 0:dv], X[:, b, LEVELS, sl], S[:, c % 2], start=True, stop=False)
                pe.matmul(po[:, c % 2, 0:dv], AT[:, c % 2], v[:, b, c, :], start=(c == 0), stop=True).then_inc(s_o, 1)
            heads(pe, lambda *a: None, chunk, 0)


def merge_out(C):
    nc, ins = C.nc, C.ins
    br = [(A_HEADS, N_AG, "hgrn_onorm_2"), (B_HEADS, N_BG, "gla_onorm_2"), (C_HEADS, N_CG, "gdn_onorm_2")]
    with ExitStack() as st:
        sb = lambda n, s: st.enter_context(nc.sbuf_tensor(f"y_{n}", s, F32))
        sem = lambda n: nc.alloc_semaphore(f"y_{n}")
        w = sb("w", [P, KD, D])
        post = sb("post", [P, D])
        on = [sb(f"on{j}", [P, D // h]) for j, (h, _, _) in enumerate(br)]
        o = sb("o", [P, 2, D])
        g = sb("g", [P, 2, D])
        mg = sb("mg", [P, 2, D])
        sq = sb("sq", [P, 2, D])
        ms = sb("ms", [P, 2, 8])
        rs = sb("rs", [P, 2, 8])
        t2 = sb("t2", [P, D])
        junk = sb("junk", [P, D])
        y = sb("y", [P, D])
        yT = sb("yT", [P, KD, P])
        mo = sb("mo", [P, D])
        ms2 = sb("ms2", [P, 2])
        pt = st.enter_context(nc.psum_tensor("y_pt", [P, KD, P], F32))
        po = st.enter_context(nc.psum_tensor("y_po", [P, 2, CH], F32))
        s_tab = sem("tables_loaded")
        s_in = [sem(f"branch_loaded{b}") for b in range(2)]
        s_sg = sem("gates_ready")
        s_ms = sem("head_sums")
        s_rs = sem("head_rs")
        s_b = sem("branch_added")
        s_T = sem("y_transposed")
        s_Tc = sem("yT_taken")
        s_o = sem("product_done")
        s_y = sem("y_ready")
        s_pm = sem("gates_multiplied")
        s_gg = sem("gates_and_gain_ready")
        s_ss = sem("row_rs")
        s_x = sem("x_updated")
        block = st.enter_context(nc.Block())
        NJ = 3

        def steps(eng, step, tile):
            with eng.Fori(0, NT // 2) as i:
                for a in range(2):
                    for j in range(NJ):
                        u = NJ * a + j
                        step(2 * NJ * i + u, u % 2, 2 * i + a, j, NJ * i + u // 2 + 1)
                    tile(2 * i + a)

        @block.sync
        def _(sp):
            sp.dma_start(w[:], ins["w_out_2"][0].rearrange("(k p) n -> p k n", p=P)).then_inc(s_tab, 16)
            sp.dma_start(post[:], ins["ln_mix_post_2"][0].partition_broadcast(P)).then_inc(s_tab, 16)
            for j, (h, _, name) in enumerate(br):
                sp.dma_start(on[j][:], ins[name][0].partition_broadcast(P)).then_inc(s_tab, 16)

            def step(n, b, t, j, use):
                sp.wait_ge(s_b, n + 1)
                rows = ds(t * P, P)
                sp.dma_start(o[:, b], C.o_dram[j][rows, :]).then_inc(s_in[b], 16)
                sp.dma_start(g[:, b], C.pn_dram[rows, br[j][1]:br[j][1] + D]).then_inc(s_in[b], 16)
                sp.dma_start(mg[:, b], C.pn_dram[rows, N_M + j * D:N_M + (j + 1) * D]).then_inc(s_in[b], 16)
            steps(sp, step, lambda t: None)

        @block.scalar
        def _(act):
            def step(n, b, t, j, use):
                H = br[j][0]
                act.wait_ge(s_in[b], 48 * use)
                act.activation(g[:, b], g[:, b], ACT.Silu)
                act.activation(mg[:, b], mg[:, b], ACT.Sigmoid).then_inc(s_sg, 1)
                act.wait_ge(s_ms, n + 1)
                act.activation(rs[:, b, 0:H], ms[:, b, 0:H], ACT.Ln, bias=C.eps[:], scale=1.0 * H / D)
                act.drain()
                act.activation(rs[:, b, 0:H], rs[:, b, 0:H], ACT.Exp, scale=-0.5).then_inc(s_rs, 1)

            def tile(t):
                act.wait_ge(s_T, t + 2)
                act.copy(yT[:], pt[:]).then_inc(s_Tc, 1)
                act.wait_ge(s_o, t + 1)
                act.activation(junk[:], po[:].rearrange("p a b -> p (a b)"), ACT.Square, accum_out=ms2[:, 0:1])
                act.drain()
                act.activation(ms2[:, 1:2], ms2[:, 0:1], ACT.Ln, bias=C.eps[:], scale=1.0 / D)
                act.drain()
                act.activation(ms2[:, 1:2], ms2[:, 1:2], ACT.Exp, scale=-0.5).then_inc(s_ss, 1)
            steps(act, step, tile)

        @block.gpsimd
        def _(pool):
            def step(n, b, t, j, use):
                H = br[j][0]
                pool.wait_ge(s_sg, n + 1)
                pool.tensor_tensor(mg[:, b], mg[:, b], g[:, b], ALU.mult).then_inc(s_pm, 1)
                pool.wait_ge(s_pm, n + 1)
                m = mg[:, b].rearrange("p (h n) -> p h n", h=H)
                pool.tensor_tensor(m, m, on[j][:].unsqueeze(1).to_broadcast([P, H, D // H]), ALU.mult).then_inc(s_gg, 1)
            pool.wait_ge(s_tab, 16 * 5)
            steps(pool, step, lambda t: None)

        @block.vector
        def _(dve):
            dve.sem_inc(s_b, 2)
            dve.wait_ge(s_tab, 16 * 5)

            def step(n, b, t, j, use):
                H = br[j][0]
                dve.wait_ge(s_in[b], 48 * use)
                dve.tensor_tensor(sq[:, b], o[:, b], o[:, b], ALU.mult)
                dve.drain()
                dve.tensor_reduce(ms[:, b, 0:H], sq[:, b].rearrange("p (h n) -> p h n", h=H), AX.X, ALU.add).then_inc(s_ms, 1)
                dve.wait_ge(s_gg, n + 1)
                dve.wait_ge(s_rs, n + 1)
                if j == 0:
                    dve.wait_ge(s_T, t + 1)
                dst, w_ = (y if j == 0 else t2), D // H
                for h in range(H):
                    e = dve.scalar_tensor_tensor(dst[:, h * w_:(h + 1) * w_], o[:, b, h * w_:(h + 1) * w_], rs[:, b, h:h + 1],
                                                 mg[:, b, h * w_:(h + 1) * w_], ALU.mult, ALU.mult)
                e.then_inc(s_b, 1)
                dve.drain()
                if j > 0:
                    e = dve.tensor_tensor(y[:], y[:], t2[:], ALU.add)
                    if j == NJ - 1:
                        e.then_inc(s_y, 1)
                    dve.drain()

            def tile(t):
                dve.wait_ge(s_ss, t + 1)
                dve.scalar_tensor_tensor(mo[:], po[:].rearrange("p a b -> p (a b)"), ms2[:, 1:2], post[:], ALU.mult, ALU.mult)
                dve.drain()
                x = C.x_sb[:, ds(t, 1), :].rearrange("p t n -> p (t n)")
                dve.tensor_tensor(x, x, mo[:], ALU.add).then_inc(s_x, 1)
            steps(dve, step, tile)

        @block.tensor
        def _(pe):
            pe.sem_inc(s_T, 1)
            pe.wait_ge(s_tab, 16 * 5)

            def tile(t):
                pe.wait_ge(s_y, t + 1)
                for k in range(KD):
                    mm = pe.transpose(pt[:, k, :], y[:, k * P:(k + 1) * P], C.ident[:])
                mm.then_inc(s_T, 1)
                pe.wait_ge(s_Tc, t + 1)
                for h in range(2):
                    for k in range(KD):
                        mm = pe.matmul(po[:, h, :], yT[:, k, :], w[:, k, h * CH:(h + 1) * CH], start=(k == 0), stop=(k == KD - 1))
                mm.then_inc(s_o, 1)
            steps(pe, lambda *a: None, tile)


def gated_delta(C):
    nc, ins = C.nc, C.ins
    H = C_HEADS
    with ExitStack() as st:
        sb = lambda n, s: st.enter_context(nc.sbuf_tensor(f"d_{n}", s, F32))
        sem = lambda n: nc.alloc_semaphore(f"d_{n}")
        PAD = 3
        causal = sb("causal", [P, CK])
        masks = sb("masks", [P, LEVELS + 1, CK])
        al = sb("al", [P, 2, H])
        ea = sb("ea", [P, H])
        cr = sb("cr", [4 * 24, P])
        cw = sb("cw", [P, 4, 3, H])
        gu = sb("gu", [P, NCK, H])
        gl = sb("gl", [P, NCK, H])
        gg = sb("gg", [P, H, NCK])
        sc = sb("sc", [P, 6, H, NCK])
        hs = sb("hs", [P, 6, NCK])
        cwh = sb("cwh", [P, 3, 4])
        raw = sb("raw", [P, 3, PAD + SEQ])
        cv = sb("cv", [P, 3, SEQ])
        dg = sb("dg", [P, 2, NCK, CK])
        qk = sb("qk", [P, 2, NCK, CK])
        sq = sb("sq", [P, 2, NCK, CK])
        ss = sb("ss", [P, 2, NCK])
        rs = sb("rs", [P, 2, NCK])
        qkT = sb("qkT", [P, 2, NCK, CK])
        vb = sb("vb", [P, NCK, CK])
        kb = sb("kb", [P, NCK, CK])
        kd = sb("kd", [P, NCK, CK])
        DT = sb("DT", [P, NCK, CK])
        MT = sb("MT", [P, NCK, CK])
        Ml = sb("Ml", [P, 2, NCK, CK])
        QKT = sb("QKT", [P, NCK, CK])
        er = sb("er", [P, NCK, CK])
        XY = sb("XY", [P, 2, NCK, CK])
        Pm = sb("Pm", [P, NCK, CK])
        wT = sb("wT", [P, NCK, CK])
        vn = sb("vn", [P, 2, CK])
        S = sb("S", [P, 2, CK])
        o = sb("o", [P, 2, CK])
        ps = st.enter_context(nc.psum_tensor("d_ps", [P, 8, CH], F32))
        names = ("tables", "raw", "conv_rows", "conv_cols", "conv_cols_taken", "u", "abs", "gates", "cumulated",
                 "exps", "scalars", "per_head", "first_tap", "conv", "silu", "diagonals", "tokens", "b_rows", "qk_tokens",
                 "v_beta", "sums", "rs", "qk_normed", "qkT", "qT_taken", "kT_taken", "beta_rows", "exponents", "decay",
                 "eb_rows", "kk", "MT", "QKT", "level_M", "P", "P_taken", "XY", "XY_ready", "w", "w_taken", "v_new",
                 "v_new_taken", "o", "o_taken", "S", "S_ready", "qdec", "pad", "kparts")
        s = {n: sem(n) for n in names}
        s_st = [sem(f"o_stored{b}") for b in range(2)]
        block = st.enter_context(nc.Block())
        flat = lambda ap: ap.rearrange("p c t -> p (c t)")
        bank2 = lambda b: ps[:, b:b + 2, :].rearrange("p b (c t) -> p (b c) t", t=CK)
        over_t = lambda col: col.unsqueeze(2).to_broadcast([P, NCK, CK])
        over_c = lambda mat: mat.unsqueeze(1).to_broadcast([P, NCK, CK])

        @block.sync
        def _(sp):
            sp.dma_start(causal[:], ins["t_causal"]).then_inc(s["tables"], 16)
            sp.dma_start(masks[:], ins["t_levels"]).then_inc(s["tables"], 16)
            sp.dma_start(al[:, 0], ins["gdn_a_log_2"][0].partition_broadcast(P)).then_inc(s["tables"], 16)
            sp.dma_start(al[:, 1], ins["gdn_dt_bias_2"][0].partition_broadcast(P)).then_inc(s["tables"], 16)
            sp.dma_start(cr[:], ins["gdn_conv_2"][0].rearrange("j (s p) -> (j s) p", p=P)).then_inc(s["tables"], 16)
            for b in range(2):
                sp.sem_inc(s_st[b], 16)

            def load(h):
                for q in range(3):
                    sp.dma_start(raw[:, q, PAD:PAD + SEQ], C.pt_dram[ds(T_C + q * D + h * P, P), :]).then_inc(s["raw"], 16)

            def stores(h):
                for c in range(NCK):
                    sp.wait_ge(s["o_taken"], NCK * h + c + 3)
                    sp.dma_start(C.o_dram[2][c * CK:(c + 1) * CK, ds(h * CK, CK)], o[:, c % 2]).then_inc(s_st[c % 2], 16)
            load(0)
            with sp.Fori(0, H - 1) as h:
                sp.wait_ge(s["conv"], h + 1)
                load(h + 1)
                stores(h)
            stores(H - 1)
            for b in range(2):
                sp.wait_ge(s_st[b], 16 * (H * NCK // 2 + 1))

        @block.scalar
        def _(act):
            act.sem_inc(s["o_taken"], 2)
            act.wait_ge(s["tables"], 80)
            act.wait_ge(s["u"], 1)
            act.activation(sc[:, 3].rearrange("p h c -> p c h"), C.ab[:, :, H:2 * H], ACT.Sigmoid)
            act.activation(ea[:], al[:, 0], ACT.Exp)
            act.activation(gl[:], gu[:], ACT.Abs)
            act.drain()
            act.activation(gl[:], gl[:], ACT.Exp, scale=-1.0)
            act.drain()
            act.activation(gl[:], gl[:], ACT.Ln, bias=1.0).then_inc(s["abs"], 1)
            act.wait_ge(s["exps"], 1)
            act.activation(sc[:, 1], sc[:, 1], ACT.Exp)
            act.activation(sc[:, 2], sc[:, 2], ACT.Exp)
            act.activation(sc[:, 4], sc[:, 0], ACT.Exp).then_inc(s["scalars"], 1)
            with act.Fori(0, H) as h:
                act.wait_ge(s["per_head"], h + 1)
                act.wait_ge(s["raw"], 48 * h + 48)
                act.wait_ge(s["tokens"], h + 1)
                for q in range(3):
                    e = act.activation(cv[:, q], raw[:, q, 0:SEQ], ACT.Identity, scale=cwh[:, q, 0:1])
                e.then_inc(s["first_tap"], 1)
                act.wait_ge(s["conv"], h + 1)
                act.activation(cv[:], cv[:], ACT.Silu).then_inc(s["silu"], 1)
                act.wait_ge(s["tokens"], h + 2)
                act.copy(qk[:, 0], bank2(0))
                act.copy(qk[:, 1], bank2(2))
                act.drain()
                act.activation(sq[:], qk[:], ACT.Square).then_inc(s["qk_tokens"], 1)
                act.wait_ge(s["sums"], h + 1)
                act.activation(rs[:], ss[:], ACT.Ln, bias=C.eps[:])
                act.drain()
                act.activation(rs[:], rs[:], ACT.Exp, scale=-0.5).then_inc(s["rs"], 1)
                act.wait_ge(s["b_rows"], h + 1)
                act.wait_ge(s["exponents"], h + 1)
                act.activation(er[:], bank2(6), ACT.Exp).then_inc(s["eb_rows"], 1)
                act.activation(DT[:], DT[:], ACT.Exp).then_inc(s["decay"], 1)
                act.wait_ge(s["qkT"], h + 1)
                act.copy(qkT[:, 0], bank2(0)).then_inc(s["qT_taken"], 1)
                for lev in range(1, LEVELS):
                    for hf in range(2):
                        n = 2 * (LEVELS - 1) * h + 2 * (lev - 1) + hf
                        act.wait_ge(s["P"], n + 1)
                        act.copy(Pm[:, 4 * hf:4 * hf + 4], ps[:, 4 + hf].rearrange("p (c t) -> p c t", t=CK)).then_inc(s["P_taken"], 1)
                act.wait_ge(s["w"], h + 1)
                act.activation(wT[:], bank2(6), ACT.Copy, scale=-1.0).then_inc(s["w_taken"], 1)
                for c in range(NCK):
                    m = NCK * h + c
                    act.wait_ge(s["v_new"], m + 1)
                    act.copy(vn[:, c % 2], ps[:, 4 + c % 2, 0:CK]).then_inc(s["v_new_taken"], 1)
                    act.wait_ge(s["o"], m + 1)
                    act.wait_ge(s_st[c % 2], 16 * ((NCK // 2) * h + c // 2 + 1))
                    act.copy(o[:, c % 2], ps[:, c % 2, 0:CK]).then_inc(s["o_taken"], 1)

        @block.gpsimd
        def _(pool):
            pool.memset(raw[:, :, 0:PAD], 0.0).then_inc(s["pad"], 1)
            pool.wait_ge(s["tables"], 80)
            with pool.Fori(0, H) as h:
                pool.wait_ge(s["MT"], h + 1)
                for lev in range(LEVELS):
                    if lev >= 3:
                        pool.wait_ge(s["P"], 2 * (LEVELS - 1) * h + 2 * (lev - 2))
                    elif lev == 2:
                        pool.wait_ge(s["XY_ready"], (2 * (LEVELS - 1) + 1) * h + 1)
                    pool.tensor_tensor(Ml[:, lev % 2], MT[:], over_c(masks[:, lev]), ALU.mult).then_inc(s["level_M"], 1)

        @block.vector
        def _(dve):
            dve.sem_inc(s["S_ready"], 1)
            dve.wait_ge(s["tables"], 80)
            dve.wait_ge(s["pad"], 1)
            dve.tensor_tensor(gu[:], C.ab[:, :, 0:H], al[:, 1].unsqueeze(1).to_broadcast([P, NCK, H]), ALU.add).then_inc(s["u"], 1)
            dve.wait_ge(s["abs"], 1)
            dve.scalar_tensor_tensor(gl[:], gu[:], 0.0, gl[:], ALU.max, ALU.add)
            dve.drain()
            dve.tensor_scalar(gl[:], gl[:], -1.0, None, ALU.mult)
            dve.drain()
            dve.tensor_tensor(gg[:], gl[:].rearrange("p c h -> p h c"), ea[:].unsqueeze(2).to_broadcast([P, H, NCK]), ALU.mult).then_inc(s["gates"], 1)
            dve.wait_ge(s["cumulated"], 1)
            f = lambda ap: ap.rearrange("p h c -> p (h c)")
            dve.tensor_copy(f(sc[:, 0]), ps[:, 0, 0:H * NCK])
            dve.tensor_copy(f(sc[:, 1]), ps[:, 1, 0:H * NCK])
            dve.tensor_copy(cw[:].rearrange("p j s h -> p (j s h)"), ps[:, 2, 0:96]).then_inc(s["conv_cols_taken"], 1)
            dve.drain()
            dve.tensor_tensor(sc[:, 2], sc[:, 1], sc[:, 0], ALU.subtract).then_inc(s["exps"], 1)
            dve.wait_ge(s["scalars"], 1)
            dve.tensor_tensor(sc[:, 4], sc[:, 4], sc[:, 3], ALU.mult)
            dve.drain()
            with dve.Fori(0, H) as h:
                dve.drain()
                dve.tensor_copy(hs[:, 0:5], sc[:, 0:5, ds(h, 1), :].rearrange("p k h c -> p k (h c)"))
                dve.tensor_copy(cwh[:].rearrange("p s j -> p j s"), cw[:, :, :, ds(h, 1)].rearrange("p j s h -> p j (s h)")).then_inc(s["per_head"], 1)
                dve.drain()
                for q in range(2):
                    e = dve.tensor_tensor(dg[:, q], over_c(C.ident[:]), over_t(hs[:, 3 * q]), ALU.mult)
                e.then_inc(s["diagonals"], 1)
                dve.wait_ge(s["raw"], 48 * h + 48)
                dve.wait_ge(s["first_tap"], h + 1)
                for j in range(1, 4):
                    for q in range(3):
                        e = dve.scalar_tensor_tensor(cv[:, q], raw[:, q, j:j + SEQ], cwh[:, q, j:j + 1], cv[:, q], ALU.mult, ALU.add)
                    if j < 3:
                        dve.drain()
                e.then_inc(s["conv"], 1)
                dve.wait_ge(s["b_rows"], h + 1)
                dve.tensor_tensor(DT[:], bank2(6), over_t(hs[:, 0]), ALU.subtract)
                dve.drain()
                dve.tensor_scalar(DT[:], DT[:], 0.0, None, ALU.min).then_inc(s["exponents"], 1)
                dve.wait_ge(s["tokens"], h + 2)
                dve.tensor_tensor(vb[:], bank2(4), over_t(hs[:, 3]), ALU.mult).then_inc(s["v_beta"], 1)
                dve.wait_ge(s["qk_tokens"], h + 1)
                dve.tensor_reduce(ss[:], sq[:], AX.X, ALU.add).then_inc(s["sums"], 1)
                dve.wait_ge(s["rs"], h + 1)
                dve.tensor_scalar(rs[:, 0], rs[:, 0], float(P) ** -0.5, None, ALU.mult)
                dve.drain()
                for q in range(2):
                    e = dve.tensor_tensor(qk[:, q], qk[:, q], over_t(rs[:, q]), ALU.mult)
                e.then_inc(s["qk_normed"], 1)
                dve.drain()
                dve.tensor_tensor(kb[:], qk[:, 1], over_t(hs[:, 4]), ALU.mult)
                dve.tensor_tensor(kd[:], qk[:, 1], over_t(hs[:, 2]), ALU.mult).then_inc(s["kparts"], 1)
                dve.wait_ge(s["qkT"], h + 1)
                dve.tensor_copy(qkT[:, 1], bank2(2)).then_inc(s["kT_taken"], 1)
                dve.wait_ge(s["decay"], h + 1)
                dve.tensor_tensor(DT[:], DT[:], over_c(causal[:]), ALU.mult)
                dve.drain()
                dve.wait_ge(s["kk"], h + 1)
                dve.tensor_tensor(MT[:], bank2(0), DT[:], ALU.mult)
                dve.drain()
                dve.wait_ge(s["beta_rows"], h + 1)
                dve.tensor_tensor(MT[:], MT[:], bank2(4), ALU.mult).then_inc(s["MT"], 1)
                dve.tensor_tensor(QKT[:], bank2(2), DT[:], ALU.mult).then_inc(s["QKT"], 1)
                dve.wait_ge(s["eb_rows"], h + 1)
                dve.tensor_tensor(er[:], er[:], qkT[:, 0], ALU.mult).then_inc(s["qdec"], 1)
                dve.wait_ge(s["level_M"], LEVELS * h + 1)
                dve.tensor_tensor(XY[:, 1], over_c(C.ident[:]), Ml[:, 0], ALU.subtract)
                dve.wait_ge(s["XY"], (2 * (LEVELS - 1) + 1) * h + 1)
                dve.tensor_tensor(XY[:, 0], over_c(C.ident[:]), bank2(4), ALU.subtract).then_inc(s["XY_ready"], 1)
                for lev in range(1, LEVELS):
                    for hf in range(2):
                        if hf == 0:
                            dve.drain()
                        dve.wait_ge(s["XY"], (2 * (LEVELS - 1) + 1) * h + 2 * (lev - 1) + hf + 2)
                        x = XY[:, :, 4 * hf:4 * hf + 4].rearrange("p a c t -> p a (c t)")
                        dve.tensor_tensor(x, x, ps[:, 2 * hf:2 * hf + 2, :], ALU.subtract).then_inc(s["XY_ready"], 1)
                for c in range(NCK):
                    m = NCK * h + c
                    dve.drain()
                    dve.wait_ge(s["S"], m + 1)
                    if c == 0:
                        dve.tensor_copy(S[:, 1], ps[:, 2, 0:CK]).then_inc(s["S_ready"], 1)
                    else:
                        dve.scalar_tensor_tensor(S[:, (c + 1) % 2], S[:, c % 2], hs[:, 1, c:c + 1], ps[:, 2 + c % 2, 0:CK],
                                                 ALU.mult, ALU.add).then_inc(s["S_ready"], 1)

        @block.tensor
        def _(pe):
            pe.sem_inc(s["tokens"], 1)
            pe.wait_ge(s["tables"], 80)
            pe.transpose(ps[:, 2, 0:96], cr[:], C.ident[0:96, 0:96])
            pe.wait_ge(s["gates"], 1)
            pe.matmul(ps[:, 0, 0:H * NCK], causal[:], gg[:].rearrange("p h c -> p (h c)"), start=True, stop=True)
            pe.matmul(ps[:, 1, 0:H * NCK], C.ones[:], gg[:].rearrange("p h c -> p (h c)"), start=True, stop=True).then_inc(s["cumulated"], 1)
            pe.wait_ge(s["conv_cols_taken"], 1)
            chunk = lambda bank, c: ps[:, bank + c // 4, (c % 4) * CK:(c % 4 + 1) * CK]
            NL = 2 * (LEVELS - 1)
            with pe.Fori(0, H) as h:
                pe.wait_ge(s["diagonals"], h + 1)
                for b in range(2):
                    mm = pe.matmul(ps[:, 6 + b], C.ones[:], flat(dg[:, 0, 4 * b:4 * b + 4]), start=True, stop=True)
                mm.then_inc(s["b_rows"], 1)
                pe.wait_ge(s["silu"], h + 1)
                pe.wait_ge(s["o_taken"], NCK * h + 2)
                pe.wait_ge(s["S_ready"], NCK * h + 1)
                for q in range(3):
                    for c in range(NCK):
                        mm = pe.transpose(chunk(2 * q, c), cv[:, q, c * CK:(c + 1) * CK], C.ident[:])
                mm.then_inc(s["tokens"], 1)
                pe.wait_ge(s["v_beta"], h + 1)
                for b in range(2):
                    mm = pe.matmul(ps[:, 4 + b], C.ones[:], flat(dg[:, 1, 4 * b:4 * b + 4]), start=True, stop=True)
                mm.then_inc(s["beta_rows"], 1)
                pe.wait_ge(s["qk_normed"], h + 1)
                for q in range(2):
                    for c in range(NCK):
                        mm = pe.transpose(chunk(2 * q, c), qk[:, q, c], C.ident[:])
                mm.then_inc(s["qkT"], 1)
                pe.wait_ge(s["qT_taken"], h + 1)
                pe.wait_ge(s["kT_taken"], h + 1)
                for q in range(2):
                    for c in range(NCK):
                        mm = pe.matmul(chunk(2 * q, c), qkT[:, 1, c], qkT[:, 1 - q, c], start=True, stop=True)
                mm.then_inc(s["kk"], 1)
                pe.wait_ge(s["MT"], h + 1)
                pe.wait_ge(s["level_M"], LEVELS * h + 1)
                for c in range(NCK):
                    mm = pe.transpose(chunk(4, c), Ml[:, 0, c], C.ident[:])
                mm.then_inc(s["XY"], 1)
                pe.wait_ge(s["QKT"], h + 1)
                for lev in range(1, LEVELS):
                    pe.wait_ge(s["level_M"], LEVELS * h + lev + 1)
                    for hf in range(2):
                        pe.wait_ge(s["XY_ready"], (NL + 1) * h + (1 if lev == 1 else 2 * (lev - 2) + hf + 2))
                        for c in range(4 * hf, 4 * hf + 4):
                            mm = pe.matmul(chunk(4, c), Ml[:, lev % 2, c], XY[:, 0, c], start=True, stop=True)
                        mm.then_inc(s["P"], 1)
                    for hf in range(2):
                        pe.wait_ge(s["P_taken"], NL * h + 2 * (lev - 1) + hf + 1)
                        for c in range(4 * hf, 4 * hf + 4):
                            pe.matmul(ps[:, 2 * hf, (c % 4) * CK:(c % 4 + 1) * CK], XY[:, 1, c], Pm[:, c], start=True, stop=True)
                        for c in range(4 * hf, 4 * hf + 4):
                            mm = pe.matmul(ps[:, 2 * hf + 1, (c % 4) * CK:(c % 4 + 1) * CK], Pm[:, c], XY[:, 1, c], start=True, stop=True)
                        mm.then_inc(s["XY"], 1)
                pe.wait_ge(s["XY_ready"], (NL + 1) * h + NL + 1)
                pe.wait_ge(s["eb_rows"], h + 1)
                pe.wait_ge(s["kparts"], h + 1)
                for c in range(NCK):
                    mm = pe.matmul(chunk(6, c), kb[:, c], XY[:, 1, c], start=True, stop=True)
                mm.then_inc(s["w"], 1)
                pe.wait_ge(s["w_taken"], h + 1)
                pe.wait_ge(s["qdec"], h + 1)
                for c in range(NCK):
                    m = NCK * h + c
                    pe.wait_ge(s["S_ready"], m + 1)
                    mm = pe.matmul(ps[:, 4 + c % 2, 0:CK], XY[:, 1, c], vb[:, c], start=True, stop=(c == 0))
                    if c > 0:
                        mm = pe.matmul(ps[:, 4 + c % 2, 0:CK], wT[:, c], S[:, c % 2], start=False, stop=True)
                    mm.then_inc(s["v_new"], 1)
                    pe.wait_ge(s["v_new_taken"], m + 1)
                    pe.matmul(ps[:, 2 + c % 2, 0:CK], kd[:, c], vn[:, c % 2], start=True, stop=True).then_inc(s["S"], 1)
                    pe.wait_ge(s["o_taken"], m + 1)
                    if c > 0:
                        pe.matmul(ps[:, c % 2, 0:CK], er[:, c], S[:, c % 2], start=True, stop=False)
                    pe.matmul(ps[:, c % 2, 0:CK], QKT[:, c], vn[:, c % 2], start=(c == 0), stop=True).then_inc(s["o"], 1)


def mlp(C):
    nc, ins = C.nc, C.ins
    FT = FF // P
    UC, DC = FF // CH, FT // 4
    with ExitStack() as st:
        sb = lambda n, s: st.enter_context(nc.sbuf_tensor(f"u_{n}", s, F32))
        sem = lambda n: nc.alloc_semaphore(f"u_{n}")
        w = sb("w", [P, 2, 8 * CH])
        r = sb("r", [P, 2, CH])
        uT = sb("uT", [P, FT, CH])
        post = sb("post", [P, D])
        junk = sb("junk", [P, D])
        mo = sb("mo", [P, 2, D])
        ms = sb("ms", [P, 4, 2])
        ps = st.enter_context(nc.psum_tensor("u_ps", [P, 8, CH], F32))
        s_tab = sem("post_loaded")
        s_w = [sem(f"w_loaded{b}") for b in range(2)]
        s_dn = sem("down_chunk_done")
        s_up = sem("up_done")
        s_r = sem("relu_ready")
        s_rf = sem("relu_squared")
        s_rs = sem("row_rs")
        s_x = sem("x_updated")
        block = st.enter_context(nc.Block())
        wu = ins["w_up_2"][0].rearrange("(k p) n -> p k n", p=P)
        wd = ins["w_down_2"][0].rearrange("(k p) n -> p k n", p=P)

        @block.sync
        def _(sp):
            sp.dma_start(post[:], ins["ln_mlp_post_2"][0].partition_broadcast(P)).then_inc(s_tab, 16)
            with sp.Fori(0, 2) as half:
                sp.wait_ge(s_dn, DC * half + 2)
                for b in range(2):
                    sp.dma_start(w[:, b].rearrange("p (k n) -> p k n", k=KD), wu[:, :, b * CH:(b + 1) * CH]).then_inc(s_w[b], 16)
                with sp.Fori(1, UC // 2) as i:
                    for b in range(2):
                        sp.wait_ge(s_up, 4 * UC * half + 8 * i + 4 * b + 4)
                        sp.dma_start(w[:, b].rearrange("p (k n) -> p k n", k=KD), wu[:, :, ds((2 * i + b) * CH, CH)]).then_inc(s_w[b], 16)
                for b in range(2):
                    sp.wait_ge(s_up, 4 * UC * half + 4 * UC + 4 + 4 * b)
                    sp.dma_start(w[:, b].rearrange("p (k n) -> p k n", k=4), wd[:, 4 * b:4 * b + 4, :]).then_inc(s_w[b], 16)
                with sp.Fori(1, DC // 2) as i:
                    for b in range(2):
                        sp.wait_ge(s_dn, DC * half + 2 * i + b + 1)
                        sp.dma_start(w[:, b].rearrange("p (k n) -> p k n", k=4), wd[:, ds((2 * i + b) * 4, 4), :]).then_inc(s_w[b], 16)

        @block.tensor
        def _(pe):
            pe.sem_inc(s_up, 8)
            pe.sem_inc(s_dn, 2)
            with pe.Fori(0, 2) as half:
                with pe.Fori(0, UC // 2) as i:
                    for b in range(2):
                        pe.wait_ge(s_w[b], 16 * ((UC + DC) // 2) * half + 16 * i + 16)
                        for c in range(4):
                            q = 4 * b + c
                            pe.wait_ge(s_r, 4 * UC * half + 8 * i + q + 1)
                            for k in range(KD):
                                mm = pe.matmul(ps[:, q], w[:, b, k * CH + c * P:k * CH + (c + 1) * P],
                                               C.hT[:, k, ds(half * CH, CH)], start=(k == 0), stop=(k == KD - 1))
                            mm.then_inc(s_up, 1)
                pe.wait_ge(s_rf, 4 * UC * half + 4 * UC + 2)
                for dc in range(DC):
                    pe.wait_ge(s_w[dc % 2], 16 * ((UC + DC) // 2) * half + 16 * (UC // 2 + dc // 2 + 1))
                    for k in range(4):
                        for t in range(4):
                            for h in range(2):
                                f = 4 * dc + k
                                mm = pe.matmul(ps[:, 2 * t + h], uT[:, f, t * P:(t + 1) * P],
                                               w[:, dc % 2, k * D + h * CH:k * D + (h + 1) * CH],
                                               start=(f == 0), stop=(f == FT - 1))
                    mm.then_inc(s_dn, 1)
                pe.wait_ge(s_x, 4 * half + 4)

        @block.scalar
        def _(act):
            act.sem_inc(s_r, 8)
            with act.Fori(0, 2) as half:
                with act.Fori(0, UC // 2) as i:
                    for q in range(8):
                        n = 4 * UC * half + 8 * i + q
                        act.wait_ge(s_up, n + 9)
                        act.wait_ge(s_rf, n + 1)
                        act.activation(r[:, q % 2], ps[:, q], ACT.Relu).then_inc(s_r, 1)
                act.wait_ge(s_dn, DC * half + DC + 2)
                for t in range(4):
                    act.activation(junk[:], ps[:, 2 * t:2 * t + 2].rearrange("p a b -> p (a b)"), ACT.Square, accum_out=ms[:, t, 0:1])
                    act.drain()
                    act.activation(ms[:, t, 1:2], ms[:, t, 0:1], ACT.Ln, bias=C.eps[:], scale=1.0 / D)
                    act.drain()
                    act.activation(ms[:, t, 1:2], ms[:, t, 1:2], ACT.Exp, scale=-0.5).then_inc(s_rs, 1)

        @block.vector
        def _(dve):
            dve.sem_inc(s_rf, 2)
            dve.wait_ge(s_tab, 16)
            with dve.Fori(0, 2) as half:
                with dve.Fori(0, UC // 2) as i:
                    for q in range(8):
                        dve.wait_ge(s_r, 4 * UC * half + 8 * i + q + 9)
                        dve.tensor_tensor(uT[:, ds(8 * i + q, 1), :].rearrange("p a b -> p (a b)"), r[:, q % 2], r[:, q % 2],
                                          ALU.mult).then_inc(s_rf, 1)
                for t in range(4):
                    dve.wait_ge(s_rs, 4 * half + t + 1)
                    dve.scalar_tensor_tensor(mo[:, t % 2], ps[:, 2 * t:2 * t + 2].rearrange("p a b -> p (a b)"), ms[:, t, 1:2], post[:],
                                             ALU.mult, ALU.mult)
                    dve.drain()
                    x = C.x_sb[:, ds(4 * half + t, 1), :].rearrange("p t n -> p (t n)")
                    dve.tensor_tensor(x, x, mo[:, t % 2], ALU.add).then_inc(s_x, 1)


def second_block(C, out):
    nc, ins = C.nc, C.ins
    C.pt_dram = nc.dram_tensor("pt_dram", (T_C + 3 * D, SEQ), F32, kind="Internal").ap()
    C.pn_dram = nc.dram_tensor("pn_dram", (SEQ, N_M + 3 * D), F32, kind="Internal").ap()
    C.o_dram = [nc.dram_tensor(f"o{b}_dram", (SEQ, D), F32, kind="Internal").ap() for b in "abc"]
    with ExitStack() as s2:
        C.gk = s2.enter_context(nc.sbuf_tensor("gk", [P, B_HEADS, SEQ], F32))
        C.ab = s2.enter_context(nc.sbuf_tensor("ab2", [P, NT, 2 * C_HEADS], F32))
        load_norm_gain(C, "lg0", ins["ln_mix_pre_2"][0])
        with ExitStack() as s3:
            C.hT = s3.enter_context(nc.sbuf_tensor("hTm", [P, KD, SEQ], F32))
            norm_transpose(C, "n2", [(0, NT, 0)])
            small_projections(C)
            w = ins["w_in_2"][0]
            pt, pn = C.pt_dram, C.pn_dram
            token = lambda a, z, c: dict(w=w[:, a:z], out=pn[:, c:c + z - a], kind="token", tiles=range(NT))
            channel = lambda a, z, r: dict(w=w[:, a:z], out=pt[r:r + z - a, :], kind="channel", tiles=None)
            project(C, "p2", C.hT, [
                channel(A_Q, A_I, T_AQ), token(A_I, B_Q, N_AI), channel(B_Q, B_V, T_BQ), token(B_V, B_GK, N_BV),
                token(B_G, C_QKV, N_BG), channel(C_QKV, C_A, T_C), token(C_G, MERGE, N_CG), token(MERGE, N_IN, N_M)])
        gated_linear(C, "a")
        gated_linear(C, "b")
        gated_delta(C)
    merge_out(C)
    load_norm_gain(C, "lg1", ins["ln_mlp_pre_2"][0])
    with ExitStack() as s3:
        C.hT = s3.enter_context(nc.sbuf_tensor("hTu", [P, KD, SEQ], F32))
        norm_transpose(C, "n3", [(0, NT, 0)])
        mlp(C)
    store_x(C, out)


def tables():
    import numpy as np
    f = np.float32
    out = {"t_ident": np.eye(P, dtype=f)}
    sel = np.zeros((2, 2, P), f)
    sel[0, 0], sel[1, 1] = 1, 1
    out["t_sel"] = sel
    for name, n in (("t_dft_x", SEQ), ("t_dft_c", CTX)):
        jk = np.outer(np.arange(n), np.arange(n)) % n
        ang = 2 * np.pi * jk / n
        out[name] = (np.stack([np.cos(ang), np.sin(ang)]) / np.sqrt(n)).astype(f)
    ang = 2 * np.pi * (np.outer(np.arange(QK), np.arange(QK)) % QK) / QK
    chan = np.zeros((2, P, P))
    for o in (0, QK):
        chan[0, o:o + QK, o:o + QK] = np.cos(ang) / np.sqrt(QK)
        chan[1, o:o + QK, o:o + QK] = -np.sin(ang) / np.sqrt(QK)
    out["t_chan"] = chan.astype(f)
    band = np.zeros((P, 5, 4, P))
    L = 4 * P
    for g, w in enumerate(WINDOWS):
        full = np.zeros((L, L))
        for t in range(L):
            a, b = max(t - w // 2, 0), min(t + w - w // 2 - 1, L - 1)
            full[a:b + 1, t] = 1.0 / (b - a + 1)
        full -= np.eye(L)
        for kind, (r, c) in enumerate(((0, 0), (1, 1), (3, 3), (0, 1), (1, 0))):
            band[:, kind, g, :] = full[r * P:(r + 1) * P, c * P:(c + 1) * P]
    out["t_band"] = band.astype(f)
    t = np.arange(SEQ)
    half = QK // 2
    inv = (10000.0 ** (-np.arange(0, half, 2, dtype=f) / half)).astype(f)
    r, c = (t // 64).astype(f)[:, None] * inv, (t % 64).astype(f)[:, None] * inv
    ang = np.concatenate([r, r, c, c], axis=1).astype(np.float64)
    sign = np.tile(np.repeat([-1.0, 1.0], QK // 4), 2)
    out["t_rope"] = np.stack([np.cos(ang), np.sin(ang) * sign]).astype(f)
    i = np.arange(CK)
    lv = np.zeros((CK, LEVELS + 1, CK))
    for q in range(LEVELS):
        s = 1 << q
        lv[:, q, :] = ((i[:, None] // (2 * s)) == (i[None, :] // (2 * s))) & ((i[:, None] // s) % 2 == 0) & ((i[None, :] // s) % 2 == 1)
    lv[:, LEVELS, :] = np.eye(CK)
    out["t_levels"] = lv.astype(f)
    out["t_causal"] = (i[:, None] <= i[None, :]).astype(f)
    start = np.ones((P, SEQ), f)
    start[:, ::CK] = 0
    out["t_restart"] = start
    return out


def build(nc, ins, out):
    C = Shared()
    C.nc, C.ins = nc, ins
    C.p_dram = nc.dram_tensor("p_dram", (SEQ + CTX, INW), F32, kind="Internal").ap()
    with ExitStack() as st:
        sb = lambda n, s, k=st: k.enter_context(nc.sbuf_tensor(n, s, F32))
        C.x_sb = sb("x_sb", [P, NTA, D])
        C.ident = sb("ident", [P, P])
        C.eps = sb("eps", [P, 1])
        C.zero = sb("zero", [P, KD])
        C.ones = sb("ones", [P, P])
        C.shift = sb("shift", [P, 2, KD])
        C.scale = sb("scale", [P, 2, KD])
        C.y_dram = nc.dram_tensor("y_dram", (SEQ, D), F32, kind="Internal").ap()
        load_constants(C)
        with ExitStack() as st1:
            C.mix = sb("mix", [P, NTA, D], st1)
            C.gate = sb("gate", [P, 2, D], st1)
            C.neglam = sb("neglam", [P, 1], st1)
            for l in range(DEPTH):
                last = l == DEPTH - 1
                with fresh_semaphores(nc):
                    modulation(C, l)
                    with ExitStack() as s2:
                        C.hT = sb(f"hT{l}", [P, KD, SEQ + CTX], s2)
                        norm_transpose(C, f"n{l}", [(0, NT, 0), (NT, NTC, 1)])
                        w = ins["w_in"][l]
                        if last:
                            segs = [dict(w=w, out=C.p_dram, kind="token", tiles=range(NT)),
                                    dict(w=w[:, K0:G0], out=C.p_dram[:, K0:G0], kind="token", tiles=range(NT, NTA))]
                        else:
                            segs = [dict(w=w, out=C.p_dram, kind="token", tiles=range(NTA))]
                        project(C, f"p{l}", C.hT, segs)
                    fourier_pool(C, l, "x")
                    if not last:
                        fourier_pool(C, l, "c")
                    with ExitStack() as s2:
                        C.qT = sb(f"qT{l}", [P, HEADS, SEQ + CTX], s2)
                        C.kT = sb(f"kT{l}", [P, HEADS, SEQ + CTX], s2)
                        C.v_sb = sb(f"v{l}", [P, NTA, 512], s2)
                        qk_prepare(C, l)
                        attention(C, l)
                    mix_out(C, l)
        with fresh_semaphores(nc):
            second_block(C, out)


def store_x(C, out):
    nc = C.nc
    with ExitStack() as st:
        s_out = nc.alloc_semaphore("x_stored")
        block = st.enter_context(nc.Block())

        @block.sync
        def _(sp):
            sp.dma_start(out[0].rearrange("(t p) d -> p t d", p=P), C.x_sb[:, 0:NT, :]).then_inc(s_out, 16)
            sp.wait_ge(s_out, 16)


_INS = ["x", "c", "ctx", "c_ctx", "norm_g", "w_mod", "b_mod", "w_in", "w_fourier", "w_pool", "pool_scale",
        "qk_norm_g", "lam_vecs", "subln_g", "w_out", "ln_mix_pre_2", "ln_mix_post_2", "ln_mlp_pre_2",
        "ln_mlp_post_2", "w_in_2", "hgrn_lb_logits_2", "gla_w_gk_2", "gla_b_gk_2", "gdn_conv_2",
        "gdn_a_log_2", "gdn_dt_bias_2", "hgrn_onorm_2", "gla_onorm_2", "gdn_onorm_2", "w_out_2",
        "w_up_2", "w_down_2"]


def kernel(**inputs):
    import numpy as np
    import concourse.bacc as bacc
    from concourse.bass_utils import run_bass_kernel_spmd
    arrays = {n: np.ascontiguousarray(inputs[n]) for n in _INS}
    arrays.update(tables())
    nc = bacc.Bacc("TRN2", target_bir_lowering=False, num_devices=1)
    ins = {n: nc.dram_tensor(n, a.shape, F32, kind="ExternalInput").ap() for n, a in arrays.items()}
    out = nc.dram_tensor("out", (1, SEQ, D), F32, kind="ExternalOutput").ap()
    build(nc, ins, out)
    r = run_bass_kernel_spmd(nc, [arrays], core_ids=[0])
    return r.results[0]["out"]
```

```python
from contextlib import ExitStack, contextmanager

import math

import concourse.bass as bass
import concourse.mybir as mybir

F32 = mybir.dt.float32
F32R = mybir.dt.float32r
ALU = mybir.AluOpType
ACT = mybir.ActivationFunctionType
AX = mybir.AxisListType

P = 128
D = 1024
KD = D // P
SEQ, CTX = 1024, 256
NT, NTC = SEQ // P, CTX // P
NTA = NT + NTC
DEPTH = 2
EPS = 1e-6
CH = 512
FW = 256
HEADS, QK, DV = 4, 64, 128
Q0, K0, V0, G0, INW = 512, 1024, 1536, 2048, 3072
WINDOWS = (2, 4, 8, 16)

NORMED = (1, QK, DV, 256, D)
A_HEADS, B_HEADS, C_HEADS = 8, 4, 8
FF = 4096
CK = 128
NCK = SEQ // CK
LEVELS = 7


class Shared:
    pass


def ds(start, size):
    return bass.ds(start, size)


def inverse_root(C, pool, out, sums, n):
    w = out.shape[-1]
    pool.tensor_tensor(out, sums, C.n_eps[:, NORMED.index(n), 0:w], ALU.add)
    pool.drain()
    pool.tensor_tensor(out, out, C.minus_half[:, 0:w], ALU.pow)
    pool.drain()
    return pool.tensor_scalar(out, out, float(n) ** 0.5, None, ALU.mult)


@contextmanager
def fresh_semaphores(nc):
    before = nc.snapshot_sems()
    yield
    nc.clear_and_free_semaphores(nc.allocated_since(before))
    nc.all_engine_barrier()


def load_constants(C):
    nc, ins = C.nc, C.ins
    with ExitStack() as st:
        s_in = nc.alloc_semaphore("c0_in")
        block = st.enter_context(nc.Block())

        @block.sync
        def _(sp):
            sp.dma_start(C.x_sb[:, 0:NT, :], ins["x"][0].rearrange("(t p) d -> p t d", p=P)).then_inc(s_in, 16)
            sp.dma_start(C.x_sb[:, NT:NTA, :], ins["ctx"][0].rearrange("(t p) d -> p t d", p=P)).then_inc(s_in, 16)
            sp.dma_start(C.ident[:], ins["t_ident"]).then_inc(s_in, 16)
            sp.wait_ge(s_in, 48)

        @block.gpsimd
        def _(pool):
            pool.memset(C.minus_half[:], -0.5)
            for q, n in enumerate(NORMED):
                pool.memset(C.n_eps[:, q], n * EPS)
            pool.memset(C.ones[:], 1.0)


def modulation(C, l):
    nc, ins = C.nc, C.ins
    NCH = 3 * D // CH
    with ExitStack() as st:
        sb = lambda n, s: st.enter_context(nc.sbuf_tensor(f"m{l}_{n}", s, F32))
        sem = lambda n: nc.alloc_semaphore(f"m{l}_{n}")
        cT = sb("cT", [P, KD, 2])
        sc = sb("sc", [P, KD, 2])
        w = sb("w", [P, 2, KD, CH])
        bm = sb("bm", [2, 3 * D])
        mrow = sb("mrow", [2, 3 * D])
        sel = sb("sel", [2, 2, P])
        ng = sb("ng", [P, KD])
        lv = sb("lv", [P, 4, QK])
        lp = sb("lp", [P, 2, QK])
        ls = sb("ls", [P, 4])
        ps = st.enter_context(nc.psum_tensor(f"m{l}_ps", [P, 2, CH], F32))
        psT = st.enter_context(nc.psum_tensor(f"m{l}_psT", [P, 16, 2], F32))
        psG = st.enter_context(nc.psum_tensor(f"m{l}_psG", [P, 4, CH], F32))
        s_in = sem("small_loaded")
        s_w = [sem(f"w_loaded{b}") for b in range(2)]
        s_sc = sem("silu_ready")
        s_mm = sem("row_product_done")
        s_ev = sem("row_taken")
        s_T = sem("columns_transposed")
        s_G = sem("gates_spread")
        s_lp = sem("lam_sums")
        s_le = sem("lam_exps")
        block = st.enter_context(nc.Block())
        wv = ins["w_mod"][l].rearrange("(k p) n -> p k n", p=P)

        @block.sync
        def _(sp):
            with nc.allow_non_contiguous_dma("4 KB of channel vectors"):
                sp.dma_start(cT[:, :, 0], ins["c"][0].rearrange("(k p) -> p k", p=P)).then_inc(s_in, 16)
                sp.dma_start(cT[:, :, 1], ins["c_ctx"].rearrange("(k p) -> p k", p=P)).then_inc(s_in, 16)
                sp.dma_start(ng[:], ins["norm_g"][l].rearrange("(k p) -> p k", p=P)).then_inc(s_in, 16)
            for r in range(2):
                sp.dma_start(bm[r:r + 1, :], ins["b_mod"][l:l + 1, :]).then_inc(s_in, 16)
            sp.dma_start(sel[:], ins["t_sel"]).then_inc(s_in, 16)
            sp.dma_start(lv[:], ins["lam_vecs"][l].rearrange("a b -> (a b)").partition_broadcast(P)
                         .rearrange("p (a b) -> p a b", a=4)).then_inc(s_in, 16)
            for b in range(2):
                sp.dma_start(w[:, b], wv[:, :, b * CH:(b + 1) * CH]).then_inc(s_w[b], 16)
            with sp.Fori(1, NCH // 2) as i:
                for b in range(2):
                    sp.wait_ge(s_mm, 2 * i + b - 1)
                    sp.dma_start(w[:, b], wv[:, :, ds((2 * i + b) * CH, CH)]).then_inc(s_w[b], 16)

        @block.scalar
        def _(act):
            act.wait_ge(s_in, 16 * 7)
            act.activation(sc[:], cT[:], ACT.Silu).then_inc(s_sc, 1)
            act.wait_ge(s_lp, 1)
            act.activation(ls[:, 2:4], ls[:, 0:2], ACT.Exp).then_inc(s_le, 1)

        @block.tensor
        def _(pe):
            pe.wait_ge(s_sc, 1)
            with pe.Fori(0, NCH // 2) as i:
                for b in range(2):
                    pe.wait_ge(s_w[b], 16 * i + 16)
                    pe.wait_ge(s_ev, 2 * i + b + 1)
                    for k in range(KD):
                        mm = pe.matmul(ps[0:2, b, :], sc[:, k, :], w[:, b, k, :], start=(k == 0), stop=(k == KD - 1))
                    mm.then_inc(s_mm, 1)
            pe.wait_ge(s_ev, NCH + 2)
            for j in range(16):
                mm = pe.transpose(psT[:, j, :], mrow[:, j * P:(j + 1) * P], C.ident[0:2, 0:2])
            mm.then_inc(s_T, 1)
            for r in range(2):
                for h in range(2):
                    mm = pe.matmul(psG[:, 2 * r + h, :], sel[:, r, :], mrow[:, 2 * D + h * CH:2 * D + (h + 1) * CH],
                                   start=True, stop=True)
            mm.then_inc(s_G, 1)

        @block.vector
        def _(dve):
            dve.sem_inc(s_ev, 2)
            dve.wait_ge(s_in, 16 * 7)
            for r in range(2):
                dve.tensor_tensor(lp[:, r, :], lv[:, 2 * r, :], lv[:, 2 * r + 1, :], ALU.mult)
            dve.drain()
            dve.tensor_reduce(ls[:, 0:2], lp[:], AX.X, ALU.add).then_inc(s_lp, 1)
            dve.wait_ge(s_le, 1)
            dve.tensor_tensor(C.neglam[:], ls[:, 3:4], ls[:, 2:3], ALU.subtract)
            dve.drain()
            lam_init = 0.8 - 0.6 * math.exp(-0.3 * l)
            dve.tensor_scalar(C.neglam[:], C.neglam[:], lam_init, None, ALU.subtract)
            with dve.Fori(0, NCH // 2) as i:
                for b in range(2):
                    dve.wait_ge(s_mm, 2 * i + b + 1)
                    dve.tensor_tensor(mrow[:, ds((2 * i + b) * CH, CH)], ps[0:2, b, :],
                                      bm[:, ds((2 * i + b) * CH, CH)], ALU.add).then_inc(s_ev, 1)
            dve.wait_ge(s_T, 1)
            for r in range(2):
                dve.tensor_copy(C.shift[:, r, :], psT[:, 0:KD, r])
                dve.scalar_tensor_tensor(C.scale[:, r, :], psT[:, KD:2 * KD, r], 1.0, ng[:], ALU.add, ALU.mult)
            dve.wait_ge(s_G, 1)
            for r in range(2):
                for h in range(2):
                    dve.tensor_copy(C.gate[:, r, h * CH:(h + 1) * CH], psG[:, 2 * r + h, :])


def norm_transpose(C, tag, segs):
    nc = C.nc
    with ExitStack() as st:
        sb = lambda n, s: st.enter_context(nc.sbuf_tensor(f"{tag}_{n}", s, F32))
        sem = lambda n: nc.alloc_semaphore(f"{tag}_{n}")
        sq = sb("sq", [P, D])
        ms = sb("ms", [P, 2])
        rs = sb("rs", [P, 2])
        xs = sb("xs", [P, 2, D])
        full = sb("full", [P, 2, KD, P])
        pt = st.enter_context(nc.psum_tensor(f"{tag}_pt", [P, 2, KD, P], F32))
        s_ms = sem("sum_ready")
        s_rs = sem("rs_ready")
        s_xs = sem("xs_ready")
        s_T = sem("transposed")
        s_eA = sem("taken_by_act")
        s_eD = sem("taken_by_dve")
        s_lo = sem("act_half_split")
        block = st.enter_context(nc.Block())
        first = segs[0][0]
        part = lambda ap, half, tile: ap[:, half * (KD // 2):(half + 1) * (KD // 2), ds((tile - first) * P, P)]
        bases, n = [], 0
        for _, m, _ in segs:
            bases.append(n)
            n += m

        @block.scalar
        def _(act):
            act.sem_inc(s_eA, 2)
            for (t0, m, r), n0 in zip(segs, bases):
                with act.Fori(0, m // 2) as i:
                    for b in range(2):
                        act.wait_ge(s_xs, n0 + 2 * i + b + 1)
                        act.activation(sq[:], C.x_sb[:, t0 + 2 * i + b, :], ACT.Square,
                                       accum_out=ms[:, b:b + 1]).then_inc(s_ms, 1)
                        act.drain()
                    for b in range(2):
                        act.wait_ge(s_T, n0 + 2 * i + b + 3)
                        act.wait_ge(s_lo, n0 + 2 * i + b + 1)
                        for k in range(KD // 2):
                            act.activation(full[:, b, k, :], pt[:, b, k, :], ACT.Identity,
                                           bias=C.shift[:, r, k:k + 1], scale=C.scale[:, r, k:k + 1])
                        act.drain()
                        act.copy(part(C.hi, 0, t0 + 2 * i + b), full[:, b, 0:KD // 2]).then_inc(s_eA, 1)

        @block.gpsimd
        def _(pool):
            pool.sem_inc(s_lo, 2)
            for (t0, m, r), n0 in zip(segs, bases):
                with pool.Fori(0, m // 2) as i:
                    for b in range(2):
                        pool.wait_ge(s_ms, n0 + 2 * i + b + 1)
                        inverse_root(C, pool, rs[:, b:b + 1], ms[:, b:b + 1], D).then_inc(s_rs, 1)
                    for b in range(2):
                        t = t0 + 2 * i + b
                        pool.wait_ge(s_eA, n0 + 2 * i + b + 3)
                        pool.tensor_tensor(part(C.lo, 0, t), full[:, b, 0:KD // 2], part(C.hi, 0, t),
                                           ALU.subtract).then_inc(s_lo, 1)

        @block.vector
        def _(dve):
            dve.sem_inc(s_xs, 2)
            dve.sem_inc(s_eD, 2)
            for (t0, m, r), n0 in zip(segs, bases):
                with dve.Fori(0, m // 2) as i:
                    for b in range(2):
                        dve.wait_ge(s_rs, n0 + 2 * i + b + 1)
                        dve.wait_ge(s_T, n0 + 2 * i + b + 1)
                        dve.tensor_scalar(xs[:, b, :], C.x_sb[:, t0 + 2 * i + b, :], rs[:, b:b + 1], None,
                                          ALU.mult).then_inc(s_xs, 1)
                    for b in range(2):
                        dve.wait_ge(s_T, n0 + 2 * i + b + 3)
                        for k in range(KD // 2, KD):
                            e = dve.tensor_scalar(full[:, b, k, :], pt[:, b, k, :],
                                                  C.scale[:, r, k:k + 1], C.shift[:, r, k:k + 1], ALU.mult, ALU.add)
                        e.then_inc(s_eD, 1)
                        t = t0 + 2 * i + b
                        dve.drain()
                        dve.tensor_copy(part(C.hi, 1, t), full[:, b, KD // 2:])
                        dve.drain()
                        dve.tensor_tensor(part(C.lo, 1, t), full[:, b, KD // 2:], part(C.hi, 1, t), ALU.subtract)
                        dve.drain()

        @block.tensor
        def _(pe):
            pe.sem_inc(s_T, 2)
            for (t0, m, r), n0 in zip(segs, bases):
                with pe.Fori(0, m // 2) as i:
                    for b in range(2):
                        pe.wait_ge(s_xs, n0 + 2 * i + b + 3)
                        pe.wait_ge(s_eA, n0 + 2 * i + b + 1)
                        pe.wait_ge(s_eD, n0 + 2 * i + b + 1)
                        for k in range(KD):
                            mm = pe.transpose(pt[:, b, k, :], xs[:, b, k * P:(k + 1) * P], C.ident[:])
                        mm.then_inc(s_T, 1)


def project(C, tag, segs):
    nc = C.nc
    NB = 8
    SG = 4
    KH = KD // 2
    with ExitStack() as st:
        sb = lambda n, s, dt=F32: st.enter_context(nc.sbuf_tensor(f"{tag}_{n}", s, dt))
        sem = lambda n: nc.alloc_semaphore(f"{tag}_{n}")
        raw = sb("raw", [P, 2, KH, CH])
        wh = sb("wh", [P, 2, KH, CH], F32R)
        wl = sb("wl", [P, 2, KH, CH], F32R)
        stg = sb("stg", [P, SG, CH])
        ps = st.enter_context(nc.psum_tensor(f"{tag}_ps", [P, NB, CH], F32))
        s_raw = [sem(f"raw{h}_loaded") for h in range(2)]
        s_wh = [sem(f"hi{h}_ready") for h in range(2)]
        s_wl = [sem(f"lo{h}_ready") for h in range(2)]
        s_half = sem("first_half_done")
        s_mm = sem("unit_done")
        s_eA = sem("taken_by_act")
        s_eD = sem("taken_by_dve")
        s_st = [sem(f"stored{q}") for q in range(SG)]
        block = st.enter_context(nc.Block())

        plan, n0, c0 = [], 0, 0
        for s in segs:
            chunks = s["w"].shape[1] // CH
            per = len(s["tiles"]) if s["kind"] == "token" else 2 * (CH // P)
            group = 1 if per == NB else 2
            assert per in (2, NB) and chunks % 2 == 0 and (group * per) % SG == 0
            assert not plan or group * per <= plan[-1]["dist"]
            plan.append(dict(s, chunks=chunks, group=group, steps=chunks // group, per=per, dist=group * per,
                             n0=n0, c0=c0, wv=s["w"].rearrange("(k p) n -> p k n", p=P)))
            n0 += chunks * per
            c0 += chunks
        total = n0

        @block.tensor
        def _(pe):
            for s in plan:
                per, group = s["per"], s["group"]
                with pe.Fori(0, s["steps"]) as i:
                    for b in range(group):
                        c = s["c0"] + group * i + b
                        for kh in range(2):
                            pe.wait_ge(s_wl[kh], c + 1)
                            for j in range(per):
                                u = b * per + j
                                n = s["n0"] + group * per * i + u
                                if kh == 0:
                                    base = (s["n0"] + NB - s["dist"]) // 2 + (group * per // 2) * i
                                    pe.wait_ge(s_eA if u % 2 == 0 else s_eD, base + u // 2 + 1)
                                for k in range(KH):
                                    kk = kh * KH + k
                                    for q, (first, second) in enumerate(((0, 0), (0, 1), (1, 0))):
                                        h, w = (C.hi, C.lo)[first], (wh, wl)[second]
                                        if s["kind"] == "token":
                                            t = s["tiles"][j]
                                            lhsT, rhs = h[:, kk, t * P:(t + 1) * P], w[:, kh, k, :]
                                        else:
                                            cc, half = j // 2, j % 2
                                            lhsT, rhs = w[:, kh, k, cc * P:(cc + 1) * P], h[:, kk, half * CH:(half + 1) * CH]
                                        mm = pe.matmul(ps[:, u, :], lhsT, rhs, start=(kk == 0 and q == 0),
                                                       stop=(kk == KD - 1 and q == 2))
                                if kh == 1:
                                    mm.then_inc(s_mm, 1)
                            if kh == 0:
                                mm.then_inc(s_half, 1)

        def split_and_take(eng, split, take, first_unit):
            for kh in range(2):
                split(kh, 0)
            for q, s in enumerate(plan):
                def step(i, b, more):
                    c = s["c0"] + s["group"] * i + b
                    if more:
                        eng.wait_ge(s_half, c + 1)
                        split(0, c + 1)
                    for j in range(first_unit, s["per"], 2):
                        take(s, i, b * s["per"] + j)
                    if more:
                        eng.wait_ge(s_mm, s["n0"] + s["per"] * (s["group"] * i + b + 1))
                        split(1, c + 1)
                steps = s["steps"] - (q == len(plan) - 1)
                if steps:
                    with eng.Fori(0, steps) as i:
                        for b in range(s["group"]):
                            step(i, b, True)
                if q == len(plan) - 1:
                    for b in range(s["group"]):
                        step(steps, b, b < s["group"] - 1)

        def wait_taken(eng, s, i, u):
            gp = s["group"] * s["per"]
            eng.wait_ge(s_mm, s["n0"] + gp * i + u + 1)
            eng.wait_ge(s_st[u % SG], 16 * (s["n0"] // SG + (gp // SG) * i + u // SG + 1))

        @block.scalar
        def _(act):
            act.sem_inc(s_eA, NB // 2)

            def split(kh, c):
                act.wait_ge(s_raw[kh], 16 * (c + 1))
                act.copy(wh[:, kh], raw[:, kh]).then_inc(s_wh[kh], 1)

            def take(s, i, u):
                wait_taken(act, s, i, u)
                act.copy(stg[:, u % SG, :], ps[:, u, :]).then_inc(s_eA, 1)
            split_and_take(act, split, take, 0)

        @block.vector
        def _(dve):
            dve.sem_inc(s_eD, NB // 2)

            def split(kh, c):
                dve.wait_ge(s_wh[kh], c + 1)
                dve.tensor_tensor(wl[:, kh], raw[:, kh], wh[:, kh], ALU.subtract).then_inc(s_wl[kh], 1)

            def take(s, i, u):
                wait_taken(dve, s, i, u)
                dve.tensor_copy(stg[:, u % SG, :], ps[:, u, :]).then_inc(s_eD, 1)
            split_and_take(dve, split, take, 1)

        @block.sync
        def _(sp):
            for q in range(SG):
                sp.sem_inc(s_st[q], 16)

            def load(s, kh, chunk):
                sp.dma_start(raw[:, kh], s["wv"][:, kh * KH:(kh + 1) * KH, ds(chunk * CH, CH)]).then_inc(s_raw[kh], 16)

            for kh in range(2):
                load(plan[0], kh, 0)
            for kh in range(2):
                sp.wait_ge(s_wl[kh], 1)
                load(plan[0], kh, 1)

            def step(s, i, b, target, chunk):
                c = s["c0"] + s["group"] * i + b
                if target:
                    sp.wait_ge(s_wl[0], c + 2)
                    load(target, 0, chunk)
                for j in range(s["per"]):
                    u = b * s["per"] + j
                    gp = s["group"] * s["per"]
                    sp.wait_ge(s_eA if u % 2 == 0 else s_eD, s["n0"] // 2 + (gp // 2) * i + u // 2 + 1 + NB // 2)
                    if s["kind"] == "token":
                        t = s["tiles"][j]
                        dst = s["out"][t * P:(t + 1) * P, ds((s["group"] * i + b) * CH, CH)]
                    else:
                        cc, half = j // 2, j % 2
                        dst = s["out"][ds((s["group"] * i + b) * CH + cc * P, P), half * CH:(half + 1) * CH]
                    sp.dma_start(dst, stg[:, u % SG, :]).then_inc(s_st[u % SG], 16)
                if target:
                    sp.wait_ge(s_wl[1], c + 2)
                    load(target, 1, chunk)

            for q, s in enumerate(plan):
                group, tail = s["group"], 2 // s["group"]
                if s["steps"] > tail:
                    with sp.Fori(0, s["steps"] - tail) as i:
                        for b in range(group):
                            step(s, i, b, s, group * i + b + 2)
                for x in range(2):
                    i = s["steps"] - tail + x // group
                    step(s, i, x % group, plan[q + 1] if q + 1 < len(plan) else None, x)
            for q in range(SG):
                sp.wait_ge(s_st[q], 16 * (total // SG + 1))


def fourier_pool(C, l, rows):
    nc, ins = C.nc, C.ins
    tiles, r0 = (NT, 0) if rows == "x" else (NTC, SEQ)
    length = tiles * P
    N = min(CH, length)
    NH = length // N
    tag = f"f{l}{rows}"
    with ExitStack() as st:
        sb = lambda n, s: st.enter_context(nc.sbuf_tensor(f"{tag}_{n}", s, F32))
        sem = lambda n: nc.alloc_semaphore(f"{tag}_{n}")
        ab = sb("ab", [P, tiles, 2 * FW])
        dft = sb("dft", [P, 2, tiles, N])
        chan = sb("chan", [P, 2, P])
        band = sb("band", [P, 5, 4, P])
        wfb = sb("wfb", [P, 2, P])
        wpb = sb("wpb", [P, 2, P])
        psc = sb("psc", [P, 2, P])
        G = sb("G", [P, 2, 2, P])
        yt = sb("yt", [P, 2, 2, length])
        pool = sb("pool", [P, 2, length])
        pg = st.enter_context(nc.psum_tensor(f"{tag}_pg", [P, 2, 2, P], F32))
        py = st.enter_context(nc.psum_tensor(f"{tag}_py", [P, 2, CH], F32))
        pp = st.enter_context(nc.psum_tensor(f"{tag}_pp", [P, 2, CH], F32))
        po = st.enter_context(nc.psum_tensor(f"{tag}_po", [P, 2, CH], F32))
        s_ab = sem("ab_loaded")
        s_tab = sem("tables_loaded")
        s_z = sem("diagonals_zeroed")
        s_wd = sem("diagonals_loaded")
        s_wp = sem("w_pool_scaled")
        s_dft = [sem(f"dft_loaded{b}") for b in range(2)]
        s_g = sem("G_product")
        s_gc = sem("G_ready")
        s_y = sem("token_dft")
        s_yc = sem("token_dft_taken")
        s_p = sem("pooled")
        s_pc = sem("pooled_taken")
        s_o = sem("branch_out")
        s_oc = sem("branch_out_taken")
        block = st.enter_context(nc.Block())
        table = ins["t_dft_x" if rows == "x" else "t_dft_c"]
        order = [(h, g) for h in range(NH) for g in range(2)]

        def table_chunk(h, g):
            return table[g].rearrange("(k p) n -> p k n", p=P)[:, :, h * N:(h + 1) * N]

        @block.sync
        def _(sp):
            sp.dma_start(ab[:], C.p_dram[r0:r0 + length, 0:2 * FW].rearrange("(t p) n -> p t n", p=P)).then_inc(s_ab, 16)
            for q, (h, g) in enumerate(order):
                if q >= 2:
                    sp.wait_ge(s_y, 2 * (q - 1))
                sp.dma_start(dft[:, q % 2], table_chunk(h, g)).then_inc(s_dft[q % 2], 16)

        @block.gpsimd
        def _(pool_eng):
            pool_eng.memset(wfb[:], 0.0).then_inc(s_z, 1)
            pool_eng.memset(wpb[:], 0.0).then_inc(s_z, 1)
            pool_eng.dma_start(chan[:], ins["t_chan"].rearrange("g p n -> p g n")).then_inc(s_tab, 16)
            pool_eng.dma_start(band[:], ins["t_band"]).then_inc(s_tab, 16)
            pool_eng.dma_start(psc[:].rearrange("p a b -> p (a b)"),
                               ins["pool_scale"][l].partition_broadcast(P)).then_inc(s_tab, 16)
            pool_eng.wait_ge(s_z, 2)
            for g in range(4):
                o = QK * (g % 2)
                pool_eng.dma_start(wfb[o:o + QK, g // 2, o:o + QK], ins["w_fourier"][l, g]).then_inc(s_wd, 16)
                pool_eng.dma_start(wpb[o:o + QK, g // 2, o:o + QK], ins["w_pool"][l, g]).then_inc(s_wd, 16)

        @block.tensor
        def _(pe):
            pe.wait_ge(s_tab, 48)
            pe.wait_ge(s_wd, 16 * 8)
            for g in range(2):
                for c in range(2):
                    mm = pe.matmul(pg[:, g, c, :], chan[:, g, :], wfb[:, c, :], start=True, stop=True)
            mm.then_inc(s_g, 1)
            pe.wait_ge(s_ab, 16)
            for q, (h, g) in enumerate(order):
                pe.wait_ge(s_dft[q % 2], 16 * (q // 2 + 1))
                for c in range(2):
                    if q >= 1:
                        pe.wait_ge(s_yc, 2 * (q - 1) + c + 1)
                    for k in range(tiles):
                        mm = pe.matmul(py[:, c, 0:N], ab[:, k, c * P:(c + 1) * P], dft[:, q % 2, k, :],
                                       start=(k == 0), stop=(k == tiles - 1))
                    mm.then_inc(s_y, 1)
            for t in range(tiles):
                if t >= 2:
                    pe.wait_ge(s_pc, t - 1)
                for g in range(4):
                    near = [(t, 0 if t == 0 else 2 if t == tiles - 1 else 1)]
                    near += [(t - 1, 3)] * (t > 0) + [(t + 1, 4)] * (t < tiles - 1)
                    o = QK * (g % 2)
                    for q, (src, kind) in enumerate(near):
                        mm = pe.matmul(pp[o:o + QK, t % 2, (g // 2) * P:(g // 2 + 1) * P],
                                       ab[:, src, FW + g * QK:FW + (g + 1) * QK], band[:, kind, g, :],
                                       start=(q == 0), stop=(q == len(near) - 1))
                mm.then_inc(s_p, 1)
            pe.wait_ge(s_gc, 1)
            pe.wait_ge(s_wp, 1)
            pe.wait_ge(s_yc, 2 * len(order))
            for t in range(tiles):
                pe.wait_ge(s_pc, t + 1)
                if t >= 2:
                    pe.wait_ge(s_oc, t - 1)
                for c in range(2):
                    for g in range(2):
                        pe.matmul(po[:, t % 2, c * P:(c + 1) * P], yt[:, g, c, t * P:(t + 1) * P], G[:, g, c, :],
                                  start=(g == 0), stop=(g == 1))
                for c in range(2):
                    mm = pe.matmul(po[:, t % 2, FW + c * P:FW + (c + 1) * P], pool[:, c, t * P:(t + 1) * P],
                                   wpb[:, c, :], start=True, stop=True)
                mm.then_inc(s_o, 1)

        @block.scalar
        def _(act):
            for q, (h, g) in enumerate(order):
                for c in range(2):
                    act.wait_ge(s_y, 2 * q + c + 1)
                    act.copy(yt[:, g, c, h * N:(h + 1) * N], py[:, c, 0:N]).then_inc(s_yc, 1)

        @block.vector
        def _(dve):
            dve.wait_ge(s_tab, 48)
            dve.wait_ge(s_wd, 16 * 8)
            dve.tensor_tensor(wpb[:], wpb[:], psc[:], ALU.mult).then_inc(s_wp, 1)
            dve.wait_ge(s_g, 1)
            dve.tensor_copy(G[:], pg[:]).then_inc(s_gc, 1)
            for t in range(tiles):
                dve.wait_ge(s_p, t + 1)
                dve.tensor_copy(pool[:, :, t * P:(t + 1) * P],
                                pp[:, t % 2, 0:2 * P].rearrange("p (c n) -> p c n", c=2)).then_inc(s_pc, 1)
            for t in range(tiles):
                dve.wait_ge(s_o, t + 1)
                dve.tensor_copy(C.mix[:, r0 // P + t, 0:2 * FW], po[:, t % 2, :]).then_inc(s_oc, 1)


def qk_prepare(C, l):
    nc, ins = C.nc, C.ins
    NG = 16
    with ExitStack() as st:
        sb = lambda n, s: st.enter_context(nc.sbuf_tensor(f"q{l}_{n}", s, F32))
        sem = lambda n: nc.alloc_semaphore(f"q{l}_{n}")
        raw = sb("raw", [P, 2, 2 * 512])
        sq = sb("sq", [P, 2, 2 * 512])
        st1 = sb("st1", [P, 2, NG])
        rs = sb("rs", [P, 2, NG])
        nrm = sb("nrm", [P, 2, 2 * 512])
        t1 = sb("t1", [P, 2 * 512])
        gq = sb("gq", [P, 2, QK])
        cs = sb("cs", [P, 2, NT, QK])
        pt = st.enter_context(nc.psum_tensor(f"q{l}_pt", [P, 2, 8, P], F32))
        s_v = sem("v_loaded")
        s_tab = sem("tables_loaded")
        s_raw = [sem(f"qk_loaded{b}") for b in range(2)]
        s_ms = sem("sums_ready")
        s_rs = sem("rs_ready")
        s_n = sem("normed")
        s_T = sem("transposed")
        s_eA = sem("q_taken")
        s_eD = sem("k_taken")
        block = st.enter_context(nc.Block())

        def src(n):
            return C.p_dram[ds(n * P, P), Q0:V0]

        @block.sync
        def _(sp):
            sp.dma_start(gq[:].rearrange("p a b -> p (a b)"),
                         ins["qk_norm_g"][l].rearrange("a b -> (a b)").partition_broadcast(P)).then_inc(s_tab, 16)
            for q in range(2):
                sp.dma_start(cs[:, q], ins["t_rope"][q].rearrange("(t p) n -> p t n", p=P)).then_inc(s_tab, 16)
            for b in range(2):
                sp.dma_start(raw[:, b, :], src(b)).then_inc(s_raw[b], 16)
            with sp.Fori(1, NT // 2) as i:
                for b in range(2):
                    sp.wait_ge(s_n, 2 * i + b - 1)
                    sp.dma_start(raw[:, b, :], src(2 * i + b)).then_inc(s_raw[b], 16)
            for b in range(2):
                sp.wait_ge(s_n, NT - 1 + b)
                if l < DEPTH - 1:
                    sp.dma_start(raw[:, b, :], src(NT + b)).then_inc(s_raw[b], 16)
                else:
                    sp.dma_start(raw[:, b, 512:1024], C.p_dram[(NT + b) * P:(NT + b + 1) * P, K0:V0]).then_inc(s_raw[b], 16)
            sp.dma_start(C.v_sb[:], C.p_dram[:, V0:G0].rearrange("(t p) n -> p t n", p=P)).then_inc(s_v, 16)
            sp.wait_ge(s_v, 16)

        def cols(ctx_tile):
            return (512, 1024) if ctx_tile and l == DEPTH - 1 else (0, 1024)

        @block.scalar
        def _(act):
            act.sem_inc(s_eA, 2)

            def take_q(n, b, ctx_tile):
                act.wait_ge(s_T, n + 3)
                if cols(ctx_tile)[0] == 0:
                    e = act.copy(C.qT[:, :, ds(n * P, P)], pt[:, b, 0:4, :])
                    e.then_inc(s_eA, 1)
                else:
                    act.drain()
                    act.sem_inc(s_eA, 1)

            with act.Fori(0, NT // 2) as i:
                for b in range(2):
                    take_q(2 * i + b, b, False)
            for b in range(2):
                take_q(NT + b, b, True)

        @block.gpsimd
        def _(pool):
            def roots(n, b, ctx_tile):
                a, z = cols(ctx_tile)
                pool.wait_ge(s_ms, n + 1)
                inverse_root(C, pool, rs[:, b, a // QK:z // QK], st1[:, b, a // QK:z // QK], QK).then_inc(s_rs, 1)

            with pool.Fori(0, NT // 2) as i:
                for b in range(2):
                    roots(2 * i + b, b, False)
            for b in range(2):
                roots(NT + b, b, True)

        @block.vector
        def _(dve):
            dve.sem_inc(s_eD, 2)
            dve.wait_ge(s_tab, 48)

            def tile_stats(n, b, load, ctx_tile):
                a, z = cols(ctx_tile)
                dve.wait_ge(s_raw[b], load)
                dve.tensor_tensor(sq[:, b, a:z], raw[:, b, a:z], raw[:, b, a:z], ALU.mult)
                dve.drain()
                dve.tensor_reduce(st1[:, b, a // QK:z // QK], sq[:, b, a:z].rearrange("p (g n) -> p g n", n=QK), AX.X,
                                  ALU.add).then_inc(s_ms, 1)

            def tile_norm(n, b, ctx_tile):
                a, z = cols(ctx_tile)
                ng = (z - a) // QK
                dve.wait_ge(s_rs, n + 1)
                dve.wait_ge(s_T, n + 1)
                out = nrm[:, b, a:z].rearrange("p (g n) -> p g n", n=QK)
                dve.tensor_tensor(out, raw[:, b, a:z].rearrange("p (g n) -> p g n", n=QK),
                                  rs[:, b, a // QK:z // QK].unsqueeze(2).to_broadcast([P, ng, QK]), ALU.mult)
                dve.drain()
                for w in range(a // 512, 2):
                    o = nrm[:, b, w * 512:(w + 1) * 512].rearrange("p (g n) -> p g n", n=QK)
                    e = dve.tensor_tensor(o, o, gq[:, w, :].unsqueeze(1).to_broadcast([P, 8, QK]), ALU.mult)
                if ctx_tile:
                    e.then_inc(s_n, 1)
                    return
                dve.drain()
                v = nrm[:, b, :].rearrange("p (g a h n) -> p g a h n", a=2, h=2, n=16)
                r = t1[:].rearrange("p (g a h n) -> p g a h n", a=2, h=2, n=16)
                for ax in range(2):
                    for h in range(2):
                        sine = cs[:, 1, ds(n, 1), :].rearrange("p t (a h n) -> p (t a) h n", a=2, h=2)[:, ax, h, :]
                        dve.tensor_tensor(r[:, :, ax, h, :], v[:, :, ax, 1 - h, :],
                                          sine.unsqueeze(1).to_broadcast([P, NG, 16]), ALU.mult)
                dve.drain()
                cosine = cs[:, 0, ds(n, 1), :].rearrange("p t n -> p (t n)")
                dve.tensor_tensor(out, out, cosine.unsqueeze(1).to_broadcast([P, NG, QK]), ALU.mult)
                dve.drain()
                dve.tensor_tensor(nrm[:, b, :], nrm[:, b, :], t1[:], ALU.add).then_inc(s_n, 1)

            def take_k(n, b):
                dve.wait_ge(s_T, n + 3)
                dve.tensor_copy(C.kT[:, :, ds(n * P, P)], pt[:, b, 4:8, :]).then_inc(s_eD, 1)

            with dve.Fori(0, NT // 2) as i:
                for b in range(2):
                    tile_stats(2 * i + b, b, 16 * i + 16, False)
                for b in range(2):
                    tile_norm(2 * i + b, b, False)
                for b in range(2):
                    take_k(2 * i + b, b)
            for b in range(2):
                tile_stats(NT + b, b, 16 * (NT // 2) + 16, True)
            for b in range(2):
                tile_norm(NT + b, b, True)
            for b in range(2):
                take_k(NT + b, b)

        @block.tensor
        def _(pe):
            pe.sem_inc(s_T, 2)

            def turn(n, b, ctx_tile):
                pe.wait_ge(s_n, n + 1)
                pe.wait_ge(s_eA, n + 1)
                pe.wait_ge(s_eD, n + 1)
                for c in range(cols(ctx_tile)[0] // P, 8):
                    mm = pe.transpose(pt[:, b, c, :], nrm[:, b, c * P:(c + 1) * P], C.ident[:])
                mm.then_inc(s_T, 1)

            with pe.Fori(0, NT // 2) as i:
                for b in range(2):
                    turn(2 * i + b, b, False)
            for b in range(2):
                turn(NT + b, b, True)


def attention(C, l):
    nc = C.nc
    SCALE = QK ** -0.5
    segs = [(NT, 0, 0, SEQ + CTX)] + ([(NTC, NT, SEQ, CTX)] if l < DEPTH - 1 else [])
    with ExitStack() as st:
        sb = lambda n, s: st.enter_context(nc.sbuf_tensor(f"a{l}_{n}", s, F32))
        sem = lambda n: nc.alloc_semaphore(f"a{l}_{n}")
        qs = sb("qs", [P, 2, P])
        pr = sb("pr", [P, 2, 2, SEQ + CTX])
        df = sb("df", [P, SEQ + CTX])
        pT = sb("pT", [P, NTA, P])
        mx = sb("mx", [P, 2, 4])
        nb = sb("nb", [P, 2, 2])
        sm = sb("sm", [P, 2, 2])
        ri = sb("ri", [P, 2, 4])
        sc = st.enter_context(nc.psum_tensor(f"a{l}_sc", [P, 2, 3, CH], F32))
        tp = st.enter_context(nc.psum_tensor(f"a{l}_tp", [P, 2, CH], F32))
        s_q = sem("query_staged")
        s_s = sem("scores_done")
        s_m = sem("max_ready")
        s_e = sem("exp_done")
        s_d = sem("difference_ready")
        s_t = sem("probs_transposed")
        s_tc = sem("transposed_taken")
        s_o = sem("pv_done")
        s_oc = sem("pv_taken")
        block = st.enter_context(nc.Block())

        bases, tot = [], 0
        for m, *_ in segs:
            bases.append(tot)
            tot += HEADS * m

        def walk(eng, before, lead, after):
            for (m, *seg), base in zip(segs, bases):
                for h in range(HEADS):
                    n0 = base + m * h
                    lead(n0, h, 0, 0, *seg)
                    if m > 2:
                        with eng.Fori(0, (m - 2) // 2) as i:
                            for b in range(2):
                                t = 2 * i + b
                                before(n0 + t, h, t, b, *seg)
                                lead(n0 + t + 1, h, t + 1, 1 - b, *seg)
                                after(n0 + t, h, t, b, *seg)
                    before(n0 + m - 2, h, m - 2, 0, *seg)
                    lead(n0 + m - 1, h, m - 1, 1, *seg)
                    after(n0 + m - 2, h, m - 2, 0, *seg)
                    before(n0 + m - 1, h, m - 1, 1, *seg)
                    after(n0 + m - 1, h, m - 1, 1, *seg)

        nothing = lambda *a: None

        def batches(nk):
            tiles = list(range(nk // P))
            return [tiles[i:i + 4] for i in range(0, len(tiles), 4)]

        nbt = [len(batches(s[3])) for s in segs]
        t_base = [0, HEADS * segs[0][0] * nbt[0]]

        def tn(n, base_index, q):
            base, per = bases[base_index], nbt[base_index]
            return t_base[base_index] + (n - base) * per + q

        def seg_of(t0):
            return [s[1] for s in segs].index(t0)

        @block.gpsimd
        def _(pool):
            def stage(n, h, t, b, t0, k0, nk):
                pool.wait_ge(s_s, 2 * n + 2)
                pool.tensor_copy(qs[:, b, :], C.qT[:, h, ds((t0 + t) * P, P)]).then_inc(s_q, 1)
            walk(pool, nothing, stage, nothing)

        @block.tensor
        def _(pe):
            pe.sem_inc(s_s, 4)

            def scores(n, h, t, b, t0, k0, nk):
                pe.wait_ge(s_q, n + 1)
                for m in range(2):
                    pe.wait_ge(s_e, 2 * n + m + 1)
                    for j, c in enumerate(range(0, nk, CH)):
                        w = min(CH, nk - c)
                        mm = pe.matmul(sc[:, m, j, 0:w], qs[m * QK:(m + 1) * QK, b, :],
                                       C.kT[m * QK:(m + 1) * QK, h, k0 + c:k0 + c + w], start=True, stop=True)
                    mm.then_inc(s_s, 1)

            def rest(n, h, t, b, t0, k0, nk):
                g = seg_of(t0)
                pe.wait_ge(s_d, n + 3)
                for q, tiles in enumerate(batches(nk)):
                    if q == 1 or nbt[g] == 1:
                        pe.wait_ge(s_oc, n + 1)
                    if q == 2:
                        pe.wait_ge(s_tc, tn(n, g, 1))
                    for k in tiles:
                        mm = pe.transpose(tp[:, q % 2, (k % 4) * P:(k % 4 + 1) * P], df[:, k * P:(k + 1) * P], C.ident[:])
                    mm.then_inc(s_t, 1)
                pe.wait_ge(s_tc, tn(n, g, nbt[g]))
                for k in range(nk // P):
                    mm = pe.matmul(tp[:, 1, 0:P], pT[:, k, :], C.v_sb[:, k0 // P + k, h * DV:(h + 1) * DV],
                                   start=(k == 0), stop=(k == nk // P - 1))
                mm.then_inc(s_o, 1)
            walk(pe, nothing, scores, rest)

        @block.scalar
        def _(act):
            act.sem_inc(s_e, 2)

            def exps(n, h, t, b, t0, k0, nk):
                act.wait_ge(s_d, n + 1)
                for m in range(2):
                    act.wait_ge(s_m, 2 * n + m + 1)
                    act.activation(pr[:, b, m, 0:nk], sc[:, m].rearrange("p a b -> p (a b)")[:, 0:nk], ACT.Exp,
                                   bias=nb[:, b, m:m + 1], scale=SCALE, accum_out=sm[:, b, m:m + 1]).then_inc(s_e, 1)

            def rest(n, h, t, b, t0, k0, nk):
                g = seg_of(t0)
                for q, tiles in enumerate(batches(nk)):
                    act.wait_ge(s_t, tn(n, g, q) + 1)
                    act.copy(pT[:, tiles[0]:tiles[-1] + 1, :].rearrange("p a b -> p (a b)"),
                             tp[:, q % 2, 0:len(tiles) * P]).then_inc(s_tc, 1)
            walk(act, rest, exps, nothing)

        @block.vector
        def _(dve):
            dve.sem_inc(s_oc, 1)
            dve.sem_inc(s_d, 2)

            def maxima(n, h, t, b, t0, k0, nk):
                for m in range(2):
                    dve.wait_ge(s_s, 2 * n + m + 5)
                    dve.tensor_reduce(mx[:, b, m:m + 1], sc[:, m].rearrange("p a b -> p (a b)")[:, 0:nk], AX.X, ALU.max)
                    dve.drain()
                    dve.tensor_scalar(nb[:, b, m:m + 1], mx[:, b, m:m + 1], -SCALE, None, ALU.mult).then_inc(s_m, 1)

            def combine(n, h, t, b, t0, k0, nk):
                dve.wait_ge(s_e, 2 * n + 4)
                dve.reciprocal(ri[:, b, 0:2], sm[:, b, 0:2])
                dve.drain()
                dve.scalar_tensor_tensor(ri[:, b, 2:3], ri[:, b, 1:2], sm[:, b, 0:1], C.neglam[:], ALU.mult, ALU.mult)
                dve.drain()
                dve.scalar_tensor_tensor(df[:, 0:nk], pr[:, b, 1, 0:nk], ri[:, b, 2:3], pr[:, b, 0, 0:nk],
                                         ALU.mult, ALU.add).then_inc(s_d, 1)

            def take(n, h, t, b, t0, k0, nk):
                dve.wait_ge(s_o, n + 1)
                dve.tensor_scalar(C.mix[:, ds(t0 + t, 1), 2 * FW + h * DV:2 * FW + (h + 1) * DV].rearrange("p t n -> p (t n)"),
                                  tp[:, 1, 0:P], ri[:, b, 0:1], None, ALU.mult).then_inc(s_oc, 1)
            walk(dve, combine, maxima, take)


def mix_out(C, l):
    nc, ins = C.nc, C.ins
    lam_init = 0.8 - 0.6 * math.exp(-0.3 * l)
    segs = [(NT, 0, 0)] + ([(NTC, NT, 1)] if l < DEPTH - 1 else [])
    tiles = sum(m for m, *_ in segs)
    with ExitStack() as st:
        sb = lambda n, s: st.enter_context(nc.sbuf_tensor(f"o{l}_{n}", s, F32))
        sem = lambda n: nc.alloc_semaphore(f"o{l}_{n}")
        w = sb("w", [P, KD, D])
        g = sb("g", [P, 2, D])
        sg = sb("sg", [P, 2, D])
        sq = sb("sq", [P, 2, 512])
        ms = sb("ms", [P, 2, HEADS])
        rs = sb("rs", [P, 2, HEADS])
        sub = sb("sub", [P, DV])
        y = sb("y", [P, 2, D])
        yT = sb("yT", [P, 2, KD, P])
        up = sb("up", [P, 2, D])
        pt = st.enter_context(nc.psum_tensor(f"o{l}_pt", [P, KD, P], F32))
        po = st.enter_context(nc.psum_tensor(f"o{l}_po", [P, 2, 2, CH], F32))
        s_w = sem("w_loaded")
        s_sub = sem("subln_loaded")
        s_g = [sem(f"gate_loaded{b}") for b in range(2)]
        s_sg = sem("silu_ready")
        s_ms = sem("head_sums")
        s_rs = sem("head_rs")
        s_y = sem("y_ready")
        s_T = sem("y_transposed")
        s_cA = sem("yT_taken_act")
        s_cD = sem("yT_taken_dve")
        s_o = sem("product_done")
        s_x = sem("x_updated")
        block = st.enter_context(nc.Block())

        @block.sync
        def _(sp):
            def load(n, b):
                sp.dma_start(g[:, b, :], C.p_dram[ds(n * P, P), G0:INW]).then_inc(s_g[b], 16)
            sp.dma_start(sub[:], ins["subln_g"][l].partition_broadcast(P)).then_inc(s_sub, 16)
            for b in range(2):
                load(b, b)
            sp.dma_start(w[:], ins["w_out"][l].rearrange("(k p) n -> p k n", p=P)).then_inc(s_w, 16)
            with sp.Fori(1, tiles // 2) as i:
                for b in range(2):
                    sp.wait_ge(s_sg, 2 * i + b - 1)
                    load(2 * i + b, b)

        @block.scalar
        def _(act):
            act.sem_inc(s_cA, 1)
            for m, t0, r in segs:
                with act.Fori(t0 // 2, (t0 + m) // 2) as i:
                    for b in range(2):
                        act.wait_ge(s_g[b], 16 * i + 16)
                        act.wait_ge(s_y, 2 * i + b + 1)
                        act.activation(sg[:, b, :], g[:, b, :], ACT.Silu).then_inc(s_sg, 1)
                    for b in range(2):
                        act.wait_ge(s_T, 2 * i + b + 3)
                        act.wait_ge(s_o, 2 * i + b + 1)
                        act.copy(yT[:, b, 0:4, :], pt[:, 0:4, :]).then_inc(s_cA, 1)

        @block.gpsimd
        def _(pool):
            with pool.Fori(0, tiles // 2) as i:
                for b in range(2):
                    pool.wait_ge(s_ms, 2 * i + b + 1)
                    inverse_root(C, pool, rs[:, b, :], ms[:, b, :], DV).then_inc(s_rs, 1)

        @block.vector
        def _(dve):
            dve.sem_inc(s_y, 2)
            dve.sem_inc(s_cD, 1)
            dve.sem_inc(s_x, 2)
            dve.wait_ge(s_sub, 16)
            dve.tensor_scalar(sub[:], sub[:], 1.0 - lam_init, None, ALU.mult)
            dve.drain()
            for m, t0, r in segs:
                with dve.Fori(t0 // 2, (t0 + m) // 2) as i:
                    for b in range(2):
                        o = C.mix[:, ds(2 * i + b, 1), 2 * FW:D].rearrange("p t n -> p (t n)")
                        dve.tensor_tensor(sq[:, b], o, o, ALU.mult)
                        dve.drain()
                        dve.tensor_reduce(ms[:, b, :], sq[:, b].rearrange("p (h n) -> p h n", h=HEADS), AX.X, ALU.add).then_inc(s_ms, 1)
                    for b in range(2):
                        dve.wait_ge(s_sg, 2 * i + b + 1)
                        dve.wait_ge(s_T, 2 * i + b + 1)
                        f = C.mix[:, ds(2 * i + b, 1), 0:2 * FW].rearrange("p t n -> p (t n)")
                        o = C.mix[:, ds(2 * i + b, 1), 2 * FW:D].rearrange("p t n -> p (t n)")
                        dve.tensor_tensor(y[:, b, 0:2 * FW], f, sg[:, b, 0:2 * FW], ALU.mult)
                        s = sg[:, b, 2 * FW:D].rearrange("p (h n) -> p h n", h=HEADS)
                        dve.tensor_tensor(s, s, sub[:].unsqueeze(1).to_broadcast([P, HEADS, DV]), ALU.mult)
                        dve.drain()
                        dve.wait_ge(s_rs, 2 * i + b + 1)
                        for h in range(HEADS):
                            e = dve.scalar_tensor_tensor(y[:, b, 2 * FW + h * DV:2 * FW + (h + 1) * DV],
                                                         o[:, h * DV:(h + 1) * DV], rs[:, b, h:h + 1],
                                                         sg[:, b, 2 * FW + h * DV:2 * FW + (h + 1) * DV], ALU.mult, ALU.mult)
                        e.then_inc(s_y, 1)
                    for b in range(2):
                        dve.wait_ge(s_T, 2 * i + b + 3)
                        dve.wait_ge(s_o, 2 * i + b + 1)
                        dve.tensor_copy(yT[:, b, 4:8, :], pt[:, 4:8, :]).then_inc(s_cD, 1)
                    for b in range(2):
                        dve.wait_ge(s_o, 2 * i + b + 3)
                        for h in range(2):
                            dve.tensor_tensor(up[:, b, h * CH:(h + 1) * CH], po[:, b, h, :],
                                              C.gate[:, r, h * CH:(h + 1) * CH], ALU.mult)
                        dve.drain()
                        x = C.x_sb[:, ds(2 * i + b, 1), :].rearrange("p t n -> p (t n)")
                        dve.tensor_tensor(x, x, up[:, b, :], ALU.add).then_inc(s_x, 1)

        @block.tensor
        def _(pe):
            pe.sem_inc(s_o, 2)
            pe.sem_inc(s_T, 2)
            pe.wait_ge(s_w, 16)
            for m, t0, r in segs:
                with pe.Fori(t0 // 2, (t0 + m) // 2) as i:
                    for b in range(2):
                        pe.wait_ge(s_y, 2 * i + b + 3)
                        pe.wait_ge(s_cA, 2 * i + b + 1)
                        pe.wait_ge(s_cD, 2 * i + b + 1)
                        for k in range(KD):
                            mm = pe.transpose(pt[:, k, :], y[:, b, k * P:(k + 1) * P], C.ident[:])
                        mm.then_inc(s_T, 1)
                    for b in range(2):
                        pe.wait_ge(s_cA, 2 * i + b + 2)
                        pe.wait_ge(s_cD, 2 * i + b + 2)
                        pe.wait_ge(s_x, 2 * i + b + 1)
                        for h in range(2):
                            for k in range(KD):
                                mm = pe.matmul(po[:, b, h, :], yT[:, b, k, :], w[:, k, h * CH:(h + 1) * CH],
                                               start=(k == 0), stop=(k == KD - 1))
                        mm.then_inc(s_o, 1)


A_Q, A_F, A_I, A_G = 0, 1024, 2048, 3072
B_Q, B_K, B_V, B_GK, B_G = 4096, 4608, 5120, 6144, 6160
C_QKV, C_A, C_G, MERGE, N_IN = 7184, 10256, 10272, 11296, 14368
RANK = 16
T_AQ, T_AF, T_BQ, T_BK, T_C = 0, 1024, 2048, 2560, 3072
N_AI, N_AG, N_BV, N_BG, N_CG, N_M = 0, 1024, 2048, 3072, 4096, 5120


def load_norm_gain(C, tag, gain):
    nc = C.nc
    with ExitStack() as st:
        s_in = nc.alloc_semaphore(f"{tag}_in")
        block = st.enter_context(nc.Block())

        @block.sync
        def _(sp):
            with nc.allow_non_contiguous_dma("4 KB of channel gains"):
                sp.dma_start(C.scale[:, 0, :], gain.rearrange("(k p) -> p k", p=P)).then_inc(s_in, 16)
            sp.wait_ge(s_in, 16)

        @block.gpsimd
        def _(pool):
            pool.memset(C.shift[:], 0.0)


def small_projections(C):
    nc, ins = C.nc, C.ins
    BH = B_HEADS
    with ExitStack() as st:
        sb = lambda n, s: st.enter_context(nc.sbuf_tensor(f"s_{n}", s, F32))
        sem = lambda n: nc.alloc_semaphore(f"s_{n}")
        w = sb("w", [P, 2, KD, RANK])
        wh = st.enter_context(nc.sbuf_tensor("s_wh", [P, 2, KD, RANK], F32R))
        wl = st.enter_context(nc.sbuf_tensor("s_wl", [P, 2, KD, RANK], F32R))
        wg = sb("wg", [RANK, BH * P])
        bg = sb("bg", [P, BH])
        low = sb("low", [RANK, 2, SEQ])
        pl = st.enter_context(nc.psum_tensor("s_pl", [P, 4, CH], F32))
        pc = st.enter_context(nc.psum_tensor("s_pc", [P, NT, 2 * C_HEADS], F32))
        pg = st.enter_context(nc.psum_tensor("s_pg", [P, 2, CH], F32))
        s_in = sem("loaded")
        s_wh = sem("hi_ready")
        s_wl = sem("lo_ready")
        s_l = sem("low_done")
        s_lc = sem("low_ready")
        s_c = sem("ab_done")
        s_g = sem("logits_done")
        s_gc = sem("logits_taken")
        block = st.enter_context(nc.Block())
        wv = ins["w_in_2"][0].rearrange("(k p) n -> p k n", p=P)

        @block.sync
        def _(sp):
            with nc.allow_non_contiguous_dma("64-byte rows, 128 KB in all"):
                sp.dma_start(w[:, 0], wv[:, :, B_GK:B_GK + RANK]).then_inc(s_in, 16)
                sp.dma_start(w[:, 1], wv[:, :, C_A:C_A + 2 * C_HEADS]).then_inc(s_in, 16)
                sp.dma_start(bg[:], ins["gla_b_gk_2"][0].rearrange("(h p) -> p h", p=P)).then_inc(s_in, 16)
            sp.dma_start(wg[:], ins["gla_w_gk_2"][0]).then_inc(s_in, 16)

        @block.scalar
        def _(act):
            act.wait_ge(s_in, 64)
            act.copy(wh[:], w[:]).then_inc(s_wh, 1)

        @block.tensor
        def _(pe):
            pe.wait_ge(s_wl, 1)
            for j in range(2):
                for h in range(2):
                    for k in range(KD):
                        for q, (a, x) in enumerate(((wh, C.hi), (wh, C.lo), (wl, C.hi))):
                            mm = pe.matmul(pl[0:RANK, 2 * j + h, :], a[:, j, k, :], x[:, k, h * CH:(h + 1) * CH],
                                           start=(k == 0 and q == 0), stop=(k == KD - 1 and q == 2))
            mm.then_inc(s_l, 1)
            pe.wait_ge(s_lc, 1)
            for t in range(NT):
                mm = pe.transpose(pc[:, t, :], low[:, 1, t * P:(t + 1) * P], C.ident[0:RANK, 0:RANK])
            mm.then_inc(s_c, 1)
            for c in range(BH):
                for h in range(2):
                    if c > 0:
                        pe.wait_ge(s_gc, 2 * (c - 1) + h + 1)
                    pe.matmul(pg[:, h, :], wg[:, c * P:(c + 1) * P], low[:, 0, h * CH:(h + 1) * CH],
                              start=True, stop=True).then_inc(s_g, 1)

        @block.vector
        def _(dve):
            dve.wait_ge(s_wh, 1)
            dve.tensor_tensor(wl[:], w[:], wh[:], ALU.subtract).then_inc(s_wl, 1)
            dve.wait_ge(s_l, 1)
            dve.tensor_copy(low[:].rearrange("p j t -> p (j t)"), pl[0:RANK].rearrange("p a b -> p (a b)")).then_inc(s_lc, 1)
            dve.wait_ge(s_c, 1)
            dve.tensor_copy(C.ab[:], pc[:])
            for c in range(BH):
                for h in range(2):
                    dve.wait_ge(s_g, 2 * c + h + 1)
                    dve.tensor_scalar(C.gk[:, c, h * CH:(h + 1) * CH], pg[:, h, :], bg[:, c:c + 1], None,
                                      ALU.add).then_inc(s_gc, 1)


def gated_linear(C, branch):
    nc, ins = C.nc, C.ins
    A = branch == "a"
    H, dv = (A_HEADS, D // A_HEADS) if A else (B_HEADS, D // B_HEADS)
    GS = 1.0 if A else 1.0 / 16.0
    L2 = LEVELS + 2
    tag = f"g{branch}"
    with ExitStack() as st:
        sb = lambda n, s: st.enter_context(nc.sbuf_tensor(f"{tag}_{n}", s, F32))
        sem = lambda n: nc.alloc_semaphore(f"{tag}_{n}")
        z = sb("z", [P, 2, SEQ]) if A else None
        q = sb("q", [P, 2, SEQ])
        k = sb("k", [P, 2, SEQ])
        v = sb("v", [P, 2, NCK, dv])
        lt = sb("lt", [P, 2, SEQ])
        bb = sb("bb", [P, 2, SEQ])
        X = sb("X", [P, 2, L2, SEQ])
        el = sb("el", [P, 2, NCK])
        masks = sb("masks", [P, LEVELS + 1, CK])
        restart = sb("restart", [P, SEQ])
        am = sb("am", [P, 2, LEVELS + 1, CK])
        AT = sb("AT", [P, 2, CK])
        kd = sb("kd", [P, 2, CK])
        S = sb("S", [P, 2, dv])
        o = sb("o", [P, 2, dv])
        pa = st.enter_context(nc.psum_tensor(f"{tag}_pa", [P, 2, LEVELS + 1, CK], F32))
        pk = st.enter_context(nc.psum_tensor(f"{tag}_pk", [P, CH], F32))
        po = st.enter_context(nc.psum_tensor(f"{tag}_po", [P, 2, CH], F32))
        pS = st.enter_context(nc.psum_tensor(f"{tag}_pS", [P, CH], F32))
        s_tab = sem("tables_loaded")
        s_in = [sem(f"head_loaded{b}") for b in range(2)]
        s_ln = sem("log_term_ready")
        s_kz = sem("k_logits_ready")
        s_b = sem("b_ready")
        s_qk = sem("q_and_k_ready")
        s_sub = sem("exponents_ready")
        s_exp = sem("exps_ready")
        s_X = sem("X_ready")
        s_A = sem("level_products_done")
        s_At = sem("A_ready")
        s_kT = sem("k_transposed")
        s_kc = sem("k_taken")
        s_o = sem("o_done")
        s_oc = sem("o_taken")
        s_S = sem("state_product_done")
        s_Sc = sem("state_ready")
        s_st = [sem(f"o_stored{b}") for b in range(2)]
        block = st.enter_context(nc.Block())
        q0 = T_AQ if A else T_BQ
        v0 = N_AI if A else N_BV
        o_dram = C.o_dram[0 if A else 1]

        def heads(eng, prepare, chunk, steps):
            for s in range(steps):
                prepare(0, 0, s, 1)

            def one(n, b, more, use):
                for c in range(NCK):
                    chunk(n, b, c, c < NCK - 1)
                    if more:
                        for s in range(c * steps // NCK, (c + 1) * steps // NCK):
                            prepare(n + 1, 1 - b, s, use)

            with eng.Fori(0, H // 2 - 1) as i:
                one(2 * i, 0, True, i + 1)
                one(2 * i + 1, 1, True, i + 2)
            one(H - 2, 0, True, H // 2)
            one(H - 1, 1, False, None)

        @block.sync
        def _(sp):
            sp.dma_start(masks[:], ins["t_levels"]).then_inc(s_tab, 16)
            sp.dma_start(restart[:], ins["t_restart"]).then_inc(s_tab, 16)

            def load(n, b):
                sp.dma_start(q[:, b, :], C.pt_dram[ds(q0 + n * P, P), :]).then_inc(s_in[b], 16)
                if A:
                    sp.dma_start(z[:, b, :], C.pt_dram[ds(T_AF + n * P, P), :]).then_inc(s_in[b], 16)
                else:
                    sp.dma_start(k[:, b, :], C.pt_dram[ds(T_BK + n * P, P), :]).then_inc(s_in[b], 16)
                sp.dma_start(v[:, b], C.pn_dram[:, ds(v0 + n * dv, dv)].rearrange("(c p) n -> p c n", p=P)).then_inc(s_in[b], 16)

            def store(n, c):
                sp.wait_ge(s_oc, NCK * n + c + 3)
                sp.dma_start(o_dram[c * P:(c + 1) * P, ds(n * dv, dv)], o[:, c % 2, :]).then_inc(s_st[c % 2], 16)

            for b in range(2):
                load(b, b)
            for b in range(2):
                sp.sem_inc(s_st[b], 16)

            def one(n, b, more):
                for c in range(NCK):
                    store(n, c)
                if more:
                    load(n + 2, b)
            with sp.Fori(0, H // 2 - 1) as i:
                for b in range(2):
                    one(2 * i + b, b, True)
            one(H - 2, 0, False)
            one(H - 1, 1, False)
            for b in range(2):
                sp.wait_ge(s_st[b], 16 * (H * NCK // 2 + 1))

        @block.scalar
        def _(act):
            act.sem_inc(s_kc, 1)
            act.sem_inc(s_oc, 2)

            def exps(n, b, lev, order):
                act.wait_ge(s_sub, (L2 - 1) * n + order)
                act.activation(X[:, b, lev], X[:, b, lev], ACT.Exp, scale=GS).then_inc(s_exp, 1)

            def prepare(n, b, s, use):
                if s == 0:
                    act.wait_ge(s_in[b], 48 * use)
                    act.activation(lt[:, b], z[:, b] if A else C.gk[:, ds(n, 1), :].rearrange("p h t -> p (h t)"), ACT.Abs)
                    act.drain()
                    act.activation(lt[:, b], lt[:, b], ACT.Exp, scale=-1.0)
                    act.drain()
                    act.activation(lt[:, b], lt[:, b], ACT.Ln, bias=1.0).then_inc(s_ln, 1)
                elif s == 1:
                    if A:
                        act.wait_ge(s_kz, n + 1)
                        act.activation(k[:, b], k[:, b], ACT.Exp)
                        act.activation(q[:, b], q[:, b], ACT.Silu).then_inc(s_qk, 1)
                    else:
                        act.mul(q[:, b], q[:, b], float(P) ** -0.5).then_inc(s_qk, 1)
                elif s == 2:
                    act.wait_ge(s_b, n + 1)
                    act.activation(el[:, b], bb[:, b].rearrange("p (c t) -> p c t", c=NCK)[:, :, CK - 1], ACT.Exp, scale=GS)
                    act.activation(X[:, b, LEVELS], bb[:, b], ACT.Exp, scale=GS).then_inc(s_exp, 1)
                elif s == 3:
                    exps(n, b, LEVELS + 1, 1)
                else:
                    exps(n, b, s - 4, s - 2)

            def chunk(n, b, c, more):
                m = NCK * n + c
                act.wait_ge(s_kT, m + 1)
                act.copy(kd[:, c % 2], pk[:, 0:CK]).then_inc(s_kc, 1)
                act.wait_ge(s_o, m + 3)
                act.wait_ge(s_st[c % 2], 16 * ((NCK // 2) * n + c // 2 + 1))
                act.copy(o[:, c % 2], po[:, c % 2, 0:dv]).then_inc(s_oc, 1)
            heads(act, prepare, chunk, 4 + LEVELS)

        @block.vector
        def _(dve):
            dve.sem_inc(s_At, 2)
            dve.sem_inc(s_Sc, 1)
            dve.wait_ge(s_tab, 32)

            def blocks(ap, lev):
                s = 1 << lev
                return ap.rearrange("p (n a s) -> p n a s", a=2, s=s)

            def prepare(n, b, s, use):
                zs = z[:, b] if A else C.gk[:, ds(n, 1), :].rearrange("p h t -> p (h t)")
                if s == 0:
                    dve.wait_ge(s_ln, n + 1)
                    dve.scalar_tensor_tensor(lt[:, b], zs, 0.0, lt[:, b], ALU.min, ALU.subtract)
                    dve.drain()
                    if A:
                        dve.tensor_tensor(k[:, b], lt[:, b], z[:, b], ALU.subtract).then_inc(s_kz, 1)
                    dve.tensor_tensor_scan(bb[:, b], restart[:], lt[:, b], 0.0, ALU.mult, ALU.add).then_inc(s_b, 1)
                    dve.drain()
                elif s == 1:
                    t = bb[:, b].rearrange("p (c t) -> p c t", c=NCK)
                    dve.tensor_tensor(X[:, b, LEVELS + 1].rearrange("p (c t) -> p c t", c=NCK),
                                      t[:, :, CK - 1:CK].to_broadcast([P, NCK, CK]), t, ALU.subtract).then_inc(s_sub, 1)
                else:
                    lev = s - 2
                    src, dst, h = blocks(bb[:, b], lev), blocks(X[:, b, lev], lev), 1 << lev
                    nb = SEQ // (2 * h)
                    mid = src[:, :, 0, h - 1:h].to_broadcast([P, nb, h])
                    dve.tensor_tensor(dst[:, :, 0, :], mid, src[:, :, 0, :], ALU.subtract)
                    dve.tensor_tensor(dst[:, :, 1, :], src[:, :, 1, :], mid, ALU.subtract).then_inc(s_sub, 1)

            def chunk(n, b, c, more):
                m = NCK * n + c
                dve.wait_ge(s_A, m + 1)
                dve.tensor_tensor(am[:, c % 2], pa[:, c % 2], masks[:], ALU.mult)
                dve.drain()
                dve.wait_ge(s_o, m + 1)
                dve.tensor_reduce(AT[:, c % 2], am[:, c % 2].rearrange("p l i -> p i l"), AX.X, ALU.add).then_inc(s_At, 1)
                dve.wait_ge(s_S, m + 1)
                nxt = S[:, (c + 1) % 2]
                if c == 0:
                    dve.tensor_copy(nxt, pS[:, 0:dv]).then_inc(s_Sc, 1)
                else:
                    dve.scalar_tensor_tensor(nxt, S[:, c % 2], el[:, b, c:c + 1], pS[:, 0:dv], ALU.mult, ALU.add).then_inc(s_Sc, 1)
            heads(dve, prepare, chunk, 2 + LEVELS)

        @block.gpsimd
        def _(pool):
            def prepare(n, b, s, use):
                e = L2 * n
                if s == 0:
                    pool.wait_ge(s_qk, n + 1)
                    pool.wait_ge(s_exp, e + 1)
                    pool.tensor_tensor(X[:, b, LEVELS], X[:, b, LEVELS], q[:, b], ALU.mult).then_inc(s_X, 1)
                elif s == 1:
                    pool.wait_ge(s_exp, e + 2)
                    pool.tensor_tensor(X[:, b, LEVELS + 1], X[:, b, LEVELS + 1], k[:, b], ALU.mult).then_inc(s_X, 1)
                else:
                    lev, h = s - 2, 1 << (s - 2)
                    pool.wait_ge(s_exp, e + s + 1)
                    f = lambda ap: ap.rearrange("p (n a s) -> p n a s", a=2, s=h)
                    x = f(X[:, b, lev])
                    pool.tensor_tensor(x[:, :, 0, :], x[:, :, 0, :], f(k[:, b])[:, :, 0, :], ALU.mult)
                    pool.tensor_tensor(x[:, :, 1, :], x[:, :, 1, :], f(q[:, b])[:, :, 1, :], ALU.mult).then_inc(s_X, 1)
            heads(pool, prepare, lambda *a: None, L2)

        @block.tensor
        def _(pe):
            pe.sem_inc(s_o, 2)

            def levels(n, b, c):
                m = NCK * n + c
                sl = slice(c * CK, (c + 1) * CK)
                pe.wait_ge(s_At, m + 1)
                for lev in range(LEVELS):
                    pe.matmul(pa[:, c % 2, lev, :], X[:, b, lev, sl], X[:, b, lev, sl], start=True, stop=True)
                pe.matmul(pa[:, c % 2, LEVELS, :], k[:, b, sl], q[:, b, sl], start=True, stop=True).then_inc(s_A, 1)

            def chunk(n, b, c, more):
                m = NCK * n + c
                sl = slice(c * CK, (c + 1) * CK)
                if c == 0:
                    pe.wait_ge(s_X, L2 * n + L2)
                    levels(n, b, 0)
                if more:
                    levels(n, b, c + 1)
                pe.wait_ge(s_kc, m + 1)
                pe.transpose(pk[:, 0:CK], X[:, b, LEVELS + 1, sl], C.ident[:]).then_inc(s_kT, 1)
                pe.wait_ge(s_kc, m + 2)
                pe.wait_ge(s_Sc, m + 1)
                pe.matmul(pS[:, 0:dv], kd[:, c % 2], v[:, b, c, :], start=True, stop=True).then_inc(s_S, 1)
                pe.wait_ge(s_oc, m + 1)
                pe.wait_ge(s_At, m + 3)
                if c > 0:
                    pe.matmul(po[:, c % 2, 0:dv], X[:, b, LEVELS, sl], S[:, c % 2], start=True, stop=False)
                pe.matmul(po[:, c % 2, 0:dv], AT[:, c % 2], v[:, b, c, :], start=(c == 0), stop=True).then_inc(s_o, 1)
            heads(pe, lambda *a: None, chunk, 0)


def merge_out(C):
    nc, ins = C.nc, C.ins
    br = [(A_HEADS, N_AG, "hgrn_onorm_2"), (B_HEADS, N_BG, "gla_onorm_2"), (C_HEADS, N_CG, "gdn_onorm_2")]
    NJ = len(br)
    with ExitStack() as st:
        sb = lambda n, s: st.enter_context(nc.sbuf_tensor(f"y_{n}", s, F32))
        sem = lambda n: nc.alloc_semaphore(f"y_{n}")
        w = sb("w", [P, KD, D])
        post = sb("post", [P, D])
        on = [sb(f"on{j}", [P, D // h]) for j, (h, _, _) in enumerate(br)]
        o = sb("o", [P, NJ, D])
        g = sb("g", [P, NJ, D])
        mg = sb("mg", [P, NJ, D])
        sq = sb("sq", [P, NJ, D])
        ms = sb("ms", [P, NJ, 8])
        rs = sb("rs", [P, NJ, 8])
        t2 = sb("t2", [P, D])
        junk = sb("junk", [P, D])
        y = sb("y", [P, 2, D])
        yT = sb("yT", [P, KD, P])
        mo = sb("mo", [P, D])
        ms2 = sb("ms2", [P, 2])
        pt = st.enter_context(nc.psum_tensor("y_pt", [P, KD, P], F32))
        po = st.enter_context(nc.psum_tensor("y_po", [P, 2, CH], F32))
        s_tab = sem("tables_loaded")
        s_in = [sem(f"branch{j}_loaded") for j in range(NJ)]
        s_act = sem("gates_and_squares_ready")
        s_gg = sem("gains_multiplied")
        s_ms = sem("head_sums")
        s_rs = sem("head_rs")
        s_b = sem("branch_added")
        s_y = sem("y_ready")
        s_T = sem("y_transposed")
        s_Tc = sem("yT_taken")
        s_o = sem("product_done")
        s_sm = sem("row_sums")
        s_ss = sem("row_rs")
        s_x = sem("x_updated")
        block = st.enter_context(nc.Block())

        def walk(eng, step, turn, tail):
            def steps(t, par):
                for j in range(NJ):
                    step(NJ * t + j, t, j, par)
            steps(0, 0)
            with eng.Fori(0, NT // 2 - 1) as i:
                for par in range(2):
                    turn(2 * i + par, par)
                    steps(2 * i + par + 1, 1 - par)
                    tail(2 * i + par)
            turn(NT - 2, 0)
            steps(NT - 1, 1)
            tail(NT - 2)
            turn(NT - 1, 1)
            tail(NT - 1)

        nothing = lambda *a: None

        @block.sync
        def _(sp):
            for j, (h, _, name) in enumerate(br):
                sp.dma_start(on[j][:], ins[name][0].partition_broadcast(P)).then_inc(s_tab, 16)
            sp.dma_start(post[:], ins["ln_mix_post_2"][0].partition_broadcast(P)).then_inc(s_tab, 16)

            def load(t, j):
                rows = ds(t * P, P)
                sp.dma_start(o[:, j], C.o_dram[j][rows, :]).then_inc(s_in[j], 16)
                sp.dma_start(g[:, j], C.pn_dram[rows, br[j][1]:br[j][1] + D]).then_inc(s_in[j], 16)
                sp.dma_start(mg[:, j], C.pn_dram[rows, N_M + j * D:N_M + (j + 1) * D]).then_inc(s_in[j], 16)
            for j in range(NJ):
                load(0, j)
            sp.dma_start(w[:], ins["w_out_2"][0].rearrange("(k p) n -> p k n", p=P)).then_inc(s_tab, 16)
            with sp.Fori(1, NT) as t:
                for j in range(NJ):
                    sp.wait_ge(s_b, NJ * (t - 1) + j + 1)
                    load(t, j)

        @block.scalar
        def _(act):
            def step(n, t, j, par):
                act.wait_ge(s_in[j], 48 * (t + 1))
                act.activation(g[:, j], g[:, j], ACT.Silu)
                act.activation(mg[:, j], mg[:, j], ACT.Tanh, scale=0.5)
                act.activation(sq[:, j], o[:, j], ACT.Square).then_inc(s_act, 1)

            def turn(t, par):
                act.wait_ge(s_T, t + 3)
                act.copy(yT[:], pt[:]).then_inc(s_Tc, 1)

            def tail(t):
                act.wait_ge(s_o, t + 1)
                act.activation(junk[:], po[:].rearrange("p a b -> p (a b)"), ACT.Square, accum_out=ms2[:, 0:1]).then_inc(s_sm, 1)
                act.drain()
            walk(act, step, turn, tail)

        @block.gpsimd
        def _(pool):
            pool.wait_ge(s_tab, 16 * 5)
            for j in range(NJ):
                pool.tensor_scalar(on[j][:], on[j][:], 0.5, None, ALU.mult)
            pool.drain()

            def step(n, t, j, par):
                H = br[j][0]
                pool.wait_ge(s_act, n + 1)
                m = g[:, j].rearrange("p (h n) -> p h n", h=H)
                pool.tensor_tensor(m, m, on[j][:].unsqueeze(1).to_broadcast([P, H, D // H]), ALU.mult).then_inc(s_gg, 1)
                pool.wait_ge(s_ms, n + 1)
                inverse_root(C, pool, rs[:, j, 0:H], ms[:, j, 0:H], D // H).then_inc(s_rs, 1)

            def tail(t):
                pool.wait_ge(s_sm, t + 1)
                inverse_root(C, pool, ms2[:, 1:2], ms2[:, 0:1], D).then_inc(s_ss, 1)
            walk(pool, step, nothing, tail)

        @block.vector
        def _(dve):
            dve.wait_ge(s_tab, 16 * 5)

            def step(n, t, j, par):
                H = br[j][0]
                dve.wait_ge(s_act, n + 1)
                dve.tensor_reduce(ms[:, j, 0:H], sq[:, j].rearrange("p (h n) -> p h n", h=H), AX.X, ALU.add).then_inc(s_ms, 1)
                dve.wait_ge(s_gg, n + 1)
                dve.scalar_tensor_tensor(mg[:, j], mg[:, j], 1.0, g[:, j], ALU.add, ALU.mult)
                dve.drain()
                dve.wait_ge(s_rs, n + 1)
                if j == 0:
                    dve.wait_ge(s_T, t + 1)
                dst, w_ = (y[:, par] if j == 0 else t2), D // H
                for h in range(H):
                    c = slice(h * w_, (h + 1) * w_)
                    e = dve.scalar_tensor_tensor(dst[:, c], o[:, j, c], rs[:, j, h:h + 1], mg[:, j, c], ALU.mult, ALU.mult)
                e.then_inc(s_b, 1)
                dve.drain()
                if j > 0:
                    e = dve.tensor_tensor(y[:, par], y[:, par], t2[:], ALU.add)
                    if j == NJ - 1:
                        e.then_inc(s_y, 1)
                    dve.drain()

            def tail(t):
                dve.wait_ge(s_ss, t + 1)
                dve.scalar_tensor_tensor(mo[:], po[:].rearrange("p a b -> p (a b)"), ms2[:, 1:2], post[:], ALU.mult, ALU.mult)
                dve.drain()
                x = C.x_sb[:, ds(t, 1), :].rearrange("p t n -> p (t n)")
                dve.tensor_tensor(x, x, mo[:], ALU.add).then_inc(s_x, 1)
            walk(dve, step, nothing, tail)

        @block.tensor
        def _(pe):
            pe.sem_inc(s_T, 2)
            pe.sem_inc(s_x, 1)
            pe.wait_ge(s_tab, 16 * 5)

            def turn(t, par):
                pe.wait_ge(s_y, t + 1)
                for k in range(KD):
                    mm = pe.transpose(pt[:, k, :], y[:, par, k * P:(k + 1) * P], C.ident[:])
                mm.then_inc(s_T, 1)
                pe.wait_ge(s_Tc, t + 1)
                pe.wait_ge(s_x, t + 1)
                for h in range(2):
                    for k in range(KD):
                        mm = pe.matmul(po[:, h, :], yT[:, k, :], w[:, k, h * CH:(h + 1) * CH], start=(k == 0), stop=(k == KD - 1))
                mm.then_inc(s_o, 1)
            walk(pe, nothing, turn, nothing)


def gated_delta(C):
    nc, ins = C.nc, C.ins
    H = C_HEADS
    with ExitStack() as st:
        sb = lambda n, s: st.enter_context(nc.sbuf_tensor(f"d_{n}", s, F32))
        sem = lambda n: nc.alloc_semaphore(f"d_{n}")
        PAD = 3
        causal = sb("causal", [P, CK])
        masks = sb("masks", [P, LEVELS + 1, CK])
        al = sb("al", [P, 2, H])
        ea = sb("ea", [P, H])
        cr = sb("cr", [4 * 24, P])
        cw = sb("cw", [P, 4, 3, H])
        gu = sb("gu", [P, NCK, H])
        gl = sb("gl", [P, NCK, H])
        gg = sb("gg", [P, H, NCK])
        sc = sb("sc", [P, 6, H, NCK])
        hs = sb("hs", [P, 6, NCK])
        cwh = sb("cwh", [P, 3, 4])
        raw = sb("raw", [P, 3, PAD + SEQ])
        cv = sb("cv", [P, 3, SEQ])
        dg = sb("dg", [P, 2, NCK, CK])
        qk = sb("qk", [P, 2, NCK, CK])
        sq = sb("sq", [P, 2, NCK, CK])
        ss = sb("ss", [P, 2, NCK])
        rs = sb("rs", [P, 2, NCK])
        qkT = sb("qkT", [P, 2, NCK, CK])
        vb = sb("vb", [P, NCK, CK])
        kb = sb("kb", [P, NCK, CK])
        kd = sb("kd", [P, NCK, CK])
        DT = sb("DT", [P, NCK, CK])
        MT = sb("MT", [P, NCK, CK])
        Ml = sb("Ml", [P, 2, NCK, CK])
        QKT = sb("QKT", [P, NCK, CK])
        er = sb("er", [P, NCK, CK])
        XY = sb("XY", [P, 2, NCK, CK])
        Pm = sb("Pm", [P, NCK, CK])
        wT = sb("wT", [P, NCK, CK])
        vn = sb("vn", [P, 2, CK])
        S = sb("S", [P, 2, CK])
        o = sb("o", [P, 2, CK])
        ps = st.enter_context(nc.psum_tensor("d_ps", [P, 8, CH], F32))
        names = ("tables", "raw", "conv_rows", "conv_cols", "conv_cols_taken", "u", "abs", "gates", "cumulated",
                 "exps", "scalars", "per_head", "first_tap", "conv", "silu", "diagonals", "tokens", "b_rows", "qk_tokens",
                 "v_beta", "sums", "rs", "qk_normed", "qkT", "qT_taken", "kT_taken", "beta_rows", "exponents", "decay",
                 "eb_rows", "kk", "MT", "QKT", "level_M", "P", "P_taken", "XY", "XY_ready", "w", "w_taken", "v_new",
                 "v_new_taken", "o", "o_taken", "S", "S_ready", "qdec", "pad", "kparts")
        s = {n: sem(n) for n in names}
        s_st = [sem(f"o_stored{b}") for b in range(2)]
        block = st.enter_context(nc.Block())
        flat = lambda ap: ap.rearrange("p c t -> p (c t)")
        bank2 = lambda b: ps[:, b:b + 2, :].rearrange("p b (c t) -> p (b c) t", t=CK)
        over_t = lambda col: col.unsqueeze(2).to_broadcast([P, NCK, CK])
        over_c = lambda mat: mat.unsqueeze(1).to_broadcast([P, NCK, CK])

        @block.sync
        def _(sp):
            sp.dma_start(causal[:], ins["t_causal"]).then_inc(s["tables"], 16)
            sp.dma_start(masks[:], ins["t_levels"]).then_inc(s["tables"], 16)
            sp.dma_start(al[:, 0], ins["gdn_a_log_2"][0].partition_broadcast(P)).then_inc(s["tables"], 16)
            sp.dma_start(al[:, 1], ins["gdn_dt_bias_2"][0].partition_broadcast(P)).then_inc(s["tables"], 16)
            sp.dma_start(cr[:], ins["gdn_conv_2"][0].rearrange("j (s p) -> (j s) p", p=P)).then_inc(s["tables"], 16)
            for b in range(2):
                sp.sem_inc(s_st[b], 16)

            def load(h):
                for q in range(3):
                    sp.dma_start(raw[:, q, PAD:PAD + SEQ], C.pt_dram[ds(T_C + q * D + h * P, P), :]).then_inc(s["raw"], 16)

            def stores(h):
                for c in range(NCK):
                    sp.wait_ge(s["o_taken"], NCK * h + c + 3)
                    sp.dma_start(C.o_dram[2][c * CK:(c + 1) * CK, ds(h * CK, CK)], o[:, c % 2]).then_inc(s_st[c % 2], 16)
            load(0)
            with sp.Fori(0, H - 1) as h:
                sp.wait_ge(s["conv"], h + 1)
                load(h + 1)
                stores(h)
            stores(H - 1)
            for b in range(2):
                sp.wait_ge(s_st[b], 16 * (H * NCK // 2 + 1))

        @block.scalar
        def _(act):
            act.sem_inc(s["o_taken"], 2)
            act.wait_ge(s["tables"], 80)
            act.wait_ge(s["u"], 1)
            act.activation(sc[:, 3].rearrange("p h c -> p c h"), C.ab[:, :, H:2 * H], ACT.Sigmoid)
            act.activation(ea[:], al[:, 0], ACT.Exp)
            act.activation(gl[:], gu[:], ACT.Abs)
            act.drain()
            act.activation(gl[:], gl[:], ACT.Exp, scale=-1.0)
            act.drain()
            act.activation(gl[:], gl[:], ACT.Ln, bias=1.0).then_inc(s["abs"], 1)
            act.wait_ge(s["exps"], 1)
            act.activation(sc[:, 1], sc[:, 1], ACT.Exp)
            act.activation(sc[:, 2], sc[:, 2], ACT.Exp)
            act.activation(sc[:, 4], sc[:, 0], ACT.Exp).then_inc(s["scalars"], 1)
            with act.Fori(0, H) as h:
                act.wait_ge(s["per_head"], h + 1)
                act.wait_ge(s["raw"], 48 * h + 48)
                act.wait_ge(s["tokens"], h + 1)
                for q in range(3):
                    e = act.activation(cv[:, q], raw[:, q, 0:SEQ], ACT.Identity, scale=cwh[:, q, 0:1])
                e.then_inc(s["first_tap"], 1)
                act.wait_ge(s["conv"], h + 1)
                act.activation(cv[:], cv[:], ACT.Silu).then_inc(s["silu"], 1)
                act.wait_ge(s["tokens"], h + 2)
                act.copy(qk[:, 0], bank2(0))
                act.copy(qk[:, 1], bank2(2))
                act.drain()
                act.activation(sq[:], qk[:], ACT.Square).then_inc(s["qk_tokens"], 1)
                act.wait_ge(s["b_rows"], h + 1)
                act.wait_ge(s["exponents"], h + 1)
                act.activation(er[:], bank2(6), ACT.Exp).then_inc(s["eb_rows"], 1)
                act.activation(DT[:], DT[:], ACT.Exp).then_inc(s["decay"], 1)
                act.wait_ge(s["qkT"], h + 1)
                act.copy(qkT[:, 0], bank2(0)).then_inc(s["qT_taken"], 1)
                for lev in range(1, LEVELS):
                    for hf in range(2):
                        n = 2 * (LEVELS - 1) * h + 2 * (lev - 1) + hf
                        act.wait_ge(s["P"], n + 1)
                        act.copy(Pm[:, 4 * hf:4 * hf + 4], ps[:, 4 + hf].rearrange("p (c t) -> p c t", t=CK)).then_inc(s["P_taken"], 1)
                act.wait_ge(s["w"], h + 1)
                act.activation(wT[:], bank2(6), ACT.Copy, scale=-1.0).then_inc(s["w_taken"], 1)
                for c in range(NCK):
                    m = NCK * h + c
                    act.wait_ge(s["v_new"], m + 1)
                    act.copy(vn[:, c % 2], ps[:, 4 + c % 2, 0:CK]).then_inc(s["v_new_taken"], 1)
                    act.wait_ge(s["o"], m + 1)
                    act.wait_ge(s_st[c % 2], 16 * ((NCK // 2) * h + c // 2 + 1))
                    act.copy(o[:, c % 2], ps[:, c % 2, 0:CK]).then_inc(s["o_taken"], 1)

        @block.gpsimd
        def _(pool):
            pool.memset(raw[:, :, 0:PAD], 0.0).then_inc(s["pad"], 1)
            pool.wait_ge(s["tables"], 80)
            with pool.Fori(0, H) as h:
                pool.wait_ge(s["sums"], h + 1)
                inverse_root(C, pool, flat(rs[:]), flat(ss[:]), 1).then_inc(s["rs"], 1)
                pool.wait_ge(s["MT"], h + 1)
                for lev in range(LEVELS):
                    if lev >= 3:
                        pool.wait_ge(s["P"], 2 * (LEVELS - 1) * h + 2 * (lev - 2))
                    elif lev == 2:
                        pool.wait_ge(s["XY_ready"], (2 * (LEVELS - 1) + 1) * h + 1)
                    pool.tensor_tensor(Ml[:, lev % 2], MT[:], over_c(masks[:, lev]), ALU.mult).then_inc(s["level_M"], 1)

        @block.vector
        def _(dve):
            dve.sem_inc(s["S_ready"], 1)
            dve.wait_ge(s["tables"], 80)
            dve.wait_ge(s["pad"], 1)
            dve.tensor_tensor(gu[:], C.ab[:, :, 0:H], al[:, 1].unsqueeze(1).to_broadcast([P, NCK, H]), ALU.add).then_inc(s["u"], 1)
            dve.wait_ge(s["abs"], 1)
            dve.scalar_tensor_tensor(gl[:], gu[:], 0.0, gl[:], ALU.max, ALU.add)
            dve.drain()
            dve.tensor_scalar(gl[:], gl[:], -1.0, None, ALU.mult)
            dve.drain()
            dve.tensor_tensor(gg[:], gl[:].rearrange("p c h -> p h c"), ea[:].unsqueeze(2).to_broadcast([P, H, NCK]), ALU.mult).then_inc(s["gates"], 1)
            dve.wait_ge(s["cumulated"], 1)
            f = lambda ap: ap.rearrange("p h c -> p (h c)")
            dve.tensor_copy(f(sc[:, 0]), ps[:, 0, 0:H * NCK])
            dve.tensor_copy(f(sc[:, 1]), ps[:, 1, 0:H * NCK])
            dve.tensor_copy(cw[:].rearrange("p j s h -> p (j s h)"), ps[:, 2, 0:96]).then_inc(s["conv_cols_taken"], 1)
            dve.drain()
            dve.tensor_tensor(sc[:, 2], sc[:, 1], sc[:, 0], ALU.subtract).then_inc(s["exps"], 1)
            dve.wait_ge(s["scalars"], 1)
            dve.tensor_tensor(sc[:, 4], sc[:, 4], sc[:, 3], ALU.mult)
            dve.drain()
            with dve.Fori(0, H) as h:
                dve.drain()
                dve.tensor_copy(hs[:, 0:5], sc[:, 0:5, ds(h, 1), :].rearrange("p k h c -> p k (h c)"))
                dve.tensor_copy(cwh[:].rearrange("p s j -> p j s"), cw[:, :, :, ds(h, 1)].rearrange("p j s h -> p j (s h)")).then_inc(s["per_head"], 1)
                dve.drain()
                for q in range(2):
                    e = dve.tensor_tensor(dg[:, q], over_c(C.ident[:]), over_t(hs[:, 3 * q]), ALU.mult)
                e.then_inc(s["diagonals"], 1)
                dve.wait_ge(s["raw"], 48 * h + 48)
                dve.wait_ge(s["first_tap"], h + 1)
                for j in range(1, 4):
                    for q in range(3):
                        e = dve.scalar_tensor_tensor(cv[:, q], raw[:, q, j:j + SEQ], cwh[:, q, j:j + 1], cv[:, q], ALU.mult, ALU.add)
                    if j < 3:
                        dve.drain()
                e.then_inc(s["conv"], 1)
                dve.wait_ge(s["b_rows"], h + 1)
                dve.tensor_tensor(DT[:], bank2(6), over_t(hs[:, 0]), ALU.subtract)
                dve.drain()
                dve.tensor_scalar(DT[:], DT[:], 0.0, None, ALU.min).then_inc(s["exponents"], 1)
                dve.wait_ge(s["tokens"], h + 2)
                dve.tensor_tensor(vb[:], bank2(4), over_t(hs[:, 3]), ALU.mult).then_inc(s["v_beta"], 1)
                dve.wait_ge(s["qk_tokens"], h + 1)
                dve.tensor_reduce(ss[:], sq[:], AX.X, ALU.add).then_inc(s["sums"], 1)
                dve.wait_ge(s["rs"], h + 1)
                dve.tensor_scalar(rs[:, 0], rs[:, 0], float(P) ** -0.5, None, ALU.mult)
                dve.drain()
                for q in range(2):
                    e = dve.tensor_tensor(qk[:, q], qk[:, q], over_t(rs[:, q]), ALU.mult)
                e.then_inc(s["qk_normed"], 1)
                dve.drain()
                dve.tensor_tensor(kb[:], qk[:, 1], over_t(hs[:, 4]), ALU.mult)
                dve.tensor_tensor(kd[:], qk[:, 1], over_t(hs[:, 2]), ALU.mult).then_inc(s["kparts"], 1)
                dve.wait_ge(s["qkT"], h + 1)
                dve.tensor_copy(qkT[:, 1], bank2(2)).then_inc(s["kT_taken"], 1)
                dve.wait_ge(s["decay"], h + 1)
                dve.tensor_tensor(DT[:], DT[:], over_c(causal[:]), ALU.mult)
                dve.drain()
                dve.wait_ge(s["kk"], h + 1)
                dve.tensor_tensor(MT[:], bank2(0), DT[:], ALU.mult)
                dve.drain()
                dve.wait_ge(s["beta_rows"], h + 1)
                dve.tensor_tensor(MT[:], MT[:], bank2(4), ALU.mult).then_inc(s["MT"], 1)
                dve.tensor_tensor(QKT[:], bank2(2), DT[:], ALU.mult).then_inc(s["QKT"], 1)
                dve.wait_ge(s["eb_rows"], h + 1)
                dve.tensor_tensor(er[:], er[:], qkT[:, 0], ALU.mult).then_inc(s["qdec"], 1)
                dve.wait_ge(s["level_M"], LEVELS * h + 1)
                dve.tensor_tensor(XY[:, 1], over_c(C.ident[:]), Ml[:, 0], ALU.subtract)
                dve.wait_ge(s["XY"], (2 * (LEVELS - 1) + 1) * h + 1)
                dve.tensor_tensor(XY[:, 0], over_c(C.ident[:]), bank2(4), ALU.subtract).then_inc(s["XY_ready"], 1)
                for lev in range(1, LEVELS):
                    for hf in range(2):
                        if hf == 0:
                            dve.drain()
                        dve.wait_ge(s["XY"], (2 * (LEVELS - 1) + 1) * h + 2 * (lev - 1) + hf + 2)
                        x = XY[:, :, 4 * hf:4 * hf + 4].rearrange("p a c t -> p a (c t)")
                        dve.tensor_tensor(x, x, ps[:, 2 * hf:2 * hf + 2, :], ALU.subtract).then_inc(s["XY_ready"], 1)
                for c in range(NCK):
                    m = NCK * h + c
                    dve.drain()
                    dve.wait_ge(s["S"], m + 1)
                    if c == 0:
                        dve.tensor_copy(S[:, 1], ps[:, 2, 0:CK]).then_inc(s["S_ready"], 1)
                    else:
                        dve.scalar_tensor_tensor(S[:, (c + 1) % 2], S[:, c % 2], hs[:, 1, c:c + 1], ps[:, 2 + c % 2, 0:CK],
                                                 ALU.mult, ALU.add).then_inc(s["S_ready"], 1)

        @block.tensor
        def _(pe):
            pe.sem_inc(s["tokens"], 1)
            pe.wait_ge(s["tables"], 80)
            pe.transpose(ps[:, 2, 0:96], cr[:], C.ident[0:96, 0:96])
            pe.wait_ge(s["gates"], 1)
            pe.matmul(ps[:, 0, 0:H * NCK], causal[:], gg[:].rearrange("p h c -> p (h c)"), start=True, stop=True)
            pe.matmul(ps[:, 1, 0:H * NCK], C.ones[:], gg[:].rearrange("p h c -> p (h c)"), start=True, stop=True).then_inc(s["cumulated"], 1)
            pe.wait_ge(s["conv_cols_taken"], 1)
            chunk = lambda bank, c: ps[:, bank + c // 4, (c % 4) * CK:(c % 4 + 1) * CK]
            NL = 2 * (LEVELS - 1)
            with pe.Fori(0, H) as h:
                pe.wait_ge(s["diagonals"], h + 1)
                for b in range(2):
                    mm = pe.matmul(ps[:, 6 + b], C.ones[:], flat(dg[:, 0, 4 * b:4 * b + 4]), start=True, stop=True)
                mm.then_inc(s["b_rows"], 1)
                pe.wait_ge(s["silu"], h + 1)
                pe.wait_ge(s["o_taken"], NCK * h + 2)
                pe.wait_ge(s["S_ready"], NCK * h + 1)
                for q in range(3):
                    for c in range(NCK):
                        mm = pe.transpose(chunk(2 * q, c), cv[:, q, c * CK:(c + 1) * CK], C.ident[:])
                mm.then_inc(s["tokens"], 1)
                pe.wait_ge(s["v_beta"], h + 1)
                for b in range(2):
                    mm = pe.matmul(ps[:, 4 + b], C.ones[:], flat(dg[:, 1, 4 * b:4 * b + 4]), start=True, stop=True)
                mm.then_inc(s["beta_rows"], 1)
                pe.wait_ge(s["qk_normed"], h + 1)
                for q in range(2):
                    for c in range(NCK):
                        mm = pe.transpose(chunk(2 * q, c), qk[:, q, c], C.ident[:])
                mm.then_inc(s["qkT"], 1)
                pe.wait_ge(s["qT_taken"], h + 1)
                pe.wait_ge(s["kT_taken"], h + 1)
                for q in range(2):
                    for c in range(NCK):
                        mm = pe.matmul(chunk(2 * q, c), qkT[:, 1, c], qkT[:, 1 - q, c], start=True, stop=True)
                mm.then_inc(s["kk"], 1)
                pe.wait_ge(s["MT"], h + 1)
                pe.wait_ge(s["level_M"], LEVELS * h + 1)
                for c in range(NCK):
                    mm = pe.transpose(chunk(4, c), Ml[:, 0, c], C.ident[:])
                mm.then_inc(s["XY"], 1)
                pe.wait_ge(s["QKT"], h + 1)
                for lev in range(1, LEVELS):
                    pe.wait_ge(s["level_M"], LEVELS * h + lev + 1)
                    for hf in range(2):
                        pe.wait_ge(s["XY_ready"], (NL + 1) * h + (1 if lev == 1 else 2 * (lev - 2) + hf + 2))
                        for c in range(4 * hf, 4 * hf + 4):
                            mm = pe.matmul(chunk(4, c), Ml[:, lev % 2, c], XY[:, 0, c], start=True, stop=True)
                        mm.then_inc(s["P"], 1)
                    for hf in range(2):
                        pe.wait_ge(s["P_taken"], NL * h + 2 * (lev - 1) + hf + 1)
                        for c in range(4 * hf, 4 * hf + 4):
                            pe.matmul(ps[:, 2 * hf, (c % 4) * CK:(c % 4 + 1) * CK], XY[:, 1, c], Pm[:, c], start=True, stop=True)
                        for c in range(4 * hf, 4 * hf + 4):
                            mm = pe.matmul(ps[:, 2 * hf + 1, (c % 4) * CK:(c % 4 + 1) * CK], Pm[:, c], XY[:, 1, c], start=True, stop=True)
                        mm.then_inc(s["XY"], 1)
                pe.wait_ge(s["XY_ready"], (NL + 1) * h + NL + 1)
                pe.wait_ge(s["eb_rows"], h + 1)
                pe.wait_ge(s["kparts"], h + 1)
                for c in range(NCK):
                    mm = pe.matmul(chunk(6, c), kb[:, c], XY[:, 1, c], start=True, stop=True)
                mm.then_inc(s["w"], 1)
                pe.wait_ge(s["w_taken"], h + 1)
                pe.wait_ge(s["qdec"], h + 1)
                for c in range(NCK):
                    m = NCK * h + c
                    pe.wait_ge(s["S_ready"], m + 1)
                    mm = pe.matmul(ps[:, 4 + c % 2, 0:CK], XY[:, 1, c], vb[:, c], start=True, stop=(c == 0))
                    if c > 0:
                        mm = pe.matmul(ps[:, 4 + c % 2, 0:CK], wT[:, c], S[:, c % 2], start=False, stop=True)
                    mm.then_inc(s["v_new"], 1)
                    pe.wait_ge(s["v_new_taken"], m + 1)
                    pe.matmul(ps[:, 2 + c % 2, 0:CK], kd[:, c], vn[:, c % 2], start=True, stop=True).then_inc(s["S"], 1)
                    pe.wait_ge(s["o_taken"], m + 1)
                    if c > 0:
                        pe.matmul(ps[:, c % 2, 0:CK], er[:, c], S[:, c % 2], start=True, stop=False)
                    pe.matmul(ps[:, c % 2, 0:CK], QKT[:, c], vn[:, c % 2], start=(c == 0), stop=True).then_inc(s["o"], 1)


def mlp(C, half):
    nc, ins = C.nc, C.ins
    FT = FF // P
    UC = FF // CH
    DL = FT // 2
    KH = KD // 2
    TT = CH // P
    with ExitStack() as st:
        sb = lambda n, s, dt=F32: st.enter_context(nc.sbuf_tensor(f"u{half}_{n}", s, dt))
        sem = lambda n: nc.alloc_semaphore(f"u{half}_{n}")
        raw = sb("raw", [P, 2, KH * CH])
        wh = sb("wh", [P, 2, KH * CH], F32R)
        wl = sb("wl", [P, 2, KH * CH], F32R)
        r = sb("r", [P, 2, CH])
        uT = sb("uT", [P, FT, CH])
        uh = sb("uh", [P, 2, CH], F32R)
        ul = sb("ul", [P, 2, CH], F32R)
        post = sb("post", [P, D])
        row = lambda q: uT[:, 2 * q:2 * q + 2, :].rearrange("p a b -> p (a b)")
        junk, mo = row(0), (row(1), row(2))
        ms = sb("ms", [P, TT, 2])
        ps = st.enter_context(nc.psum_tensor(f"u{half}_ps", [P, 8, CH], F32))
        s_tab = sem("post_loaded")
        s_raw = [sem(f"raw{b}_loaded") for b in range(2)]
        s_wh = [sem(f"hi{b}_ready") for b in range(2)]
        s_wl = [sem(f"lo{b}_ready") for b in range(2)]
        s_half = sem("first_half_done")
        s_up = sem("up_done")
        s_r = sem("relu_ready")
        s_rf = sem("relu_squared")
        s_uh = sem("hidden_hi_ready")
        s_ul = sem("hidden_lo_ready")
        s_f = sem("hidden_tile_used")
        s_ms = sem("row_sums")
        s_rs = sem("row_rs")
        block = st.enter_context(nc.Block())
        wu = ins["w_up_2"][0].rearrange("(k p) n -> p k n", p=P)
        wd = ins["w_down_2"][0].rearrange("(k p) n -> p k n", p=P)

        @block.sync
        def _(sp):
            def up(c, kh):
                sp.dma_start(raw[:, kh].rearrange("p (k n) -> p k n", k=KH),
                             wu[:, kh * KH:(kh + 1) * KH, ds(c * CH, CH)]).then_inc(s_raw[kh], 16)

            for kh in range(2):
                up(0, kh)
            sp.dma_start(post[:], ins["ln_mlp_post_2"][0].partition_broadcast(P)).then_inc(s_tab, 16)
            with sp.Fori(1, UC) as c:
                for kh in range(2):
                    sp.wait_ge(s_wl[kh], c)
                    up(c, kh)
            with sp.Fori(0, DL // 2) as i:
                for b in range(2):
                    sp.wait_ge(s_wl[b], UC + i)
                    sp.dma_start(raw[:, b].rearrange("p (k n) -> p k n", k=2),
                                 wd[:, ds((2 * i + b) * 2, 2), :]).then_inc(s_raw[b], 16)

        def triple(ps_ap, lhs, rhs, start, stop):
            for q, (a, b) in enumerate(((0, 0), (0, 1), (1, 0))):
                mm = nc.tensor.matmul(ps_ap, lhs[a], rhs[b], start=(start and q == 0), stop=(stop and q == 2))
            return mm

        @block.tensor
        def _(pe):
            pe.sem_inc(s_r, 8)
            with pe.Fori(0, UC // 2) as i:
                for a in range(2):
                    for kh in range(2):
                        pe.wait_ge(s_wl[kh], 2 * i + a + 1)
                        for c in range(4):
                            q = 4 * a + c
                            if kh == 0:
                                pe.wait_ge(s_r, 8 * i + q + 1)
                            for k in range(KH):
                                cols = slice(k * CH + c * P, k * CH + (c + 1) * P)
                                kk = kh * KH + k
                                mm = triple(ps[:, q], (wh[:, kh, cols], wl[:, kh, cols]), (C.hi[:, kk, :], C.lo[:, kk, :]),
                                            kk == 0, kk == KD - 1)
                            if kh == 1:
                                mm.then_inc(s_up, 1)
                        if kh == 0:
                            mm.then_inc(s_half, 1)
            pe.wait_ge(s_r, FT + 8)

            def down(i, first, last):
                for x in range(4):
                    b, k = x // 2, x % 2
                    if k == 0:
                        pe.wait_ge(s_wl[b], UC + i + 1)
                    pe.wait_ge(s_ul, 4 * i + x + 1)
                    for t in range(TT):
                        for h in range(2):
                            cols, rows = slice(k * D + h * CH, k * D + (h + 1) * CH), slice(t * P, (t + 1) * P)
                            mm = triple(ps[:, 2 * t + h], (uh[:, x % 2, rows], ul[:, x % 2, rows]),
                                        (wh[:, b, cols], wl[:, b, cols]), first and x == 0, last and x == 3)
                    mm.then_inc(s_f, 1)
            down(0, True, False)
            with pe.Fori(1, FT // 4 - 1) as i:
                down(i, False, False)
            down(FT // 4 - 1, False, True)

        def split_walk(eng, weights, take, hidden):
            for b in range(2):
                weights(b, 1)
            with eng.Fori(0, UC // 2) as i:
                for a in range(2):
                    c = 2 * i + a
                    eng.wait_ge(s_half, c + 1)
                    weights(0, c + 2)
                    for q in range(4):
                        take(8 * i + 4 * a + q, 4 * a + q)
                    eng.wait_ge(s_up, 4 * c + 4)
                    weights(1, c + 2)
            eng.wait_ge(s_rf, FT + 2)
            hidden(0, 0)

            def down(i, first, last):
                for x in range(4):
                    f = 4 * i + x
                    if not (first and x == 0):
                        eng.wait_ge(s_f, f)
                    if not (last and x == 3):
                        hidden(f + 1, (x + 1) % 2)
                    if x == 0 and not first:
                        weights(1, UC + 1 + i)
                    if x == 2 and not last:
                        weights(0, UC + 2 + i)
            down(0, True, False)
            with eng.Fori(1, FT // 4 - 1) as i:
                down(i, False, False)
            down(FT // 4 - 1, False, True)

        @block.scalar
        def _(act):
            def weights(b, count):
                act.wait_ge(s_raw[b], 16 * count)
                act.copy(wh[:, b], raw[:, b]).then_inc(s_wh[b], 1)

            def take(n, q):
                act.wait_ge(s_up, n + 1)
                act.wait_ge(s_rf, n + 1)
                act.activation(r[:, q % 2], ps[:, q], ACT.Relu).then_inc(s_r, 1)

            def hidden(f, b):
                act.copy(uh[:, b], uT[:, ds(f, 1), :].rearrange("p a b -> p (a b)")).then_inc(s_uh, 1)
            split_walk(act, weights, take, hidden)
            act.wait_ge(s_f, FT)
            for t in range(TT):
                act.activation(junk, ps[:, 2 * t:2 * t + 2].rearrange("p a b -> p (a b)"), ACT.Square,
                               accum_out=ms[:, t, 0:1]).then_inc(s_ms, 1)
                act.drain()

        @block.gpsimd
        def _(pool):
            for t in range(TT):
                pool.wait_ge(s_ms, t + 1)
                inverse_root(C, pool, ms[:, t, 1:2], ms[:, t, 0:1], D).then_inc(s_rs, 1)

        @block.vector
        def _(dve):
            dve.sem_inc(s_rf, 2)

            def weights(b, count):
                dve.wait_ge(s_wh[b], count)
                dve.tensor_tensor(wl[:, b], raw[:, b], wh[:, b], ALU.subtract).then_inc(s_wl[b], 1)

            def take(n, q):
                dve.wait_ge(s_r, n + 9)
                dve.tensor_tensor(uT[:, ds(n, 1), :].rearrange("p a b -> p (a b)"), r[:, q % 2], r[:, q % 2],
                                  ALU.mult).then_inc(s_rf, 1)

            def hidden(f, b):
                dve.wait_ge(s_uh, f + 1)
                dve.tensor_tensor(ul[:, b], uT[:, ds(f, 1), :].rearrange("p a b -> p (a b)"), uh[:, b],
                                  ALU.subtract).then_inc(s_ul, 1)
            split_walk(dve, weights, take, hidden)
            dve.wait_ge(s_tab, 16)
            for t in range(TT):
                dve.wait_ge(s_rs, t + 1)
                dve.scalar_tensor_tensor(mo[t % 2], ps[:, 2 * t:2 * t + 2].rearrange("p a b -> p (a b)"), ms[:, t, 1:2], post[:],
                                         ALU.mult, ALU.mult)
                dve.drain()
                x = C.x_sb[:, TT * half + t, :]
                dve.tensor_tensor(x, x, mo[t % 2], ALU.add)


def second_block(C, out):
    nc, ins = C.nc, C.ins
    C.pt_dram = nc.dram_tensor("pt_dram", (T_C + 3 * D, SEQ), F32, kind="Internal").ap()
    C.pn_dram = nc.dram_tensor("pn_dram", (SEQ, N_M + 3 * D), F32, kind="Internal").ap()
    C.o_dram = [nc.dram_tensor(f"o{b}_dram", (SEQ, D), F32, kind="Internal").ap() for b in "abc"]
    with fresh_semaphores(nc):
        with ExitStack() as s2:
            C.gk = s2.enter_context(nc.sbuf_tensor("gk", [P, B_HEADS, SEQ], F32))
            C.ab = s2.enter_context(nc.sbuf_tensor("ab2", [P, NT, 2 * C_HEADS], F32))
            load_norm_gain(C, "lg0", ins["ln_mix_pre_2"][0])
            with ExitStack() as s3:
                C.hi = s3.enter_context(nc.sbuf_tensor("him", [P, KD, SEQ], F32R))
                C.lo = s3.enter_context(nc.sbuf_tensor("lom", [P, KD, SEQ], F32R))
                norm_transpose(C, "n2", [(0, NT, 0)])
                small_projections(C)
                w = ins["w_in_2"][0]
                pt, pn = C.pt_dram, C.pn_dram
                token = lambda a, z, c: dict(w=w[:, a:z], out=pn[:, c:c + z - a], kind="token", tiles=range(NT))
                channel = lambda a, z, r: dict(w=w[:, a:z], out=pt[r:r + z - a, :], kind="channel", tiles=None)
                project(C, "p2", [
                    channel(A_Q, A_I, T_AQ), token(A_I, B_Q, N_AI), channel(B_Q, B_V, T_BQ), token(B_V, B_GK, N_BV),
                    token(B_G, C_QKV, N_BG), channel(C_QKV, C_A, T_C), token(C_G, MERGE, N_CG), token(MERGE, N_IN, N_M)])
            gated_linear(C, "a")
            gated_linear(C, "b")
            gated_delta(C)
        merge_out(C)
        load_norm_gain(C, "lg1", ins["ln_mlp_pre_2"][0])
    with fresh_semaphores(nc):
        for half in range(2):
            with ExitStack() as s3:
                C.hi = s3.enter_context(nc.sbuf_tensor(f"hiu{half}", [P, KD, CH], F32R))
                C.lo = s3.enter_context(nc.sbuf_tensor(f"lou{half}", [P, KD, CH], F32R))
                norm_transpose(C, f"n3{half}", [(NT // 2 * half, NT // 2, 0)])
                mlp(C, half)
    store_x(C, out)


def tables():
    import numpy as np
    f = np.float32
    out = {"t_ident": np.eye(P, dtype=f)}
    sel = np.zeros((2, 2, P), f)
    sel[0, 0], sel[1, 1] = 1, 1
    out["t_sel"] = sel
    for name, n in (("t_dft_x", SEQ), ("t_dft_c", CTX)):
        jk = np.outer(np.arange(n), np.arange(n)) % n
        ang = 2 * np.pi * jk / n
        out[name] = (np.stack([np.cos(ang), np.sin(ang)]) / np.sqrt(n)).astype(f)
    ang = 2 * np.pi * (np.outer(np.arange(QK), np.arange(QK)) % QK) / QK
    chan = np.zeros((2, P, P))
    for o in (0, QK):
        chan[0, o:o + QK, o:o + QK] = np.cos(ang) / np.sqrt(QK)
        chan[1, o:o + QK, o:o + QK] = -np.sin(ang) / np.sqrt(QK)
    out["t_chan"] = chan.astype(f)
    band = np.zeros((P, 5, 4, P))
    L = 4 * P
    for g, w in enumerate(WINDOWS):
        full = np.zeros((L, L))
        for t in range(L):
            a, b = max(t - w // 2, 0), min(t + w - w // 2 - 1, L - 1)
            full[a:b + 1, t] = 1.0 / (b - a + 1)
        full -= np.eye(L)
        for kind, (r, c) in enumerate(((0, 0), (1, 1), (3, 3), (0, 1), (1, 0))):
            band[:, kind, g, :] = full[r * P:(r + 1) * P, c * P:(c + 1) * P]
    out["t_band"] = band.astype(f)
    t = np.arange(SEQ)
    half = QK // 2
    inv = (10000.0 ** (-np.arange(0, half, 2, dtype=f) / half)).astype(f)
    r, c = (t // 64).astype(f)[:, None] * inv, (t % 64).astype(f)[:, None] * inv
    ang = np.concatenate([r, r, c, c], axis=1).astype(np.float64)
    sign = np.tile(np.repeat([-1.0, 1.0], QK // 4), 2)
    out["t_rope"] = np.stack([np.cos(ang), np.sin(ang) * sign]).astype(f)
    i = np.arange(CK)
    lv = np.zeros((CK, LEVELS + 1, CK))
    for q in range(LEVELS):
        s = 1 << q
        lv[:, q, :] = ((i[:, None] // (2 * s)) == (i[None, :] // (2 * s))) & ((i[:, None] // s) % 2 == 0) & ((i[None, :] // s) % 2 == 1)
    lv[:, LEVELS, :] = np.eye(CK)
    out["t_levels"] = lv.astype(f)
    out["t_causal"] = (i[:, None] <= i[None, :]).astype(f)
    start = np.ones((P, SEQ), f)
    start[:, ::CK] = 0
    out["t_restart"] = start
    return out


def build(nc, ins, out):
    C = Shared()
    C.nc, C.ins = nc, ins
    C.p_dram = nc.dram_tensor("p_dram", (SEQ + CTX, INW), F32, kind="Internal").ap()
    with ExitStack() as st:
        sb = lambda n, s, k=st: k.enter_context(nc.sbuf_tensor(n, s, F32))
        C.x_sb = sb("x_sb", [P, NTA, D])
        C.ident = sb("ident", [P, P])
        C.minus_half = sb("minus_half", [P, 16])
        C.n_eps = sb("n_eps", [P, len(NORMED), 16])
        C.ones = sb("ones", [P, P])
        C.shift = sb("shift", [P, 2, KD])
        C.scale = sb("scale", [P, 2, KD])
        load_constants(C)
        with ExitStack() as st1:
            C.gate = sb("gate", [P, 2, D], st1)
            C.neglam = sb("neglam", [P, 1], st1)
            for l in range(DEPTH):
                last = l == DEPTH - 1
                with fresh_semaphores(nc):
                    modulation(C, l)
                    with ExitStack() as s2:
                        C.hi = s2.enter_context(nc.sbuf_tensor(f"hi{l}", [P, KD, SEQ + CTX], F32R))
                        C.lo = s2.enter_context(nc.sbuf_tensor(f"lo{l}", [P, KD, SEQ + CTX], F32R))
                        norm_transpose(C, f"n{l}", [(0, NT, 0), (NT, NTC, 1)])
                        w = ins["w_in"][l]
                        c = slice(K0, G0) if last else slice(0, INW)
                        project(C, f"p{l}", [dict(w=w, out=C.p_dram, kind="token", tiles=range(NT)),
                                             dict(w=w[:, c], out=C.p_dram[:, c], kind="token", tiles=range(NT, NTA))])
                    with ExitStack() as s1:
                        C.mix = sb(f"mix{l}", [P, NTA, D], s1)
                        fourier_pool(C, l, "x")
                        if not last:
                            fourier_pool(C, l, "c")
                        with ExitStack() as s2:
                            C.qT = sb(f"qT{l}", [P, HEADS, SEQ + CTX], s2)
                            C.kT = sb(f"kT{l}", [P, HEADS, SEQ + CTX], s2)
                            C.v_sb = sb(f"v{l}", [P, NTA, 512], s2)
                            qk_prepare(C, l)
                            attention(C, l)
                        mix_out(C, l)
        second_block(C, out)


def store_x(C, out):
    nc = C.nc
    with ExitStack() as st:
        s_out = nc.alloc_semaphore("x_stored")
        block = st.enter_context(nc.Block())

        @block.sync
        def _(sp):
            sp.dma_start(out[0].rearrange("(t p) d -> p t d", p=P), C.x_sb[:, 0:NT, :]).then_inc(s_out, 16)
            sp.wait_ge(s_out, 16)


_INS = ["x", "c", "ctx", "c_ctx", "norm_g", "w_mod", "b_mod", "w_in", "w_fourier", "w_pool", "pool_scale",
        "qk_norm_g", "lam_vecs", "subln_g", "w_out", "ln_mix_pre_2", "ln_mix_post_2", "ln_mlp_pre_2",
        "ln_mlp_post_2", "w_in_2", "hgrn_lb_logits_2", "gla_w_gk_2", "gla_b_gk_2", "gdn_conv_2",
        "gdn_a_log_2", "gdn_dt_bias_2", "hgrn_onorm_2", "gla_onorm_2", "gdn_onorm_2", "w_out_2",
        "w_up_2", "w_down_2"]


def kernel(**inputs):
    import numpy as np
    import concourse.bacc as bacc
    from concourse.bass_utils import run_bass_kernel_spmd
    arrays = {n: np.ascontiguousarray(inputs[n]) for n in _INS}
    arrays.update(tables())
    nc = bacc.Bacc("TRN2", target_bir_lowering=False, num_devices=1)
    ins = {n: nc.dram_tensor(n, a.shape, F32, kind="ExternalInput").ap() for n, a in arrays.items()}
    out = nc.dram_tensor("out", (1, SEQ, D), F32, kind="ExternalOutput").ap()
    build(nc, ins, out)
    r = run_bass_kernel_spmd(nc, [arrays], core_ids=[0])
    return r.results[0]["out"]
```
